# Optimizing a Trainium2 kernel written in Bass

```python
import jax, jax.numpy as jnp
from jax import lax
import numpy as np

D_MODEL = 1024
BATCH = 1
SEQ = 512
DEPTH = 1
DEC_BATCH = 8
DEC_SEQ = 8
PAST_LEN = 2048
PAGE_SIZE = 128

N_META = 16
HEAD_DIM = 64
A_HEADS = 8
A_KV_HEADS = 2
A_GROUP = A_HEADS // A_KV_HEADS
IDX_HEADS = 4
IDX_DIM = 64
B_HEADS = 8
A_WIDTH = A_HEADS * HEAD_DIM
A_KV_WIDTH = A_KV_HEADS * HEAD_DIM
IDX_WIDTH = IDX_HEADS * IDX_DIM
B_WIDTH = B_HEADS * HEAD_DIM
ATTN_SCALE = HEAD_DIM ** -0.5
IDX_SCALE = (IDX_DIM * IDX_HEADS) ** -0.5
ROPE_THETA = 500000.0
TOPK_CAP = 256
Q_BLOCK = 128
PEER_HEADS = 8
PEER_KEYS = 128
N_EXPERTS = PEER_KEYS * PEER_KEYS
PEER_QDIM = 256
PEER_HALF = PEER_QDIM // 2
PEER_TOPK = 16
PEER_BLOCK = 128
FORGET_BIAS_INIT = 2.0
LN_EPS = 1e-5
ALPHA = (2.0 * DEPTH) ** 0.25
BETA = (8.0 * DEPTH) ** -0.25
NEG = -1e30
IN_SPLITS = (A_WIDTH, A_KV_WIDTH, A_KV_WIDTH, IDX_WIDTH, IDX_DIM, IDX_HEADS,
             B_WIDTH, B_WIDTH, B_WIDTH, B_HEADS, D_MODEL, D_MODEL)
IN_WIDTH = sum(IN_SPLITS)
IN_OFFSETS = tuple(int(o) for o in np.cumsum(IN_SPLITS)[:-1])

kernel_name = 'hybrid_dsa_fox_peer_step'

def layer_norm(x, g, b):
    xf = x.astype(jnp.float32)
    mu = jnp.mean(xf, axis=-1, keepdims=True)
    var = jnp.mean(jnp.square(xf - mu), axis=-1, keepdims=True)
    y = (xf - mu) * lax.rsqrt(var + LN_EPS) * g.astype(jnp.float32) + b.astype(jnp.float32)
    return y.astype(x.dtype)

def partial_rope(x, pos):
    d = x.shape[-1]
    rot = d // 4
    half = rot // 2
    inv = ROPE_THETA ** (-jnp.arange(half, dtype=jnp.float32) / half)
    ang = pos.astype(jnp.float32)[:, None] * inv[None, :]
    cos = jnp.cos(ang)[None, :, None, :]
    sin = jnp.sin(ang)[None, :, None, :]
    xf = x.astype(jnp.float32)
    x1 = xf[..., :half]
    x2 = xf[..., half:rot]
    out = jnp.concatenate([x1 * cos - x2 * sin, x2 * cos + x1 * sin, xf[..., rot:]], axis=-1)
    return out.astype(x.dtype)

def project(x, pos, w_in, b_forget):
    bsz, t = x.shape[:2]
    z = x @ w_in
    q_a, k_a, v_a, q_i, k_i, w_i, q_b, k_b, v_b, f_b, g_a, g_b = jnp.split(z, IN_OFFSETS, axis=-1)
    q_a = partial_rope(q_a.reshape(bsz, t, A_HEADS, HEAD_DIM), pos)
    k_a = partial_rope(k_a.reshape(bsz, t, A_KV_HEADS, HEAD_DIM), pos)
    v_a = v_a.reshape(bsz, t, A_KV_HEADS, HEAD_DIM)
    q_i = partial_rope(q_i.reshape(bsz, t, IDX_HEADS, IDX_DIM), pos)
    k_i = partial_rope(k_i.reshape(bsz, t, 1, IDX_DIM), pos)[:, :, 0]
    q_b = q_b.reshape(bsz, t, B_HEADS, HEAD_DIM)
    k_b = k_b.reshape(bsz, t, B_HEADS, HEAD_DIM)
    v_b = v_b.reshape(bsz, t, B_HEADS, HEAD_DIM)
    logf = jax.nn.log_sigmoid(f_b.astype(jnp.float32) + b_forget.astype(jnp.float32))
    return q_a, k_a, v_a, q_i, k_i, w_i, q_b, k_b, v_b, logf, g_a, g_b

def index_scores(q_i, w_i, k_i):
    s = jnp.einsum('bqhd,bsd->bqhs', q_i, k_i, preferred_element_type=jnp.float32)
    return jnp.einsum('bqh,bqhs->bqs', w_i.astype(jnp.float32), jax.nn.relu(s)) * IDX_SCALE

def gather_rows(rows, idx):
    return jax.vmap(lambda r, i: r[i])(rows, idx)

def sparse_attend(q, kg, vg, valid):
    bsz, nq = q.shape[:2]
    qg = q.reshape(bsz, nq, A_KV_HEADS, A_GROUP, HEAD_DIM)
    s = jnp.einsum('bqgrd,bqkgd->bqgrk', qg, kg, preferred_element_type=jnp.float32) * ATTN_SCALE
    s = jnp.where(valid[:, :, None, None, :], s, NEG)
    p = jax.nn.softmax(s, axis=-1)
    o = jnp.einsum('bqgrk,bqkgd->bqgrd', p.astype(vg.dtype), vg)
    return o.reshape(bsz, nq, A_WIDTH)

def dsa_prompt(q_a, k_a, v_a, q_i, k_i, w_i, n_sel):
    bsz, length = q_a.shape[:2]
    pad = (-length) % Q_BLOCK
    total = length + pad

    def front(a):
        return jnp.pad(a, [(0, 0), (pad, 0)] + [(0, 0)] * (a.ndim - 2))

    q_a, k_a, v_a, q_i, k_i, w_i = (front(a) for a in (q_a, k_a, v_a, q_i, k_i, w_i))
    kpos = jnp.arange(total)

    def block(start):
        qa = lax.dynamic_slice_in_dim(q_a, start, Q_BLOCK, axis=1)
        qi = lax.dynamic_slice_in_dim(q_i, start, Q_BLOCK, axis=1)
        wi = lax.dynamic_slice_in_dim(w_i, start, Q_BLOCK, axis=1)
        qpos = start + jnp.arange(Q_BLOCK)
        admissible = (kpos[None, :] <= qpos[:, None]) & (kpos[None, :] >= pad)
        scores = jnp.where(admissible[None], index_scores(qi, wi, k_i), NEG)
        vals, sel = lax.top_k(scores, n_sel)
        valid = vals > 0.5 * NEG
        return sparse_attend(qa, gather_rows(k_a, sel), gather_rows(v_a, sel), valid)

    out = lax.map(block, jnp.arange(total // Q_BLOCK) * Q_BLOCK)
    return out.transpose(1, 0, 2, 3).reshape(bsz, total, A_WIDTH)[:, pad:]

def dsa_sample(q_a, k_a, v_a, q_i, k_i, w_i, cache_k, cache_v, cache_k_idx, page_table, n_sel):
    nb, sn = q_a.shape[:2]
    past = page_table.shape[1] * PAGE_SIZE
    k_idx_all = jnp.concatenate([cache_k_idx[page_table].reshape(nb, past, IDX_DIM), k_i], axis=1)
    kpos = jnp.arange(past + sn)
    qpos = past + jnp.arange(sn)
    admissible = kpos[None, :] <= qpos[:, None]
    scores = jnp.where(admissible[None], index_scores(q_i, w_i, k_idx_all), NEG)
    vals, sel = lax.top_k(scores, n_sel)
    valid = vals > 0.5 * NEG
    from_past = (sel < past)[..., None, None]
    sel_past = jnp.minimum(sel, past - 1)
    phys = jax.vmap(lambda pt, s: pt[s])(page_table, sel_past // PAGE_SIZE)
    off = sel_past % PAGE_SIZE
    sel_new = jnp.clip(sel - past, 0, sn - 1)
    kg = jnp.where(from_past, cache_k[phys, off], gather_rows(k_a, sel_new))
    vg = jnp.where(from_past, cache_v[phys, off], gather_rows(v_a, sel_new))
    return sparse_attend(q_a, kg, vg, valid)

def fox_prompt(q, k, v, logf):
    bsz, length = q.shape[:2]
    pad = (-length) % Q_BLOCK
    total = length + pad

    def front(a):
        return jnp.pad(a, [(0, 0), (pad, 0)] + [(0, 0)] * (a.ndim - 2))

    q, k, v, logf = (front(a) for a in (q, k, v, logf))
    c = jnp.cumsum(logf, axis=1).transpose(0, 2, 1)
    kpos = jnp.arange(total)

    def block(start):
        qb = lax.dynamic_slice_in_dim(q, start, Q_BLOCK, axis=1)
        cq = lax.dynamic_slice_in_dim(c, start, Q_BLOCK, axis=2)
        qpos = start + jnp.arange(Q_BLOCK)
        mask = (kpos[None, :] <= qpos[:, None]) & (kpos[None, :] >= pad)
        s = jnp.einsum('bqhd,bshd->bhqs', qb, k, preferred_element_type=jnp.float32) * ATTN_SCALE
        s = s + cq[:, :, :, None] - c[:, :, None, :]
        s = jnp.where(mask[None, None], s, NEG)
        p = jax.nn.softmax(s, axis=-1)
        o = jnp.einsum('bhqs,bshd->bqhd', p.astype(v.dtype), v)
        return o.reshape(bsz, Q_BLOCK, B_WIDTH)

    out = lax.map(block, jnp.arange(total // Q_BLOCK) * Q_BLOCK)
    return out.transpose(1, 0, 2, 3).reshape(bsz, total, B_WIDTH)[:, pad:]

def fox_sample(q, k, v, logf, cache_k, cache_v, cache_logf, page_table):
    nb, sn = q.shape[:2]
    past = page_table.shape[1] * PAGE_SIZE
    kp = cache_k[page_table].reshape(nb, past, B_HEADS, HEAD_DIM)
    vp = cache_v[page_table].reshape(nb, past, B_HEADS, HEAD_DIM)
    lp = cache_logf[page_table].reshape(nb, past, B_HEADS).astype(jnp.float32)
    tail = (lax.cumsum(lp, axis=1, reverse=True) - lp).transpose(0, 2, 1)
    cn = jnp.cumsum(logf, axis=1).transpose(0, 2, 1)
    s_past = jnp.einsum('bqhd,bshd->bhqs', q, kp, preferred_element_type=jnp.float32) * ATTN_SCALE
    s_past = s_past + tail[:, :, None, :] + cn[:, :, :, None]
    s_new = jnp.einsum('bqhd,bshd->bhqs', q, k, preferred_element_type=jnp.float32) * ATTN_SCALE
    s_new = s_new + cn[:, :, :, None] - cn[:, :, None, :]
    s_new = jnp.where(jnp.tril(jnp.ones((sn, sn), dtype=bool)), s_new, NEG)
    p = jax.nn.softmax(jnp.concatenate([s_past, s_new], axis=-1), axis=-1)
    o = (jnp.einsum('bhqs,bshd->bqhd', p[..., :past].astype(vp.dtype), vp)
         + jnp.einsum('bhqs,bshd->bqhd', p[..., past:].astype(v.dtype), v))
    return o.reshape(nb, sn, B_WIDTH)

def peer(x, w_q, sub_keys, expert_u, expert_v):
    n_tok = x.shape[0]
    pad = (-n_tok) % PEER_BLOCK
    xb_all = jnp.pad(x, ((0, pad), (0, 0))).reshape(-1, PEER_BLOCK, D_MODEL)
    n_cand = PEER_TOPK * PEER_TOPK

    def block(xb):
        q = (xb @ w_q).reshape(PEER_BLOCK, PEER_HEADS, 2, PEER_HALF)
        s = jnp.einsum('thcd,chkd->thck', q, sub_keys, preferred_element_type=jnp.float32)
        sv, si = lax.top_k(s, PEER_TOPK)
        cand = sv[:, :, 0, :, None] + sv[:, :, 1, None, :]
        cidx = si[:, :, 0, :, None] * PEER_KEYS + si[:, :, 1, None, :]
        top, j = lax.top_k(cand.reshape(PEER_BLOCK, PEER_HEADS, n_cand), PEER_TOPK)
        experts = jnp.take_along_axis(cidx.reshape(PEER_BLOCK, PEER_HEADS, n_cand), j, axis=-1)
        gate = jax.nn.softmax(top, axis=-1)
        pre = jnp.einsum('thkd,td->thk', expert_u[experts], xb, preferred_element_type=jnp.float32)
        coef = (gate * jax.nn.gelu(pre, approximate=False)).astype(x.dtype)
        return jnp.einsum('thk,thkd->td', coef, expert_v[experts])

    out = lax.map(block, xb_all)
    return out.reshape(-1, D_MODEL)[:n_tok]

def finish_layer(x, y_a, y_b, g_a, g_b, w_branch_a, w_branch_b, w_out, ln1_g, ln1_b,
                 peer_w_q, peer_sub_keys, peer_u, peer_v, ln2_g, ln2_b):
    merged = jax.nn.sigmoid(g_a) * (y_a @ w_branch_a) + jax.nn.sigmoid(g_b) * (y_b @ w_branch_b)
    h = layer_norm(ALPHA * x + merged @ w_out, ln1_g, ln1_b)
    f = peer(h.reshape(-1, D_MODEL), peer_w_q, peer_sub_keys, peer_u, peer_v).reshape(h.shape)
    return layer_norm(ALPHA * h + f, ln2_g, ln2_b)

def setup_inputs(seed: int = 0) -> dict:
    key = jax.random.key(seed)
    ks = jax.random.split(key, 24)
    nrm = jax.random.normal
    n_pages = PAST_LEN // PAGE_SIZE
    n_used = DEC_BATCH * n_pages
    n_pool = n_used + n_used // 4
    page_table = jax.random.permutation(ks[0], n_pool)[:n_used].reshape(DEC_BATCH, n_pages).astype(jnp.int32)
    col_scale = np.concatenate([np.full((w,), BETA if i in (2, 8) else 1.0, dtype=np.float32)
                                for i, w in enumerate(IN_SPLITS)])
    return {
        'x_prompt': nrm(ks[1], (BATCH, SEQ, D_MODEL), jnp.float32),
        'x_sample': nrm(ks[2], (DEC_BATCH, DEC_SEQ, D_MODEL), jnp.float32),
        'cache_k_a': nrm(ks[3], (DEPTH, n_pool, PAGE_SIZE, A_KV_HEADS, HEAD_DIM), jnp.float32),
        'cache_v_a': 0.5 * nrm(ks[4], (DEPTH, n_pool, PAGE_SIZE, A_KV_HEADS, HEAD_DIM), jnp.float32),
        'cache_k_idx': nrm(ks[5], (DEPTH, n_pool, PAGE_SIZE, IDX_DIM), jnp.float32),
        'cache_k_b': nrm(ks[6], (DEPTH, n_pool, PAGE_SIZE, B_HEADS, HEAD_DIM), jnp.float32),
        'cache_v_b': 0.5 * nrm(ks[7], (DEPTH, n_pool, PAGE_SIZE, B_HEADS, HEAD_DIM), jnp.float32),
        'cache_logf_b': jax.nn.log_sigmoid(FORGET_BIAS_INIT + nrm(ks[8], (DEPTH, n_pool, PAGE_SIZE, B_HEADS), jnp.float32)),
        'page_table': page_table,
        'meta_tokens': nrm(ks[9], (N_META, D_MODEL), jnp.float32),
        'w_in': nrm(ks[10], (DEPTH, D_MODEL, IN_WIDTH), jnp.float32) * (D_MODEL ** -0.5) * jnp.asarray(col_scale),
        'b_forget': FORGET_BIAS_INIT + 0.1 * nrm(ks[11], (DEPTH, B_HEADS), jnp.float32),
        'w_branch_a': nrm(ks[12], (DEPTH, A_WIDTH, D_MODEL), jnp.float32) * (A_WIDTH ** -0.5) * BETA,
        'w_branch_b': nrm(ks[13], (DEPTH, B_WIDTH, D_MODEL), jnp.float32) * (B_WIDTH ** -0.5) * BETA,
        'w_out': nrm(ks[14], (DEPTH, D_MODEL, D_MODEL), jnp.float32) * (D_MODEL ** -0.5) * BETA,
        'ln1_g': 1.0 + 0.02 * nrm(ks[15], (DEPTH, D_MODEL), jnp.float32),
        'ln1_b': 0.02 * nrm(ks[16], (DEPTH, D_MODEL), jnp.float32),
        'peer_w_q': nrm(ks[17], (DEPTH, D_MODEL, PEER_HEADS * PEER_QDIM), jnp.float32) * (D_MODEL ** -0.5),
        'peer_sub_keys': nrm(ks[18], (DEPTH, 2, PEER_HEADS, PEER_KEYS, PEER_HALF), jnp.float32) * (PEER_HALF ** -0.5),
        'peer_u': nrm(ks[19], (DEPTH, N_EXPERTS, D_MODEL), jnp.float32) * (D_MODEL ** -0.5),
        'peer_v': nrm(ks[20], (DEPTH, N_EXPERTS, D_MODEL), jnp.float32) * BETA,
        'ln2_g': 1.0 + 0.02 * nrm(ks[21], (DEPTH, D_MODEL), jnp.float32),
        'ln2_b': 0.02 * nrm(ks[22], (DEPTH, D_MODEL), jnp.float32),
    }

def reference(x_prompt, x_sample, cache_k_a, cache_v_a, cache_k_idx, cache_k_b, cache_v_b, cache_logf_b,
              page_table, meta_tokens, w_in, b_forget, w_branch_a, w_branch_b, w_out, ln1_g, ln1_b,
              peer_w_q, peer_sub_keys, peer_u, peer_v, ln2_g, ln2_b):
    bsz, seq = x_prompt.shape[:2]
    dec_seq = x_sample.shape[1]
    past = page_table.shape[1] * PAGE_SIZE
    n_sel_prompt = min(TOPK_CAP, seq // 4)
    n_sel_sample = min(TOPK_CAP, (past + dec_seq) // 4)
    meta = jnp.broadcast_to(meta_tokens[None].astype(x_prompt.dtype), (bsz, N_META, D_MODEL))
    xp = jnp.concatenate([meta, x_prompt], axis=1)
    xs = x_sample
    pos_p = jnp.arange(seq + N_META, dtype=jnp.int32)
    pos_s = past + jnp.arange(dec_seq, dtype=jnp.int32)
    new_p = ([], [], [], [], [], [])
    new_s = ([], [], [], [], [], [])
    for l in range(DEPTH):
        q_a, k_a, v_a, q_i, k_i, w_i, q_b, k_b, v_b, logf, g_a, g_b = project(xp, pos_p, w_in[l], b_forget[l])
        y_a = dsa_prompt(q_a, k_a, v_a, q_i, k_i, w_i, n_sel_prompt)
        y_b = fox_prompt(q_b, k_b, v_b, logf)
        for lst, row in zip(new_p, (k_a, v_a, k_i, k_b, v_b, logf)):
            lst.append(row)
        xp = finish_layer(xp, y_a, y_b, g_a, g_b, w_branch_a[l], w_branch_b[l], w_out[l], ln1_g[l], ln1_b[l],
                          peer_w_q[l], peer_sub_keys[l], peer_u[l], peer_v[l], ln2_g[l], ln2_b[l])
        q_a, k_a, v_a, q_i, k_i, w_i, q_b, k_b, v_b, logf, g_a, g_b = project(xs, pos_s, w_in[l], b_forget[l])
        y_a = dsa_sample(q_a, k_a, v_a, q_i, k_i, w_i, cache_k_a[l], cache_v_a[l], cache_k_idx[l],
                         page_table, n_sel_sample)
        y_b = fox_sample(q_b, k_b, v_b, logf, cache_k_b[l], cache_v_b[l], cache_logf_b[l], page_table)
        for lst, row in zip(new_s, (k_a, v_a, k_i, k_b, v_b, logf)):
            lst.append(row)
        xs = finish_layer(xs, y_a, y_b, g_a, g_b, w_branch_a[l], w_branch_b[l], w_out[l], ln1_g[l], ln1_b[l],
                          peer_w_q[l], peer_sub_keys[l], peer_u[l], peer_v[l], ln2_g[l], ln2_b[l])
    y_prompt = xp[:, N_META:]
    return (y_prompt, xs,
            jnp.stack(new_p[0]), jnp.stack(new_p[1]), jnp.stack(new_p[2]),
            jnp.stack(new_p[3]), jnp.stack(new_p[4]), jnp.stack(new_p[5]),
            jnp.stack(new_s[0]), jnp.stack(new_s[1]), jnp.stack(new_s[2]),
            jnp.stack(new_s[3]), jnp.stack(new_s[4]), jnp.stack(new_s[5]))


_drawn_inputs = setup_inputs


def setup_inputs(seed=0):
    import zlib

    import numpy as np

    out = dict(_drawn_inputs(seed))
    spreads = {}
    factors = {}
    for name, (base, spread) in spreads.items():
        noise = np.random.default_rng([zlib.crc32(name.encode()), seed]).standard_normal(out[name].shape)
        drawn = base * np.exp(spread * noise) if base else spread * noise
        out[name] = __import__('jax').numpy.asarray(drawn.astype(out[name].dtype))
    for name, factor in factors.items():
        out[name] = (out[name] * factor).astype(out[name].dtype)
    return out
```

```python
from contextlib import ExitStack

import numpy as np

import concourse.bass as bass
from concourse import mybir

ALU = mybir.AluOpType
ACT = mybir.ActivationFunctionType
F32 = mybir.dt.float32
U32 = mybir.dt.uint32
I32 = mybir.dt.int32
BF16 = mybir.dt.bfloat16
AX_X = mybir.AxisListType.X

D = 1024
KD = D // 128
N_META, SEQ = 16, 512
LP = N_META + SEQ
NB, SN = 8, 8
NS = NB * SN
T = LP + NS
HT = T // 2
HD = 64
NH = 8
NKV = 2
NI = 4
PAGE, NPG = 128, 16
PAST = PAGE * NPG
NPOOL = NB * NPG * 5 // 4
KEYS = PAST + SN
ATTN_SCALE = HD ** -0.5
IDX_SCALE = (64 * NI) ** -0.5
SEL_P = 128
SEL_S = 256
NEG = -1e30
TAKEN = -3e38
ALPHA = 2.0 ** 0.25
EPS = 1e-5
VW = NH * HD + NKV * HD + NI
PH, PK = 8, 16
NE = PH * PK
TILES = [(128 * i, min(128, T - 128 * i)) for i in range(5)]
QTILES = [(128 * i, min(128, LP - 128 * i), min(128 * (i + 1), LP)) for i in range(5)]

QB, KB, QA, KA, QI, KI = 0, 8, 16, 24, 26, 30
NHEADS = 31
PROJ = ([(QA + 2 * j, 2, True, ATTN_SCALE) for j in range(4)] + [(KA, 2, True, 1.0)]
        + [(QI + 2 * j, 2, True, 1.0) for j in range(2)] + [(KI, 1, True, 1.0)]
        + [(QB + 2 * j, 2, False, ATTN_SCALE) for j in range(4)]
        + [(KB + 2 * j, 2, False, 1.0) for j in range(4)])
NPROJ = len(PROJ)
ROPES = [m for m, p in enumerate(PROJ) if p[2]]

CONSTS = [("ident", 128), ("iota16", 16), ("eps", 1), ("causal", 128), ("rot", 128), ("row_of", 512),
          ("head_of", 512), ("new_causal", 8), ("idx_causal", 8), ("w_place", 128), ("head_no", 1),
          ("cos", T), ("sin", T), ("restart", T)]
CAT, _o = {}, 0
for _n, _w in CONSTS:
    CAT[_n] = (_o, _w)
    _o += _w
NCONST = _o
GATE_AT = 70


def tables():
    c = np.zeros((128, NCONST), np.float32)

    def put(name, a):
        o, w = CAT[name]
        c[:a.shape[0], o:o + w] = a.reshape(a.shape[0], w)

    p = np.arange(128)
    put("ident", np.eye(128, dtype=np.float32))
    put("causal", np.where(p[None, :] > p[:, None], np.float32(NEG), np.float32(0)))
    rot = np.zeros((128, 128), np.float32)
    for base in (0, 64):
        for j in range(8):
            rot[base + j + 8, base + j] = -1.0
            rot[base + j, base + j + 8] = 1.0
    put("rot", rot)
    row_of = np.zeros((64, 4, 128), np.float32)
    head_of = np.zeros((64, 4, 128), np.float32)
    for pr in range(4):
        for e in range(2):
            for h in range(NH):
                for t in range(SN):
                    col = e * 64 + h * 8 + t
                    row_of[(2 * pr + e) * 8 + t, pr, col] = 1.0
                    head_of[(2 * pr + e) * 8 + h, pr, col] = 1.0
    put("row_of", row_of)
    put("head_of", head_of)
    t = p % 8
    s = np.arange(8)
    put("new_causal", np.where(s[None, :] > t[:, None], np.float32(NEG), np.float32(0)))
    put("idx_causal", np.where(s[None, :] > t[:64, None], np.float32(NEG), np.float32(0)))
    wp = np.zeros((128, 2, 64), np.float32)
    for g in range(2):
        for b in range(4):
            for h in range(NI):
                for tt in range(SN):
                    wp[b * 32 + h * 8 + tt, g, (g * 4 + b) * 8 + tt] = 1.0
    put("w_place", wp)
    put("iota16", np.tile(np.arange(16, dtype=np.float32), (128, 1)))
    put("head_no", (p % 8).astype(np.float32)[:, None])
    put("eps", np.full((128, 1), EPS, np.float32))
    pos = np.concatenate([np.arange(LP), np.tile(PAST + np.arange(SN), NB)]).astype(np.float32)
    inv = np.power(np.float32(500000.0), -np.arange(8, dtype=np.float32) / np.float32(8))
    ang = (pos[None, :] * inv[:, None]).astype(np.float32).astype(np.float64)
    cos, sin = np.ones((128, T), np.float32), np.zeros((128, T), np.float32)
    for base in (0, 64):
        for half in (0, 8):
            cos[base + half:base + half + 8] = np.cos(ang)
            sin[base + half:base + half + 8] = np.sin(ang)
    put("cos", cos)
    put("sin", sin)
    restart = np.ones((8, T), np.float32)
    restart[:, 0] = 0.0
    restart[:, LP::SN] = 0.0
    put("restart", restart)
    return c


def program(nc, io):
    ctx = ExitStack()
    with ctx:
        arena = ctx.enter_context(nc.sbuf_tensor("arena", [128, 53100], F32))
        ps = ctx.enter_context(nc.psum_tensor("ps", [128, 8 * 512], F32))

        def sem(name):
            return ctx.enter_context(nc.semaphore(name))

        def sems(name, n):
            return [sem(f"{name}{i}") for i in range(n)]

        class Region:

            def __init__(self, at):
                self.at = at

            def take(self, *shape, p=128):
                n = int(np.prod(shape))
                v = arena[0:p, self.at:self.at + n]
                self.at += n
                assert self.at <= 53100, self.at
                if len(shape) == 2:
                    v = v.rearrange("p (a b) -> p a b", a=shape[0])
                elif len(shape) == 3:
                    v = v.rearrange("p (a b c) -> p a b c", a=shape[0], b=shape[1])
                return v

        def bank(b, w=512, p0=0, p1=128):
            return ps[p0:p1, b * 512:b * 512 + w]

        base = Region(0)
        consts = base.take(NCONST)

        def const(name, p=128):
            o, w = CAT[name]
            return consts[0:p, o:o + w]

        ident, causal = const("ident"), const("causal")
        row_of = const("row_of", 64).rearrange("p (a b) -> p a b", a=4)
        head_of = const("head_of", 64).rearrange("p (a b) -> p a b", a=4)
        w_place = const("w_place").rearrange("p (a b) -> p a b", a=2)
        small = base.take(128)
        ident_b, causal_b = base.take(64).bitcast(BF16), base.take(64).bitcast(BF16)
        newc_b = base.take(4).bitcast(BF16)
        row_of_b = base.take(256, p=64).bitcast(BF16).rearrange("p (a b) -> p a b", a=4)
        xT_at = base.at
        xT = base.take(KD, T)
        yaT, ybT = base.take(4, T), base.take(4, T)
        vtm_at = base.at
        vtm = base.take(5, VW)
        qs_at = base.at
        qs = base.take(NB, 4, 128)
        qas = base.take(NB, 128)
        qis = base.take(4, 128)
        zeroed = arena[:, qs_at:base.at]
        kbn, kan, kin = base.take(4, NS), base.take(NS), base.take(4, SN)
        wd = base.take(2, 64)
        wrow = base.take(2)
        pages = base.take(2 * NB * NPG, p=1).bitcast(I32)
        page_rows = base.take(NPG, p=64).bitcast(I32)
        lidx = base.take(NPG, p=64).bitcast(U32)
        after_base = base.at

        r = Region(after_base)
        heads = r.take(NHEADS, T)
        work_at = r.at
        wring = [r.take(KD, 128) for _ in range(3)]
        w_v = r.take(KD, VW)
        zsb = [r.take(T) for _ in range(2)]
        rot_s = r.take(T)
        w_f = r.take(KD, NH)
        bf = r.take(1)
        f_z, f_tmp, f_log, f_sum = (yaT[0:NH, j, :] for j in range(4))
        r = Region(work_at)
        prob = [r.take(640) for _ in range(3)]
        probT = [r.take(512) for _ in range(2)]
        diag = [r.take(128) for _ in range(3)]
        isc = r.take(640)
        relu = [r.take(640) for _ in range(2)]
        maskb = r.take(320).bitcast(BF16)
        NSLOT = 8
        r = Region(after_base)
        ring = [r.take(2048) for _ in range(NSLOT)]
        kv_pair = [arena[:, after_base + j * 4096:after_base + (j + 1) * 4096] for j in range(4)]
        diag_s = r.take(128)
        probT_s = [r.take(512) for _ in range(2)]
        probTn = r.take(128, p=8)
        r = Region(max(work_at, r.at))
        tail = r.take(KEYS, p=64)
        lp_at = r.at
        lp = r.take(PAST, p=64)
        isamp = r.take(KEYS, p=64)
        prob_s = r.take(KEYS)
        smask = r.take(KEYS // 2, p=64).bitcast(BF16)
        relu_s = [r.take(512) for _ in range(2)]
        vnew = [r.take(2, VW, p=8), Region(lp_at).take(2, VW, p=8)]
        r = Region(vtm_at)
        hT = r.take(KD, T)
        subk = r.take(2 * PH, 128)
        peer_at = r.at
        r = Region(after_base)
        hrow = r.take(5, D)
        lng, lnb = r.take(D), r.take(D)
        peer2_at = r.at
        xrow = [r.take(D) for _ in range(2)]
        wmix = [r.take(3 * KD, 128) for _ in range(2)]
        mergedT = r.take(KD, T)
        w_out = r.take(KD, D)
        sig = [r.take(T) for _ in range(2)]
        r = Region(xT_at)
        qpT = r.take(2 * PH, T)
        assert r.at <= vtm_at and peer_at <= after_base
        r = Region(peer_at)
        sv = r.take(2 * PH, PK)
        si_at = r.at
        si = r.take(2 * PH, PK).bitcast(U32)
        siF = r.take(2 * PH, PK)
        top, gate, ja, jb, gexp = (r.take(PH, PK) for _ in range(5))
        tj = r.take(PH, PK).bitcast(U32)
        jbits = r.take(PH, PK).bitcast(U32)
        e0, e1 = r.take(PH, PK), r.take(PH, PK)
        ids = [r.take(NE).bitcast(U32) for _ in range(2)]
        assert r.at <= after_base, r.at - after_base
        r = Region(peer2_at)
        sc = r.take(2 * PH, 128)
        cand = r.take(PH, PK * PK)
        oh = r.take(NE, PK)
        facc = r.take(D)
        pre = r.take(NE)
        gl = r.take(NE)
        coef = [r.take(NE) for _ in range(2)]
        ND = 4
        diag_p = [r.take(128) for _ in range(ND)]
        NR = 14
        rows = [r.take(D) for _ in range(NR)]
        r = Region(CAT["causal"][0])
        wq = [r.take(KD, 128) for _ in range(3)]
        assert r.at <= NCONST

        x_loaded, v_w_loaded, f_w_loaded = sem("x_loaded"), sem("v_w_loaded"), sem("f_w_loaded")
        w_loaded = sems("w_loaded", 3)
        z_ready, z_copied = sem("z_ready"), sem("z_copied")
        rot_ready, rope_done = sem("rot_ready"), sem("rope_done")
        f_ready, f_act, logf_ready = sem("f_ready"), sem("f_act"), sem("logf_ready")
        ones_set, zero_set = sem("ones_set"), sem("zero_set")
        negc_stored, bias_loaded, v_stored = sem("negc_stored"), sem("bias_loaded"), sem("v_stored")
        k_stored, logf_stored, y_stored = sem("k_stored"), sem("logf_stored"), sem("y_stored")
        dve_seq, act_seq = sem("dve_seq"), sem("act_seq")
        phase = sem("phase")
        s_ready, s_read, negmax_ready = sem("s_ready"), sem("s_read"), sem("negmax_ready")
        idx_added, mask_ready, diag_ready = sem("idx_added"), sem("mask_ready"), sem("diag_ready")
        pt_ready, pt_copied = sem("pt_ready"), sem("pt_copied")
        o_ready, o_copied = sem("o_ready"), sem("o_copied")
        ring_loaded = sems("ring_loaded", NSLOT)
        slot_read, pair_read = sem("slot_read"), sem("pair_read")
        spread_a, spread_d = sem("spread_a"), sem("spread_d")
        wrow_loaded, wd_ready = sem("wrow_loaded"), sem("wd_ready")
        lidx_ready, lp_loaded, lf_ones = sem("lidx_ready"), sem("lp_loaded"), sem("lf_ones")
        tail_new, tail_ready = sem("tail_new"), sem("tail_ready")
        ia_ready, relu_done, ib_ready, ib_copied = (sem(n) for n in ("ia_ready", "relu_done", "ib_ready", "ib_copied"))
        smask_ready, ss_ready, smax_ready = sem("smask_ready"), sem("ss_ready"), sem("smax_ready")
        sx_done, sdiag_ready, st_ready, st_copied = (sem(n) for n in ("sx_done", "sdiag_ready", "st_ready", "st_copied"))
        so_ready, so_copied, masks_ready = sem("so_ready"), sem("so_copied"), sem("masks_ready")
        vnew_loaded = sems("vnew_loaded", 2)
        mix_loaded, wo_loaded, ln_loaded = sems("mix_loaded", 2), sem("wo_loaded"), sem("ln_loaded")
        mix_ready, sig_done, mix_done = sem("mix_ready"), sem("sig_done"), sem("mix_done")
        xr_loaded, h_ready, res_done = sems("xr_loaded", 2), sem("h_ready"), sem("res_done")
        var_ready, std_ready, ln_done = sem("var_ready"), sem("std_ready"), sem("ln_done")
        ht_ready, ht_copied = sem("ht_ready"), sem("ht_copied")
        wq_loaded, qp_ready, qp_copied = sems("wq_loaded", 3), sem("qp_ready"), sem("qp_copied")
        subk_loaded, ln2_loaded = sem("subk_loaded"), sem("ln2_loaded")
        sc_ready, sc_copied, gexp_in, gexp_out = (sem(n) for n in ("sc_ready", "sc_copied", "gexp_in", "gexp_out"))
        ids_ready, row_loaded = sem("ids_ready"), sems("row_loaded", NR)
        dve_used, pe_used = sem("dve_used"), sem("pe_used")
        gelu_done, coef_ready, dp_ready = sem("gelu_done"), sem("coef_ready"), sem("dp_ready")

        csc = nc.dram_tensor("neg_cumulative", [NH, T], F32, kind="Internal").ap()

        def col(j, w=1, p=128):
            return small[0:p, j:j + w]

        COL_TOP8, COL_NEGMAX, COL_RSUM, COL_RINV = 8, 80, 84, 88
        COL_SMAX, COL_SSUM, COL_SINV, COL_TOPS = 16, 17, 18, 24
        COL_BN, COL_MV, COL_STD, COL_RSTD = 32, 48, 50, 52
        COL_TOPP, COL_GSUM, COL_GINV = 56, 64, 72

        def blocks(seen):
            return [(k, min(128, seen - k)) for k in range(0, seen, 128)]

        units, uses = [], []
        for i in range(5):
            if i:
                uses += [("idx", i, h) for h in range(NI)]
            for kind in ("fox", "dsa"):
                for h in range(NH):
                    units.append((kind, i, h, len(uses)))
                    uses.append((kind, i, h))
        NU = len(units)
        idx_use = {(i, h): n for n, (k, i, h) in enumerate(uses) if k == "idx"}
        ROUNDS_P, ROUNDS_S = SEL_P // 8, SEL_S // 8

        gathers = [(i, v, k) for i in range(5) for v in (0, 1) for k in range(NE)]
        by_dve = [v == 0 or k % 8 in ((3, 5, 7) if i < 4 else (1, 3, 5, 7)) for i, v, k in gathers]
        read_before = []
        n_dve = n_pe = 0
        for d in by_dve:
            read_before.append(n_dve if d else n_pe)
            n_dve, n_pe = n_dve + d, n_pe + (not d)

        QSPANS, QBANKS = ((0, 128), (128, T)), (4, 6)

        def gather_no(i, v, k):
            return (2 * i + v) * NE + k

        def halves(b, rows_=128):
            return ps[0:rows_, b * 512:(b + 2) * 512].rearrange("p (a c) -> p a c", a=2)[:, :, 0:HT]

        def split(v):
            return v.rearrange("p (a c) -> p a c", a=2)

        def end_phase(eng, n):
            eng.drain().then_inc(phase, 1)
            eng.wait_ge(phase, 5 * n)

        block = ctx.enter_context(nc.Block())

        @block.sync
        def _(sp):
            def project():
                sp.dma_start(xT[:], io["xT"]).then_inc(x_loaded, 16)
                for m in range(NPROJ):
                    if m >= 3:
                        sp.wait_ge(z_ready, m - 2)
                    sp.dma_start(wring[m % 3], io["w_proj"][m]).then_inc(w_loaded[m % 3], 16)
                    if m == 2:
                        sp.dma_start(consts[:], io["cst"]).then_inc(x_loaded, 16)
                        sp.dma_start(pages[:], io["pages"]).then_inc(x_loaded, 16)
                        sp.dma_start(page_rows[:], io["page_rows"]).then_inc(x_loaded, 16)
                sp.wait_ge(logf_ready, 1)
                sp.dma_start(io["logf_out"], f_log).then_inc(logf_stored, 16)
                sp.dma_start(csc, f_z).then_inc(negc_stored, 16)
                sp.wait_ge(negc_stored, 16)
                sp.dma_start(heads[64:65, KB:KB + NH, :],
                             csc.rearrange("(o h) t -> o h t", o=1)).then_inc(bias_loaded, 16)
                sp.wait_ge(z_copied, NPROJ + 5)
                for i, (t0, nt) in enumerate(TILES):
                    sp.dma_start(io["v_out"][t0:t0 + nt, :], vtm[0:nt, i, :]).then_inc(v_stored, 16)
                sp.wait_ge(rope_done, len(ROPES))
                sp.dma_start(io["k_out"][:, 0:2, :], heads[0:64, KA:KA + 2, :]).then_inc(k_stored, 16)
                sp.dma_start(io["k_out"][:, 2:3, :], heads[0:64, KI:KI + 1, :]).then_inc(k_stored, 16)
                sp.dma_start(io["k_out"][:, 3:11, :], heads[0:64, KB:KB + NH, :]).then_inc(k_stored, 16)
                sp.wait_ge(v_stored, 16 * 5)
                for g in range(2):
                    src = io["v_out"][LP + 32 * g:LP + 32 * g + 32, NH * HD + NKV * HD:VW]
                    for b in range(4):
                        for h in range(NI):
                            sp.dma_start(wrow[b * 32 + h * 8:b * 32 + h * 8 + 8, g:g + 1],
                                         src[b * 8:b * 8 + 8, h:h + 1],
                                         allow_slow_non_contiguous=True).then_inc(wrow_loaded, 16)
                sp.wait_ge(bias_loaded, 16)

            def sample():
                for b in range(NB):
                    sp.dma_start(tail[b * 8:b * 8 + 8, PAST:KEYS],
                                 csc[:, LP + b * SN:LP + (b + 1) * SN]).then_inc(tail_new, 16)

                def four_pages(at):
                    return nc.values_load_multi_w_load_instructions(
                        pages[0:1, at:at + 4], engines=(mybir.EngineType.SP,), min_val=0, max_val=NPOOL - 1)[1]

                for c in range(4):
                    for b in range(NB):
                        for j, no in enumerate(four_pages(b * NPG + 4 * c)):
                            e, p = b % 2, b // 2
                            sp.dma_start(ring[c][e * 64:e * 64 + 64, p * 512 + j * 128:p * 512 + j * 128 + 128],
                                         io["kidx"][bass.ds(no, 1)].rearrange("o p n -> (o p) n")
                                         ).then_inc(ring_loaded[c], 16)
                u = 0
                for pr in range(4):
                    for src in ("k_b", "v_b"):
                        for c in range(4):
                            for e in range(2):
                                s = u % NSLOT
                                if u < 4:
                                    sp.wait_ge(ia_ready, 2 * (u + 1))
                                if u >= NSLOT:
                                    sp.wait_ge(slot_read, u - NSLOT + 1)
                                for j, no in enumerate(four_pages((NB + 2 * pr + e) * NPG + 4 * c)):
                                    sp.dma_start(ring[s][:, j * 512:(j + 1) * 512],
                                                 io[src][bass.ds(no, 1)].rearrange("o p n -> (o p) n")
                                                 ).then_inc(ring_loaded[s], 16)
                                u += 1
                for b in range(NB):
                    s = b % 4
                    if b < 4:
                        sp.wait_ge(slot_read, u - NSLOT + 2 * s + 2)
                    else:
                        sp.wait_ge(pair_read, b // 2 - 1)
                    for j0 in range(0, NPG, 4):
                        for j, no in enumerate(four_pages(b * NPG + j0), j0):
                            sp.dma_start(kv_pair[s][:, j * 256:(j + 1) * 256],
                                         io["kv_a"][bass.ds(no, 1)].rearrange("o p n -> (o p) n")
                                         ).then_inc(ring_loaded[2 * s], 16)

            def merge():
                for m in range(KD):
                    if m >= 2:
                        sp.wait_ge(mix_ready, 4 * (m - 1))
                    sp.dma_start(wmix[m % 2], io["w_mix"][m]).then_inc(mix_loaded[m % 2], 16)
                    if m == 1:
                        sp.dma_start(w_out[:], io["w_out"]).then_inc(wo_loaded, 16)
                        sp.dma_start(lng, io["ln"][0:1, :].partition_broadcast(128)).then_inc(ln_loaded, 16)
                        sp.dma_start(lnb, io["ln"][1:2, :].partition_broadcast(128)).then_inc(ln_loaded, 16)
                for i, (t0, nt) in enumerate(TILES):
                    if i >= 2:
                        sp.wait_ge(res_done, i - 1)
                    sp.dma_start(xrow[i % 2][0:nt, :], io["x"][t0:t0 + nt, :]).then_inc(xr_loaded[i % 2], 16)
                sp.wait_ge(mix_done, KD)
                sp.dma_start(subk[:], io["subk"]).then_inc(subk_loaded, 16)

            def peer():
                sp.dma_start(lng, io["ln"][2:3, :].partition_broadcast(128)).then_inc(ln2_loaded, 16)
                sp.dma_start(lnb, io["ln"][3:4, :].partition_broadcast(128)).then_inc(ln2_loaded, 16)
                for n in range(4 * PH):
                    if n >= 3:
                        sp.wait_ge(qp_ready, n - 2)
                    sp.dma_start(wq[n % 3], io["w_q"][n % (2 * PH)]).then_inc(wq_loaded[n % 3], 16)
                for i, (t0, nt) in enumerate(TILES):
                    sp.wait_ge(ln_done, 5 + i + 1)
                    sp.dma_start(io["y_out"][t0:t0 + nt, :], facc[0:nt, :]).then_inc(y_stored, 16)
                sp.wait_ge(y_stored, 16 * 5)

            project()
            end_phase(sp, 1)
            sp.wait_ge(k_stored, 16 * 3)
            sp.wait_ge(logf_stored, 16)
            sp.wait_ge(wrow_loaded, 16 * 32)
            end_phase(sp, 2)
            sample()
            end_phase(sp, 3)
            merge()
            end_phase(sp, 4)
            peer()

        @block.gpsimd
        def _(pool):
            pool.memset(zeroed, 0.0).then_inc(zero_set, 1)
            pool.wait_ge(zero_set, 1)
            pool.memset(heads[64:65, QB:QB + NH, :], 1.0).then_inc(ones_set, 1)
            end_phase(pool, 1)
            end_phase(pool, 2)
            pool.memset(prob_s[0:64, 0:PAST], 1.0).then_inc(lf_ones, 1)
            pool.wait_ge(lidx_ready, 1)
            for j in range(NPG):
                pool.indirect_dma_start(out=lp[:, j * 128:(j + 1) * 128], out_offset=None, in_=io["logf_b"],
                                        in_offset=bass.IndirectOffsetOnAxis(ap=lidx[:, j:j + 1], axis=0)
                                        ).then_inc(lp_loaded, 16)
            for q in range(8):
                pr = q % 4
                if q == 1:
                    pool.wait_ge(tail_ready, 1)
                if q >= 2:
                    pool.wait_ge(so_ready, q - 1)
                for e in range(2):
                    t0 = LP + (2 * pr + e) * SN
                    pool.dma_start(vnew[q % 2][:, e, :], io["v_out"][t0:t0 + SN, :]).then_inc(vnew_loaded[q % 2], 16)
            end_phase(pool, 3)
            end_phase(pool, 4)
            for n, (i, v, k) in enumerate(gathers):
                nt = TILES[i][1]
                if v == 0 and k == 0:
                    pool.wait_ge(ids_ready, i + 1)
                if n >= NR:
                    pool.wait_ge(dve_used if by_dve[n - NR] else pe_used, read_before[n - NR] + 1)
                pool.indirect_dma_start(out=rows[n % NR][0:nt, :], out_offset=None,
                                        in_=io["peer_v"] if v else io["peer_u"],
                                        in_offset=bass.IndirectOffsetOnAxis(ap=ids[i % 2][0:nt, k:k + 1], axis=0)
                                        ).then_inc(row_loaded[n % NR], 16)

        @block.tensor
        def _(pe):
            def project():
                pe.wait_ge(x_loaded, 64)

                def rotate(m):
                    n = 64 * PROJ[m][1]
                    pe.wait_ge(z_copied, m + 1)
                    if m:
                        pe.wait_ge(rope_done, m)
                    for a in range(2):
                        last = pe.matmul(bank(4 + a, HT, 0, n), const("rot")[0:n, 0:n],
                                         zsb[m % 2][0:n, a * HT:(a + 1) * HT], start=True, stop=True)
                    last.then_inc(rot_ready, 1)

                for m in range(NPROJ):
                    n = 64 * PROJ[m][1]
                    pe.wait_ge(w_loaded[m % 3], 16 * (m // 3 + 1))
                    if m >= 2:
                        pe.wait_ge(z_copied, m - 1)
                    for a in range(2):
                        for k in range(KD):
                            last = pe.matmul(bank(2 * (m % 2) + a, HT, 0, n), wring[m % 3][:, k, 0:n],
                                             xT[:, k, a * HT:(a + 1) * HT], start=(k == 0), stop=(k == KD - 1))
                    last.then_inc(z_ready, 1)
                    if m and PROJ[m - 1][2]:
                        rotate(m - 1)
                pe.wait_ge(f_w_loaded, 32)
                for a in range(2):
                    for k in range(KD):
                        last = pe.matmul(bank(6 + a, HT, 0, NH), w_f[:, k, :], xT[:, k, a * HT:(a + 1) * HT],
                                         start=(k == 0), stop=(k == KD - 1))
                last.then_inc(f_ready, 1)
                pe.wait_ge(v_w_loaded, 16)
                for i, (t0, nt) in enumerate(TILES):
                    n = NPROJ + i
                    pe.wait_ge(z_copied, n - 1)
                    for a, (c0, c1) in enumerate(((0, 512), (512, VW))):
                        for k in range(KD):
                            last = pe.matmul(bank(2 * (n % 2) + a, c1 - c0, 0, nt), xT[:, k, t0:t0 + nt],
                                             w_v[:, k, c0:c1], start=(k == 0), stop=(k == KD - 1))
                    last.then_inc(z_ready, 1)

            def prompt():
                def scores(n, q, kt, q0, nq, seen, rows_, bias=None, b0=0):
                    if n >= 2:
                        pe.wait_ge(s_read, n - 1)
                    for c0 in range(0, seen, 512):
                        c1 = min(c0 + 512, seen)
                        out = bank(2 * (n % 2) + c0 // 512, c1 - c0, 0, nq)
                        biased = bias is not None and c1 > b0
                        last = pe.matmul(out, heads[0:rows_, q, q0:q0 + nq], heads[0:rows_, kt, c0:c1],
                                         start=True, stop=not biased)
                        if biased:
                            at = max(b0, c0)
                            last = pe.matmul(out[:, at - c0:], ident_b[0:nq, 0:nq], bias[0:nq, at - b0:c1 - b0],
                                             start=False, stop=True)
                    last.then_inc(s_ready, 1)

                def transpose(u):
                    _, i, h, n = units[u]
                    q0, nq, seen = QTILES[i]
                    pe.wait_ge(diag_ready, u + 1)
                    if u >= 2:
                        pe.wait_ge(pt_copied, u - 1)
                    for j, (k0, nk) in enumerate(blocks(seen)):
                        last = pe.matmul(ps[0:nk, (4 + u % 2) * 512 + j * nq:(4 + u % 2) * 512 + (j + 1) * nq],
                                         prob[u % 3][0:nq, k0:k0 + nk], diag[u % 3][0:nq, 0:nq],
                                         start=True, stop=True)
                    last.then_inc(pt_ready, 1)

                def weigh(u):
                    kind, i, h, n = units[u]
                    q0, nq, seen = QTILES[i]
                    v0 = h * HD if kind == "fox" else NH * HD + (h // 4) * HD
                    pe.wait_ge(pt_copied, u + 1)
                    if u >= 2:
                        pe.wait_ge(o_copied, u - 1)
                    p0, c0 = 64 * (h % 2), 6 * 512 + 128 * (u % 2)
                    bl = blocks(seen)
                    for j, (k0, nk) in enumerate(bl):
                        last = pe.matmul(ps[p0:p0 + 64, c0:c0 + nq], vtm[0:nk, j, v0:v0 + HD],
                                         probT[u % 2][0:nk, j * nq:(j + 1) * nq],
                                         start=(j == 0), stop=(j == len(bl) - 1))
                    last.then_inc(o_ready, 1)

                pe.wait_ge(masks_ready, 1)
                for u in range(NU + 3):
                    if u < NU:
                        kind, i, h, n = units[u]
                        q0, nq, seen = QTILES[i]
                        if kind == "fox":
                            if h == 0 and i:
                                for hi in range(NI):
                                    scores(idx_use[i, hi], QI + hi, KI, q0, nq, seen, 64)
                            scores(n, QB + h, KB + h, q0, nq, seen, 65, causal_b, seen - nq)
                        else:
                            if h == 0 and i:
                                pe.wait_ge(mask_ready, i)
                            scores(n, QA + h, KA + h // 4, q0, nq, seen, 64, maskb if i else causal_b)
                    if 2 <= u < NU + 2:
                        transpose(u - 2)
                    if u >= 3:
                        weigh(u - 3)

            def sample():
                pe.wait_ge(wd_ready, 1)
                for c in range(5):
                    w = 512 if c < 4 else SN
                    if c < 4:
                        pe.wait_ge(ring_loaded[c], 16 * 32)
                    for g in range(2):
                        n = 2 * c + g
                        if c:
                            pe.wait_ge(relu_done, n - 1)
                        for p in (2 * g, 2 * g + 1):
                            rhs = ring[c][:, p * 512:(p + 1) * 512] if c < 4 else kin[:, p, :]
                            last = pe.matmul(bank(g, w), qis[:, p, :], rhs, start=(p % 2 == 0), stop=(p % 2 == 1))
                        last.then_inc(ia_ready, 1)
                    pe.wait_ge(relu_done, 2 * c + 2)
                    if c >= 2:
                        pe.wait_ge(ib_copied, c - 1)
                    for g in range(2):
                        last = pe.matmul(bank(2 + c % 2, w, 0, 64), wd[:, g, :], relu_s[g][:, 0:w],
                                         start=(g == 0), stop=(g == 1))
                    last.then_inc(ib_ready, 1)
                pe.wait_ge(tail_ready, 1)
                pe.wait_ge(ib_copied, 5)
                tcount = 0
                for q in range(8):
                    fox, pr = q < 4, q % 4
                    if q:
                        pe.wait_ge(sx_done, q)
                    if q == 4:
                        pe.wait_ge(smask_ready, 1)
                    pick, bias = (head_of, tail) if fox else (row_of_b, smask)
                    for c in range(4):
                        out = bank(c)
                        for e in range(2):
                            b = 2 * pr + e
                            if fox:
                                u = pr * 16 + 2 * c + e
                                before = 1 if u % NSLOT < 4 else 0
                                pe.wait_ge(ring_loaded[u % NSLOT], 16 * (32 * before + 4 * (u // NSLOT + 1)))
                                kk = ring[u % NSLOT].rearrange("p (j h n) -> p j h n", j=4, h=4)
                                for hp in range(4):
                                    last = pe.matmul(out, qs[:, b, hp, :], kk[:, :, hp, :],
                                                     start=(e == 0 and hp == 0), stop=False)
                                last.then_inc(slot_read, 1)
                            else:
                                if c == 0:
                                    s = b % 4
                                    pe.wait_ge(ring_loaded[2 * s], 16 * ((32 if 2 * s < 4 else 0) + 32 + 16 * (b // 4 + 1)))
                                kv = kv_pair[b % 4].rearrange("p (j n) -> p j n", j=NPG)
                                pe.matmul(out, qas[:, b, :], kv[:, 4 * c:4 * c + 4, 0:128], start=(e == 0), stop=False)
                        pe.matmul(out, pick[:, pr, :], bias[:, c * 512:(c + 1) * 512], start=False, stop=True)
                    out = bank(4, SN)
                    for e in range(2):
                        b = 2 * pr + e
                        if fox:
                            for hp in range(4):
                                pe.matmul(out, qs[:, b, hp, :], kbn[:, hp, b * SN:(b + 1) * SN],
                                          start=(e == 0 and hp == 0), stop=False)
                        else:
                            pe.matmul(out, qas[:, b, :], kan[:, b * SN:(b + 1) * SN], start=(e == 0), stop=False)
                    if fox:
                        pe.matmul(out, ident_b, newc_b, start=False, stop=False)
                    pe.matmul(out, pick[:, pr, :], bias[:, PAST:KEYS], start=False, stop=True).then_inc(ss_ready, 1)

                    def transpose(c, n):
                        if n >= 2:
                            pe.wait_ge(st_copied, n - 1)
                        if c < 4:
                            for j in range(4):
                                k0 = c * 512 + j * 128
                                last = pe.matmul(ps[:, (5 + n % 2) * 512 + j * 128:(5 + n % 2) * 512 + (j + 1) * 128],
                                                 prob_s[:, k0:k0 + 128], diag_s, start=True, stop=True)
                        else:
                            last = pe.matmul(bank(5 + n % 2, 128, 0, SN), prob_s[:, PAST:KEYS], diag_s,
                                             start=True, stop=True)
                        last.then_inc(st_ready, 1)

                    def weigh(c, n):
                        pe.wait_ge(st_copied, n + 1)
                        if c == 0 and q:
                            pe.wait_ge(so_copied, q)
                        if c == 4:
                            pe.wait_ge(vnew_loaded[q % 2], 32 * (q // 2 + 1))
                        for e in range(2):
                            b = 2 * pr + e
                            if fox and c < 4:
                                u = pr * 16 + 8 + 2 * c + e
                                before = 1 if u % NSLOT < 4 else 0
                                pe.wait_ge(ring_loaded[u % NSLOT], 16 * (32 * before + 4 * (u // NSLOT + 1)))
                            for j in range(4 if c < 4 else 1):
                                for hp in range(4 if fox else 1):
                                    w = 16 if fox else 64
                                    c0 = 64 * e + 16 * hp
                                    if c == 4:
                                        v0 = hp * 128 if fox else 512
                                        vals, p = vnew[q % 2][:, e, v0:v0 + 128], probTn[0:SN, c0:c0 + w]
                                    elif fox:
                                        vals = ring[u % NSLOT][:, j * 512 + hp * 128:j * 512 + (hp + 1) * 128]
                                        p = probT_s[n % 2][:, j * 128 + c0:j * 128 + c0 + w]
                                    else:
                                        vals = kv_pair[b % 4][:, (4 * c + j) * 256 + 128:(4 * c + j) * 256 + 256]
                                        p = probT_s[n % 2][:, j * 128 + c0:j * 128 + c0 + w]
                                    last = pe.matmul(ps[:, 7 * 512 + c0:7 * 512 + c0 + w], vals, p,
                                                     start=(c == j == e == hp == 0), stop=(c == 4),
                                                     skip_group_check=True)
                            if c < 4 and fox:
                                last.then_inc(slot_read, 1)
                            elif c == 3 and e == 1:
                                last.then_inc(pair_read, 1)
                        if c == 4:
                            last.then_inc(so_ready, 1)

                    pe.wait_ge(sdiag_ready, q + 1)
                    transpose(0, tcount)
                    for c in range(5):
                        if c < 4:
                            transpose(c + 1, tcount + 1)
                        weigh(c, tcount)
                        tcount += 1

            def merge():
                for m in range(KD):
                    pe.wait_ge(mix_loaded[m % 2], 16 * (m // 2 + 1))
                    for j, (src, nk, k0) in enumerate(((xT, 8, 0), (xT, 8, 8), (yaT, 4, 16), (ybT, 4, 20))):
                        if m:
                            if j < 2:
                                pe.wait_ge(sig_done, 2 * (m - 1) + j + 1)
                            else:
                                pe.wait_ge(mix_done, m)
                        for a in range(2):
                            for k in range(nk):
                                last = pe.matmul(bank(2 * j + a, HT), wmix[m % 2][:, k0 + k, :],
                                                 src[:, k, a * HT:(a + 1) * HT], start=(k == 0), stop=(k == nk - 1))
                        last.then_inc(mix_ready, 1)
                pe.wait_ge(mix_done, KD)
                pe.wait_ge(wo_loaded, 16)

                def turn(i):
                    t0, nt = TILES[i]
                    pe.wait_ge(ln_done, i + 1)
                    if i:
                        pe.wait_ge(ht_copied, i)
                    for k in range(KD):
                        last = pe.transpose(ps[:, 4 * 512 + k * 128:4 * 512 + k * 128 + nt],
                                            hrow[0:nt, i, k * 128:(k + 1) * 128], ident[0:nt, 0:nt])
                    last.then_inc(ht_ready, 1)

                for i, (t0, nt) in enumerate(TILES):
                    if i >= 2:
                        pe.wait_ge(res_done, i - 1)
                    for a in range(2):
                        for m in range(KD):
                            last = pe.matmul(bank(2 * (i % 2) + a, 512, 0, nt), mergedT[:, m, t0:t0 + nt],
                                             w_out[:, m, a * 512:(a + 1) * 512], start=(m == 0), stop=(m == KD - 1))
                    last.then_inc(h_ready, 1)
                    if i:
                        turn(i - 1)
                turn(4)

            def peer():
                def queries(n):
                    m, t0, t1 = n % (2 * PH), *QSPANS[n // (2 * PH)]
                    w = (t1 - t0) // 2
                    pe.wait_ge(wq_loaded[n % 3], 16 * (n // 3 + 1))
                    if n >= 2:
                        pe.wait_ge(qp_copied, n - 1)
                    for a in range(2):
                        for k in range(KD):
                            last = pe.matmul(bank(QBANKS[n % 2] + a, w), wq[n % 3][:, k, :],
                                             hT[:, k, t0 + a * w:t0 + (a + 1) * w], start=(k == 0), stop=(k == KD - 1))
                    last.then_inc(qp_ready, 1)

                for m in range(2 * PH):
                    queries(m)
                pe.wait_ge(qp_copied, 2 * PH)
                pe.wait_ge(subk_loaded, 16)

                def key_scores(i):
                    t0, nt = TILES[i]
                    if i:
                        pe.wait_ge(sc_copied, i)
                    for m in range(2 * PH):
                        last = pe.matmul(ps[0:nt, m * 128:(m + 1) * 128], qpT[:, m, t0:t0 + nt], subk[:, m, :],
                                         start=True, stop=True)
                    last.then_inc(sc_ready, 1)

                key_scores(0)
                for m in range(2 * PH, 4 * PH):
                    queries(m)
                pe.wait_ge(qp_copied, 4 * PH)
                for i, (t0, nt) in enumerate(TILES):
                    if i < 4:
                        key_scores(i + 1)
                    if i:
                        pe.wait_ge(ln_done, 5 + i)
                    for k in range(NE):
                        n = gather_no(i, 1, k)
                        if by_dve[n]:
                            continue
                        pe.wait_ge(row_loaded[n % NR], 16 * (n // NR + 1))
                        pe.wait_ge(dp_ready, read_before[n] + 1)
                        for a in range(2):
                            last = pe.matmul(bank(4 + a, 512, 0, nt), diag_p[read_before[n] % ND][0:nt, 0:nt],
                                             rows[n % NR][0:nt, a * 512:(a + 1) * 512],
                                             start=(k == 0), stop=(k == NE - 2))
                        last.then_inc(pe_used, 1)

            project()
            end_phase(pe, 1)
            prompt()
            end_phase(pe, 2)
            sample()
            end_phase(pe, 3)
            merge()
            end_phase(pe, 4)
            peer()

        @block.scalar
        def _(act):
            done = [0]

            def step(ins):
                done[0] += 1
                ins.then_inc(act_seq, 1)
                act.wait_ge(act_seq, done[0])

            def project():
                act.dma_start(w_f[:], io["w_f"]).then_inc(f_w_loaded, 16)
                act.dma_start(bf[0:NH, :], io["b_forget"]).then_inc(f_w_loaded, 16)
                act.dma_start(w_v[:], io["w_v"]).then_inc(v_w_loaded, 16)
                for m, (h0, nh, rope, scale) in enumerate(PROJ):
                    n = 64 * nh
                    act.wait_ge(z_ready, m + 1)
                    if rope:
                        if m >= 2:
                            act.wait_ge(rope_done, m - 1)
                        act.activation(split(zsb[m % 2])[0:n], halves(2 * (m % 2), n), ACT.Copy,
                                       scale=scale).then_inc(z_copied, 1)
                    else:
                        z = halves(2 * (m % 2))
                        act.activation(split(heads[0:64, h0, :]), z[0:64], ACT.Copy, scale=scale)
                        act.activation(split(heads[0:64, h0 + 1, :]), z[64:128], ACT.Copy,
                                       scale=scale).then_inc(z_copied, 1)
                act.wait_ge(f_ready, 1)
                act.wait_ge(f_w_loaded, 32)
                step(act.activation(split(f_z), halves(6, NH), ACT.Identity, bias=bf[0:NH, :]))
                step(act.activation(f_tmp, f_z, ACT.Abs))
                step(act.activation(f_tmp, f_tmp, ACT.Exp, scale=-1.0))
                act.activation(f_tmp, f_tmp, ACT.Ln, bias=1.0).then_inc(f_act, 1)
                for i, (t0, nt) in enumerate(TILES):
                    n = NPROJ + i
                    act.wait_ge(z_ready, n + 1)
                    b = 2 * (n % 2)
                    act.activation(vtm[0:nt, i, :], ps[0:nt, b * 512:b * 512 + VW], ACT.Copy).then_inc(z_copied, 1)
                act.wait_ge(zero_set, 1)
                act.wait_ge(z_copied, NPROJ + 5)
                for h in range(NH):
                    for e in range(2):
                        half = h % 2
                        dst = qs.rearrange("p (b e) h c -> p b e h c", e=2)[
                            64 * half:64 * half + 64, :, e, h // 2, e * 64 + h * 8:e * 64 + h * 8 + 8]
                        src = heads[0:64, QB + h, LP:T].rearrange("p (b e t) -> p b e t", e=2, t=SN)[:, :, e, :]
                        last = act.activation(dst, src, ACT.Copy)
                    last = act.activation(kbn[64 * half:64 * half + 64, h // 2, :], heads[0:64, KB + h, LP:T], ACT.Copy)
                last.then_inc(spread_a, 1)

            def prompt():
                def move(u):
                    _, i, h, n = units[u]
                    q0, nq, seen = QTILES[i]
                    act.wait_ge(pt_ready, u + 1)
                    if u >= 2:
                        act.wait_ge(o_ready, u - 1)
                    full, rest = seen // 128, seen % 128
                    c0 = (4 + u % 2) * 512
                    last = act.activation(probT[u % 2][:, 0:full * nq], ps[:, c0:c0 + full * nq], ACT.Copy)
                    if rest:
                        last = act.activation(probT[u % 2][0:rest, full * nq:(full + 1) * nq],
                                              ps[0:rest, c0 + full * nq:c0 + (full + 1) * nq], ACT.Copy)
                    last.then_inc(pt_copied, 1)

                for u in range(NU + 2):
                    if u < NU:
                        kind, i, h, n = units[u]
                        q0, nq, seen = QTILES[i]
                        if kind == "fox" and h == 0 and i:
                            for hi in range(NI):
                                ni, a = idx_use[i, hi], NI * (i - 1) + hi
                                act.wait_ge(s_ready, ni + 1)
                                if a >= 2:
                                    act.wait_ge(idx_added, a - 1)
                                act.activation(relu[a % 2][0:nq, 0:seen],
                                               ps[0:nq, (ni % 2) * 1024:(ni % 2) * 1024 + seen], ACT.Relu
                                               ).then_inc(s_read, 1)
                        act.wait_ge(negmax_ready, u + 1)
                        if u >= 3:
                            act.wait_ge(pt_ready, u - 2)
                        act.activation(prob[u % 3][0:nq, 0:seen], ps[0:nq, (n % 2) * 1024:(n % 2) * 1024 + seen],
                                       ACT.Exp, bias=col(COL_NEGMAX + u % 3, p=nq),
                                       accum_out=col(COL_RSUM + u % 3, p=nq)).then_inc(s_read, 1)
                    if u >= 2:
                        move(u - 2)

            def sample():
                for c in range(5):
                    w = 512 if c < 4 else SN
                    for g in range(2):
                        act.wait_ge(ia_ready, 2 * c + g + 1)
                        if c:
                            act.wait_ge(ib_ready, c)
                        act.activation(relu_s[g][:, 0:w], bank(g, w), ACT.Relu).then_inc(relu_done, 1)
                n = 0
                for q in range(8):
                    fox, pr = q < 4, q % 4
                    act.wait_ge(smax_ready, q + 1)
                    if q:
                        act.wait_ge(st_ready, 5 * q)
                    else:
                        act.wait_ge(tail_ready, 1)
                    act.activation(prob_s, ps[:, 0:KEYS], ACT.Exp, bias=col(COL_SMAX),
                                   accum_out=col(COL_SSUM)).then_inc(sx_done, 1)
                    for c in range(5):
                        act.wait_ge(st_ready, n + 1)
                        if c < 4:
                            act.activation(probT_s[n % 2], bank(5 + n % 2), ACT.Copy).then_inc(st_copied, 1)
                        else:
                            if q:
                                act.wait_ge(so_ready, q)
                            act.activation(probTn, bank(5 + n % 2, 128, 0, SN), ACT.Copy).then_inc(st_copied, 1)
                        n += 1
                    act.wait_ge(so_ready, q + 1)
                    out = ps[:, 7 * 512:7 * 512 + 128]
                    for half in range(2):
                        y = (ybT if fox else yaT)[64 * half:64 * half + 64, :, LP + pr * 16:LP + pr * 16 + 16]
                        if fox:
                            src = out[64 * half:64 * half + 64].rearrange("p (e a h t) -> p e a h t", e=2, a=4, h=2)
                            last = act.activation(y.rearrange("p a (e t) -> p e a t", e=2), src[:, :, :, half, :],
                                                  ACT.Copy)
                            continue
                        for g in range(NKV):
                            src = out[64 * g:64 * g + 64].rearrange("p (e a h t) -> p e a h t", e=2, a=4, h=2)
                            last = act.activation(y[:, 2 * g:2 * g + 2, :].rearrange("p a (e t) -> p e a t", e=2),
                                                  src[:, :, 2 * g:2 * g + 2, half, :], ACT.Copy)
                    last.then_inc(so_copied, 1)

            def merge():
                for m in range(KD):
                    for j in range(2):
                        act.wait_ge(mix_ready, 4 * m + j + 1)
                        if m:
                            act.wait_ge(mix_done, m)
                        act.activation(split(sig[j]), halves(2 * j), ACT.Sigmoid).then_inc(sig_done, 1)

                def turned(i):
                    t0, nt = TILES[i]
                    act.wait_ge(ht_ready, i + 1)
                    act.activation(hT[:, :, t0:t0 + nt],
                                   ps[:, 4 * 512:6 * 512].rearrange("p (k c) -> p k c", k=KD)[:, :, 0:nt],
                                   ACT.Copy).then_inc(ht_copied, 1)

                for i, (t0, nt) in enumerate(TILES):
                    root(i, nt)
                    if i:
                        turned(i - 1)
                turned(4)

            def root(n, nt):
                act.wait_ge(var_ready, n + 1)
                act.activation(col(COL_STD, p=nt), col(COL_MV + 1, p=nt), ACT.Sqrt,
                               bias=const("eps", nt)).then_inc(std_ready, 1)

            def peer():
                def queries(n):
                    t0, t1 = QSPANS[n // (2 * PH)]
                    w = (t1 - t0) // 2
                    b = QBANKS[n % 2]
                    act.wait_ge(qp_ready, n + 1)
                    act.activation(split(qpT[:, n % (2 * PH), t0:t1]),
                                   ps[:, b * 512:(b + 2) * 512].rearrange("p (a c) -> p a c", a=2)[:, :, 0:w],
                                   ACT.Copy).then_inc(qp_copied, 1)

                for m in range(2 * PH):
                    queries(m)

                def key_scores(i):
                    nt = TILES[i][1]
                    act.wait_ge(sc_ready, i + 1)
                    if i:
                        act.wait_ge(ids_ready, i)
                    act.activation(sc[0:nt].rearrange("p a b -> p (a b)"), ps[0:nt, 0:2048], ACT.Copy
                                   ).then_inc(sc_copied, 1)

                def gate_exp(i):
                    nt = TILES[i][1]
                    act.wait_ge(gexp_in, i + 1)
                    act.activation(gexp[0:nt], gate[0:nt], ACT.Exp).then_inc(gexp_out, 1)

                key_scores(0)
                gate_exp(0)
                for i, (t0, nt) in enumerate(TILES):
                    for g in range(4):
                        for m in range(4 * g, 4 * g + 4) if i == 0 else ():
                            queries(2 * PH + m)
                        act.wait_ge(dve_used, read_before[gather_no(i, 0, 32 * g + 31)] + 1)
                        if i or g:
                            act.wait_ge(coef_ready, 4 * i + g)
                        act.activation(gl[0:nt, 32 * g:32 * g + 32], pre[0:nt, 32 * g:32 * g + 32], ACT.Gelu
                                       ).then_inc(gelu_done, 1)
                    if i < 4:
                        key_scores(i + 1)
                    for k in range(NE):
                        n = gather_no(i, 1, k)
                        if by_dve[n]:
                            continue
                        r_ = read_before[n]
                        act.wait_ge(coef_ready, 4 * i + k // 32 + 1)
                        if r_ >= ND:
                            act.wait_ge(pe_used, r_ - ND + 1)
                        act.activation(diag_p[r_ % ND][0:nt, 0:nt], ident[0:nt, 0:nt], ACT.Copy,
                                       scale=coef[i % 2][0:nt, k:k + 1]).then_inc(dp_ready, 1)
                        if i < 4 and k == GATE_AT:
                            gate_exp(i + 1)
                    root(5 + i, nt)

            project()
            end_phase(act, 1)
            prompt()
            end_phase(act, 2)
            sample()
            end_phase(act, 3)
            merge()
            end_phase(act, 4)
            peer()

        @block.vector
        def _(dve):
            done = [0]

            def step(ins):
                done[0] += 1
                ins.then_inc(dve_seq, 1)
                dve.wait_ge(dve_seq, done[0])

            def project():
                dve.wait_ge(x_loaded, 64)
                for m in ROPES:
                    h0, nh, _, _ = PROJ[m]
                    n = 64 * nh
                    dve.wait_ge(rot_ready, m + 1)
                    step(dve.tensor_tensor(split(rot_s)[0:n], halves(4, n), split(const("sin", n)), ALU.mult))
                    step(dve.tensor_tensor(zsb[m % 2][0:n], zsb[m % 2][0:n], const("cos", n), ALU.mult))
                    for j in range(nh):
                        p0 = 64 * j
                        last = dve.tensor_tensor(heads[0:64, h0 + j, :], zsb[m % 2][p0:p0 + 64], rot_s[p0:p0 + 64],
                                                 ALU.add)
                    last.then_inc(rope_done, 1)
                    dve.wait_ge(rope_done, m + 1)
                dve.wait_ge(f_act, 1)
                step(dve.scalar_tensor_tensor(f_log, f_z, 0.0, f_tmp, ALU.min, ALU.subtract))
                step(dve.tensor_tensor_scan(f_sum, const("restart", NH), f_log, 0.0, ALU.mult, ALU.add))
                dve.tensor_scalar(f_z, f_sum, -1.0, None, ALU.mult).then_inc(logf_ready, 1)
                dve.wait_ge(zero_set, 1)
                for h in range(NH):
                    for e in range(2):
                        g = h // 4
                        dst = qas.rearrange("p (b e) c -> p b e c", e=2)[
                            64 * g:64 * g + 64, :, e, e * 64 + h * 8:e * 64 + h * 8 + 8]
                        src = heads[0:64, QA + h, LP:T].rearrange("p (b e t) -> p b e t", e=2, t=SN)[:, :, e, :]
                        dve.tensor_copy(dst, src)
                for h in range(NI):
                    for e in range(2):
                        for pp in range(2):
                            c0 = (2 * pp + e) * 32 + h * 8
                            dst = qis.rearrange("p (a b) c -> p a b c", b=2)[64 * e:64 * e + 64, :, pp, c0:c0 + 8]
                            src = heads[0:64, QI + h, LP:T].rearrange(
                                "p (a b e t) -> p a b e t", b=2, e=2, t=SN)[:, :, pp, e, :]
                            dve.tensor_copy(dst, src)
                for g in range(NKV):
                    dve.tensor_copy(kan[64 * g:64 * g + 64, :], heads[0:64, KA + g, LP:T])
                for e in range(2):
                    last = dve.tensor_copy(
                        kin[64 * e:64 * e + 64, :, :],
                        heads[0:64, KI, LP:T].rearrange("p (a e t) -> p a e t", e=2, t=SN)[:, :, e, :])
                last.then_inc(spread_d, 1)

            def take8(v, top8):
                step(dve.max(top8, v))
                step(dve.match_replace(v, top8, v, TAKEN))

            def prompt():
                dve.tensor_copy(ident_b, ident)
                dve.tensor_copy(newc_b, const("new_causal"))
                dve.tensor_copy(row_of_b, row_of)
                dve.tensor_copy(causal_b, causal).then_inc(masks_ready, 1)
                for i in range(1, 5):
                    nt = QTILES[i][1]
                    step(dve.tensor_scalar(vtm[0:nt, i, 640:VW], vtm[0:nt, i, 640:VW], IDX_SCALE, None, ALU.mult))

                def weights(u):
                    _, i, h, n = units[u]
                    q0, nq, seen = QTILES[i]
                    dve.wait_ge(s_read, n + 1)
                    step(dve.reciprocal(col(COL_RINV + u % 3, p=nq), col(COL_RSUM + u % 3, p=nq)))
                    if u >= 3:
                        dve.wait_ge(pt_ready, u - 2)
                    dve.tensor_scalar(diag[u % 3][0:nq, 0:nq], ident[0:nq, 0:nq], col(COL_RINV + u % 3, p=nq),
                                      None, ALU.mult).then_inc(diag_ready, 1)

                def result(u):
                    kind, i, h, n = units[u]
                    q0, nq, seen = QTILES[i]
                    dve.wait_ge(o_ready, u + 1)
                    p0, c0 = 64 * (h % 2), 6 * 512 + 128 * (u % 2)
                    y = ybT if kind == "fox" else yaT
                    dve.tensor_copy(y[p0:p0 + 64, h // 2, q0:q0 + nq], ps[p0:p0 + 64, c0:c0 + nq]
                                    ).then_inc(o_copied, 1)

                for u in range(NU + 4):
                    if u < NU:
                        kind, i, h, n = units[u]
                        q0, nq, seen = QTILES[i]
                        v = isc[0:nq, 0:seen]
                        if kind == "fox" and h == 0 and i:
                            for hi in range(NI):
                                a = NI * (i - 1) + hi
                                w = vtm[0:nq, i, 640 + hi:641 + hi]
                                dve.wait_ge(s_read, idx_use[i, hi] + 1)
                                rl = relu[a % 2][0:nq, 0:seen]
                                if hi == 0:
                                    dve.tensor_scalar(v, rl, w, None, ALU.mult).then_inc(idx_added, 1)
                                else:
                                    dve.scalar_tensor_tensor(v, rl, w, v, ALU.mult, ALU.add).then_inc(idx_added, 1)
                                dve.wait_ge(idx_added, a + 1)
                            own = isc[0:nq, seen - nq:seen]
                            step(dve.tensor_tensor(own, own, causal[0:nq, 0:nq], ALU.add))
                        dve.wait_ge(s_ready, n + 1)
                        if u >= 3:
                            dve.wait_ge(s_read, units[u - 3][3] + 1)
                        dve.tensor_reduce(col(COL_NEGMAX + u % 3, p=nq),
                                          ps[0:nq, (n % 2) * 1024:(n % 2) * 1024 + seen], AX_X, ALU.max,
                                          negate=True).then_inc(negmax_ready, 1)
                    if 1 <= u <= NU:
                        weights(u - 1)
                    if u >= 4:
                        result(u - 4)
                    if u < NU and kind == "fox" and i:
                        for _r in range(ROUNDS_P // NH):
                            take8(v, col(COL_TOP8, 8, nq))
                        if h == NH - 1:
                            if i > 1:
                                dve.wait_ge(s_ready, units[u - NH][3] + 1)
                            dve.tensor_scalar(maskb[0:nq, 0:seen], v, TAKEN, NEG, ALU.not_equal, ALU.mult
                                              ).then_inc(mask_ready, 1)

            def sample():
                dve.wait_ge(wrow_loaded, 16 * 32)
                step(dve.tensor_scalar(wd[:, 0, :], w_place[:, 0, :], wrow[:, 0:1], IDX_SCALE, ALU.mult, ALU.mult))
                dve.tensor_scalar(wd[:, 1, :], w_place[:, 1, :], wrow[:, 1:2], IDX_SCALE, ALU.mult, ALU.mult
                                  ).then_inc(wd_ready, 1)
                dve.tensor_scalar(lidx, page_rows, 8.0, const("head_no", 64), ALU.mult, ALU.add).then_inc(lidx_ready, 1)
                for c in range(5):
                    w = 512 if c < 4 else SN
                    dve.wait_ge(ib_ready, c + 1)
                    dve.tensor_copy(isamp[:, c * 512:c * 512 + w], bank(2 + c % 2, w, 0, 64)).then_inc(ib_copied, 1)
                dve.wait_ge(ib_copied, 5)
                step(dve.tensor_tensor(isamp[:, PAST:KEYS], isamp[:, PAST:KEYS], const("idx_causal", 64), ALU.add))
                step(dve.memset(tail[:, 0:1], 0.0))
                dve.wait_ge(lp_loaded, 16 * NPG)
                dve.wait_ge(lf_ones, 1)
                dve.wait_ge(tail_new, 16 * NB)
                dve.tensor_tensor_scan(tail[:, 1:PAST], prob_s[0:64, 1:PAST], lp[:, 0:PAST - 1], 0.0,
                                       ALU.mult, ALU.add).then_inc(tail_ready, 1)
                for q in range(8):
                    dve.wait_ge(ss_ready, q + 1)
                    if q:
                        dve.wait_ge(sx_done, q)
                    dve.tensor_reduce(col(COL_SMAX), ps[:, 0:KEYS], AX_X, ALU.max, negate=True
                                      ).then_inc(smax_ready, 1)
                    dve.wait_ge(sx_done, q + 1)
                    step(dve.reciprocal(col(COL_SINV), col(COL_SSUM)))
                    if q:
                        dve.wait_ge(st_ready, 5 * q)
                    dve.tensor_scalar(diag_s, ident, col(COL_SINV), None, ALU.mult).then_inc(sdiag_ready, 1)
                    if q < 4:
                        for _r in range(ROUNDS_S // 4):
                            take8(isamp, col(COL_TOPS, 8, 64))
                        if q == 3:
                            dve.tensor_scalar(smask, isamp, TAKEN, NEG, ALU.not_equal, ALU.mult
                                              ).then_inc(smask_ready, 1)

            def normalise(n, v, y, nt):
                for a in range(2):
                    step(dve.bn_stats(col(COL_BN + 6 * a, 6, nt), v[:, a * 512:(a + 1) * 512]))
                dve.bn_aggr(col(COL_MV, 2, nt), col(COL_BN, 12, nt)).then_inc(var_ready, 1)
                dve.wait_ge(std_ready, n + 1)
                step(dve.reciprocal(col(COL_RSTD, p=nt), col(COL_STD, p=nt)))
                step(dve.tensor_scalar(v, v, col(COL_MV, p=nt), col(COL_RSTD, p=nt), ALU.subtract, ALU.mult))
                step(dve.tensor_tensor(v, v, lng[0:nt], ALU.mult))
                dve.tensor_tensor(y, v, lnb[0:nt], ALU.add).then_inc(ln_done, 1)

            def merge():
                for m in range(KD):
                    for j in range(2):
                        dve.wait_ge(sig_done, 2 * m + j + 1)
                        dve.wait_ge(mix_ready, 4 * m + 2 + j + 1)
                        step(dve.tensor_tensor(split(sig[j]), split(sig[j]), halves(4 + 2 * j), ALU.mult))
                    dve.tensor_tensor(mergedT[:, m, :], sig[0], sig[1], ALU.add).then_inc(mix_done, 1)
                for i, (t0, nt) in enumerate(TILES):
                    v = hrow[0:nt, i, :]
                    dve.wait_ge(h_ready, i + 1)
                    dve.wait_ge(xr_loaded[i % 2], 16 * (i // 2 + 1))
                    b = 2 * (i % 2)
                    dve.scalar_tensor_tensor(v, xrow[i % 2][0:nt], ALPHA, ps[0:nt, b * 512:b * 512 + D],
                                             ALU.mult, ALU.add).then_inc(res_done, 1)
                    dve.wait_ge(res_done, i + 1)
                    if i == 0:
                        dve.wait_ge(ln_loaded, 32)
                    normalise(i, v, v, nt)

            def top16(v, vals, places):
                step(dve.max(vals[:, 0:8], v))
                step(dve.max_index(places[:, 0:8], vals[:, 0:8], v))
                step(dve.match_replace(v, vals[:, 0:8], v, TAKEN))
                step(dve.max(vals[:, 8:16], v))
                step(dve.max_index(places[:, 8:16], vals[:, 8:16], v))

            def route(i, s):
                nt = TILES[i][1]
                if s == 0:
                    dve.wait_ge(sc_copied, i + 1)
                if s < 16:
                    top16(sc[0:nt, s, :], sv[0:nt, s, :], si[0:nt, s, :])
                    return
                h = s - 16
                sv4 = sv.rearrange("p (h c) a -> p h c a", c=2)
                siF4 = siF.rearrange("p (h c) a -> p h c a", c=2)
                if h < PH:
                    cd = cand[0:nt, h, :]
                    step(dve.tensor_tensor(cd.rearrange("p (a b) -> p a b", a=PK),
                                           sv4[0:nt, h, 0, :, None].to_broadcast([nt, PK, PK]),
                                           sv4[0:nt, h, 1, None, :].to_broadcast([nt, PK, PK]), ALU.add))
                    top16(cd, top[0:nt, h, :], tj[0:nt, h, :])
                elif s == 24:
                    dve.tensor_tensor(gate[0:nt], top[0:nt], top[0:nt, :, 0:1].to_broadcast([nt, PH, PK]),
                                      ALU.subtract).then_inc(gexp_in, 1)
                    step(dve.tensor_copy(siF[0:nt], si[0:nt]))
                    step(dve.tensor_scalar(jbits[0:nt], tj[0:nt], 4, None, ALU.logical_shift_right))
                    step(dve.tensor_copy(ja[0:nt], jbits[0:nt]))
                elif s == 25:
                    step(dve.tensor_scalar(jbits[0:nt], tj[0:nt], 15, None, ALU.bitwise_and))
                    step(dve.tensor_copy(jb[0:nt], jbits[0:nt]))
                elif s in (26, 27, 28, 29):
                    c, first = divmod(s - 26, 2)
                    jx, ex = ((ja, e0), (jb, e1))[c]
                    o4 = oh[0:nt].rearrange("p (h k) a -> p h k a", h=PH)
                    if first == 0:
                        step(dve.tensor_tensor(
                            oh[0:nt], jx[0:nt].rearrange("p h k -> p (h k)")[:, :, None].to_broadcast([nt, NE, PK]),
                            const("iota16", nt)[:, None, :].to_broadcast([nt, NE, PK]), ALU.is_equal))
                    else:
                        step(dve.tensor_tensor(o4, o4, siF4[0:nt, :, c, None, :].to_broadcast([nt, PH, PK, PK]),
                                               ALU.mult))
                        step(dve.tensor_reduce(ex[0:nt].rearrange("p h k -> p (h k)"), oh[0:nt], AX_X, ALU.add))
                elif s == 30:
                    dve.scalar_tensor_tensor(ids[i % 2][0:nt], e0[0:nt].rearrange("p h k -> p (h k)"), 128.0,
                                             e1[0:nt].rearrange("p h k -> p (h k)"), ALU.mult, ALU.add
                                             ).then_inc(ids_ready, 1)
                elif s == 31:
                    dve.wait_ge(gexp_out, i + 1)
                    step(dve.tensor_reduce(col(COL_GSUM, PH, nt), gexp[0:nt], AX_X, ALU.add))
                    step(dve.reciprocal(col(COL_GINV, PH, nt), col(COL_GSUM, PH, nt)))
                    step(dve.tensor_tensor(gate[0:nt], gexp[0:nt],
                                           col(COL_GINV, PH, nt)[:, :, None].to_broadcast([nt, PH, PK]), ALU.mult))

            def peer():
                for s in range(32):
                    route(0, s)
                for i, (t0, nt) in enumerate(TILES):
                    h = hrow[0:nt, i, :]

                    def coefs(g):
                        dve.wait_ge(gelu_done, 4 * i + g + 1)
                        gf = gate[0:nt].rearrange("p h k -> p (h k)")
                        dve.tensor_tensor(coef[i % 2][0:nt, 32 * g:32 * g + 32], gf[:, 32 * g:32 * g + 32],
                                          gl[0:nt, 32 * g:32 * g + 32], ALU.mult).then_inc(coef_ready, 1)

                    for k in range(NE):
                        n = gather_no(i, 0, k)
                        dve.wait_ge(row_loaded[n % NR], 16 * (n // NR + 1))
                        dve.tensor_tensor_reduce(out=rows[n % NR][0:nt], in0=rows[n % NR][0:nt], in1=h, scale=1.0,
                                                 scalar=0.0, op0=ALU.mult, op1=ALU.add,
                                                 accum_out=pre[0:nt, k:k + 1]).then_inc(dve_used, 1)
                        if k >= 32 and k % 32 == 4:
                            coefs(k // 32 - 1)
                    coefs(3)
                    dve.wait_ge(coef_ready, 4 * i + 4)
                    if i:
                        dve.wait_ge(y_stored, 16 * i)
                    mine = [k for k in range(NE) if by_dve[gather_no(i, 1, k)]]
                    for j, k in enumerate(mine):
                        n = gather_no(i, 1, k)
                        dve.wait_ge(row_loaded[n % NR], 16 * (n // NR + 1))
                        c = coef[i % 2][0:nt, k:k + 1]
                        if j == 0:
                            ins = dve.tensor_scalar(facc[0:nt], rows[n % NR][0:nt], c, None, ALU.mult)
                        else:
                            ins = dve.scalar_tensor_tensor(facc[0:nt], rows[n % NR][0:nt], c, facc[0:nt],
                                                           ALU.mult, ALU.add)
                        ins.then_inc(dve_used, 1)
                        dve.wait_ge(dve_used, read_before[n] + 1)
                        if i < 4 and j < 32:
                            route(i + 1, j)
                    dve.wait_ge(pe_used, read_before[gather_no(i, 1, NE - 2)] + 1)
                    step(dve.tensor_tensor(facc[0:nt], facc[0:nt], ps[0:nt, 4 * 512:4 * 512 + D], ALU.add))
                    step(dve.scalar_tensor_tensor(facc[0:nt], h, ALPHA, facc[0:nt], ALU.mult, ALU.add))
                    if i == 0:
                        dve.wait_ge(ln2_loaded, 32)
                    normalise(5 + i, facc[0:nt], facc[0:nt], nt)

            project()
            end_phase(dve, 1)
            prompt()
            end_phase(dve, 2)
            sample()
            end_phase(dve, 3)
            merge()
            end_phase(dve, 4)
            peer()


_OUTS = {"y_out": (T, D), "k_out": (HD, 11, T), "v_out": (T, VW), "logf_out": (NH, T)}


def lay_out(i):
    c = np.ascontiguousarray
    x = np.concatenate([i["meta_tokens"], i["x_prompt"][0], i["x_sample"].reshape(NS, D)], axis=0)
    w = i["w_in"][0]
    cuts = np.cumsum([0, 512, 128, 128, 256, 64, 4, 512, 512, 512, 8, D, D])
    wqa, wka, wva, wqi, wki, wwi, wqb, wkb, wvb, wf, wga, wgb = (w[:, a:b] for a, b in zip(cuts[:-1], cuts[1:]))

    def chunks(a):
        return a.reshape(-1, 128, a.shape[1]).transpose(1, 0, 2)

    def column_tiles(a):
        return chunks(a).reshape(128, a.shape[0] // 128, -1, 128).transpose(2, 0, 1, 3)

    pad = np.zeros((D, 64), np.float32)
    mix = np.concatenate([column_tiles(a) for a in (wga, wgb, i["w_branch_a"][0], i["w_branch_b"][0])], axis=2)
    table = i["page_table"]
    back = table[:, ::-1]
    kb = i["cache_k_b"][0, :, ::-1].transpose(0, 2, 3, 1)
    ka = i["cache_k_a"][0].transpose(0, 2, 3, 1).reshape(NPOOL, 128, PAGE)
    out = {
        "cst": tables(),
        "xT": chunks(x.T),
        "x": x,
        "w_proj": column_tiles(np.concatenate([wqa, wka, wqi, wki, pad, wqb, wkb], axis=1)),
        "w_v": chunks(np.concatenate([wvb, wva, wwi], axis=1)),
        "w_f": chunks(wf),
        "b_forget": i["b_forget"].reshape(NH, 1),
        "pages": np.concatenate([table.reshape(1, -1), back.reshape(1, -1)], axis=1),
        "page_rows": np.repeat(back, NH, axis=0),
        "kidx": i["cache_k_idx"][0].transpose(0, 2, 1),
        "k_b": kb.reshape(NPOOL, 4, 128, PAGE).transpose(0, 2, 1, 3).reshape(NPOOL, 128, 512),
        "v_b": i["cache_v_b"][0, :, ::-1].reshape(NPOOL, PAGE, 512),
        "kv_a": np.concatenate([ka, i["cache_v_a"][0].reshape(NPOOL, PAGE, 128)], axis=2),
        "logf_b": i["cache_logf_b"][0, :, ::-1].transpose(0, 2, 1).reshape(NPOOL * NH, PAGE),
        "w_mix": mix,
        "w_out": chunks(i["w_out"][0]),
        "ln": np.concatenate([i["ln1_g"], i["ln1_b"], i["ln2_g"], i["ln2_b"]], axis=0),
        "w_q": column_tiles(i["peer_w_q"][0]),
        "subk": i["peer_sub_keys"][0].transpose(3, 1, 0, 2).reshape(128, 2 * PH, 128),
        "peer_u": i["peer_u"][0],
        "peer_v": i["peer_v"][0],
    }
    return {k: c(v) for k, v in out.items()}


def give_back(r):
    y, k, v, f = r["y_out"], r["k_out"].transpose(2, 1, 0), r["v_out"], r["logf_out"].T
    rows_ = {"k_a": k[:, 0:2], "v_a": v[:, 512:640].reshape(T, NKV, HD), "k_i": k[:, 2], "k_b": k[:, 3:11],
             "v_b": v[:, 0:512].reshape(T, NH, HD), "f": f}
    prompt = [a[None, None, 0:LP] for a in rows_.values()]
    sample = [a[LP:T].reshape((1, NB, SN) + a.shape[1:]) for a in rows_.values()]
    return (y[None, N_META:LP], y[LP:T].reshape(NB, SN, D), *prompt, *sample)


def kernel(**inputs):
    import concourse.bacc as _bacc
    from concourse.bass_utils import run_bass_kernel_spmd as _run

    arrays = lay_out({k: np.asarray(v) for k, v in inputs.items()})
    nc = _bacc.Bacc("TRN2", target_bir_lowering=False, num_devices=1)
    io = {n: nc.dram_tensor(n, a.shape, mybir.dt.from_np(a.dtype), kind="ExternalInput").ap()
          for n, a in arrays.items()}
    for n, shape in _OUTS.items():
        io[n] = nc.dram_tensor(n, shape, F32, kind="ExternalOutput").ap()
    program(nc, io)
    got = _run(nc, [arrays], core_ids=[0]).results[0]
    return tuple(np.ascontiguousarray(a) for a in give_back(got))
```

```python
from contextlib import ExitStack

import numpy as np

import concourse.bass as bass
from concourse import mybir

ALU = mybir.AluOpType
ACT = mybir.ActivationFunctionType
F32 = mybir.dt.float32
U32 = mybir.dt.uint32
I32 = mybir.dt.int32
BF16 = mybir.dt.bfloat16
AX_X = mybir.AxisListType.X

D = 1024
KD = D // 128
N_META, SEQ = 16, 512
LP = N_META + SEQ
NB, SN = 8, 8
NS = NB * SN
T = LP + NS
HT = T // 2
HD = 64
NH = 8
NKV = 2
NI = 4
PAGE, NPG = 128, 16
PAST = PAGE * NPG
NPOOL = NB * NPG * 5 // 4
KEYS = PAST + SN
ATTN_SCALE = HD ** -0.5
IDX_SCALE = (64 * NI) ** -0.5
SEL_P = 128
SEL_S = 256
NEG = -1e30
TAKEN = -3e38
ALPHA = 2.0 ** 0.25
EPS = 1e-5
VW = NH * HD + NKV * HD + NI
PH, PK = 8, 16
NE = PH * PK
TILES = [(128 * i, min(128, T - 128 * i)) for i in range(5)]
QTILES = [(128 * i, min(128, LP - 128 * i), min(128 * (i + 1), LP)) for i in range(5)]

QB, KB, QA, KA, QI, KI = 0, 8, 16, 24, 26, 30
NHEADS = 31
PROJ = ([(QA + 2 * j, 2, True, ATTN_SCALE) for j in range(4)] + [(KA, 2, True, 1.0)]
        + [(QI + 2 * j, 2, True, 1.0) for j in range(2)] + [(KI, 1, True, 1.0)]
        + [(QB + 2 * j, 2, False, ATTN_SCALE) for j in range(4)]
        + [(KB + 2 * j, 2, False, 1.0) for j in range(4)])
NPROJ = len(PROJ)
ROPES = [m for m, p in enumerate(PROJ) if p[2]]

CONSTS = [("ident", 128), ("iota16", 16), ("eps", 1), ("causal", 128), ("rot", 128), ("row_of", 512),
          ("head_of", 512), ("new_causal", 8), ("idx_causal", 8), ("w_place", 128), ("head_no", 1),
          ("key_row", 1), ("part", 1), ("cos", T), ("sin", T), ("restart", T)]
CAT, _o = {}, 0
for _n, _w in CONSTS:
    CAT[_n] = (_o, _w)
    _o += _w
NCONST = _o
GATE_AT = 70


def tables():
    c = np.zeros((128, NCONST), np.float32)

    def put(name, a):
        o, w = CAT[name]
        c[:a.shape[0], o:o + w] = a.reshape(a.shape[0], w)

    p = np.arange(128)
    put("ident", np.eye(128, dtype=np.float32))
    put("causal", np.where(p[None, :] > p[:, None], np.float32(NEG), np.float32(0)))
    rot = np.zeros((128, 128), np.float32)
    for base in (0, 64):
        for j in range(8):
            rot[base + j + 8, base + j] = -1.0
            rot[base + j, base + j + 8] = 1.0
    put("rot", rot)
    row_of = np.zeros((64, 4, 128), np.float32)
    head_of = np.zeros((64, 4, 128), np.float32)
    for pr in range(4):
        for e in range(2):
            for h in range(NH):
                for t in range(SN):
                    col = e * 64 + h * 8 + t
                    row_of[(2 * pr + e) * 8 + t, pr, col] = 1.0
                    head_of[(2 * pr + e) * 8 + h, pr, col] = 1.0
    put("row_of", row_of)
    put("head_of", head_of)
    t = p % 8
    s = np.arange(8)
    put("new_causal", np.where(s[None, :] > t[:, None], np.float32(NEG), np.float32(0)))
    put("idx_causal", np.where(s[None, :] > t[:64, None], np.float32(NEG), np.float32(0)))
    wp = np.zeros((128, 2, 64), np.float32)
    for g in range(2):
        for b in range(4):
            for h in range(NI):
                for tt in range(SN):
                    wp[b * 32 + h * 8 + tt, g, (g * 4 + b) * 8 + tt] = 1.0
    put("w_place", wp)
    put("iota16", np.tile(np.arange(16, dtype=np.float32), (128, 1)))
    put("head_no", (p % 8).astype(np.float32)[:, None])
    put("key_row", (p % 64).astype(np.float32)[:, None])
    put("part", p.astype(np.float32)[:, None])
    put("eps", np.full((128, 1), EPS, np.float32))
    pos = np.concatenate([np.arange(LP), np.tile(PAST + np.arange(SN), NB)]).astype(np.float32)
    inv = np.power(np.float32(500000.0), -np.arange(8, dtype=np.float32) / np.float32(8))
    ang = (pos[None, :] * inv[:, None]).astype(np.float32).astype(np.float64)
    cos, sin = np.ones((128, T), np.float32), np.zeros((128, T), np.float32)
    for base in (0, 64):
        for half in (0, 8):
            cos[base + half:base + half + 8] = np.cos(ang)
            sin[base + half:base + half + 8] = np.sin(ang)
    put("cos", cos)
    put("sin", sin)
    restart = np.ones((8, T), np.float32)
    restart[:, 0] = 0.0
    restart[:, LP::SN] = 0.0
    put("restart", restart)
    return c


def program(nc, io):
    ctx = ExitStack()
    with ctx:
        arena = ctx.enter_context(nc.sbuf_tensor("arena", [128, 53100], F32))
        ps = ctx.enter_context(nc.psum_tensor("ps", [128, 8 * 512], F32))

        def sem(name):
            return ctx.enter_context(nc.semaphore(name))

        def sems(name, n):
            return [sem(f"{name}{i}") for i in range(n)]

        class Region:

            def __init__(self, at):
                self.at = at

            def take(self, *shape, p=128):
                n = int(np.prod(shape))
                v = arena[0:p, self.at:self.at + n]
                self.at += n
                assert self.at <= 53100, self.at
                if len(shape) == 2:
                    v = v.rearrange("p (a b) -> p a b", a=shape[0])
                elif len(shape) == 3:
                    v = v.rearrange("p (a b c) -> p a b c", a=shape[0], b=shape[1])
                return v

        def bank(b, w=512, p0=0, p1=128):
            return ps[p0:p1, b * 512:b * 512 + w]

        base = Region(0)
        consts = base.take(NCONST)

        def const(name, p=128):
            o, w = CAT[name]
            return consts[0:p, o:o + w]

        ident, causal = const("ident"), const("causal")
        row_of = const("row_of", 64).rearrange("p (a b) -> p a b", a=4)
        head_of = const("head_of", 64).rearrange("p (a b) -> p a b", a=4)
        w_place = const("w_place").rearrange("p (a b) -> p a b", a=2)
        small = base.take(128)
        ident_b, causal_b = base.take(64).bitcast(BF16), base.take(64).bitcast(BF16)
        newc_b = base.take(4).bitcast(BF16)
        row_of_b = base.take(256, p=64).bitcast(BF16).rearrange("p (a b) -> p a b", a=4)
        xT_at = base.at
        xT = base.take(KD, T)
        yaT, ybT = base.take(4, T), base.take(4, T)
        vtm_at = base.at
        vtm = base.take(5, VW)
        qs_at = base.at
        qs = base.take(NB, 4, 128)
        qas = base.take(NB, 128)
        qis = base.take(4, 128)
        zeroed = arena[:, qs_at:base.at]
        kbn, kan, kin = base.take(4, NS), base.take(NS), base.take(4, SN)
        wd = base.take(2, 64)
        wrow = base.take(2)
        pages = base.take(2 * NB * NPG, p=1).bitcast(I32)
        page_rows = base.take(NPG, p=64).bitcast(I32)
        lidx = base.take(NPG, p=64).bitcast(U32)
        after_base = base.at

        r = Region(after_base)
        heads = r.take(NHEADS, T)
        work_at = r.at
        wring = [r.take(KD, 128) for _ in range(3)]
        w_v = r.take(KD, VW)
        zsb = [r.take(T) for _ in range(2)]
        rot_s = r.take(T)
        w_f = r.take(KD, NH)
        bf = r.take(1)
        f_z, f_tmp, f_log, f_sum = (yaT[0:NH, j, :] for j in range(4))
        r = Region(work_at)
        prob = [r.take(640) for _ in range(3)]
        probT = [r.take(512) for _ in range(2)]
        diag = [r.take(128) for _ in range(3)]
        isc = r.take(640)
        relu = [r.take(640) for _ in range(2)]
        maskb = r.take(320).bitcast(BF16)
        log_at = r.at
        lp = Region(log_at).take(PAST, p=64)
        kidx_at = [xT_at, xT_at + 2048, log_at + PAST, log_at + PAST + 2048]
        kidx = [Region(a).take(2048) for a in kidx_at]
        r = Region(CAT["cos"][0])
        key_pages, kv_pages = r.take(4 * NPG).bitcast(I32), r.take(NB * NPG).bitcast(I32)
        key_rows, kv_rows = key_pages.bitcast(U32), kv_pages.bitcast(U32)
        smask = r.take(KEYS // 2, p=64).bitcast(BF16)
        relu_s = [r.take(512), Region(xT_at + 4096).take(512)]
        assert r.at <= NCONST
        r = Region(vtm_at)
        vnew = [r.take(2, VW, p=8) for _ in range(2)]
        diag_s, probTn = r.take(128), r.take(128, p=8)
        assert r.at <= qs_at
        NSLOT = 8
        r = Region(after_base)
        ring = [r.take(2048) for _ in range(NSLOT)]
        probT_s = r.take(4, 512)
        tail, isamp = r.take(KEYS, p=64), r.take(KEYS, p=64)
        prob_s = r.take(KEYS)
        osb = r.take(512)
        lf_one = probT_s[0:64].rearrange("p a b -> p (a b)")
        assert r.at <= kidx_at[2]
        KV_AT = [xT_at, kidx_at[2]] + [after_base + 4096 * j for j in range(4)]
        kv_pair = [Region(a).take(NPG, 256) for a in KV_AT]
        KV_SLOT = [0, 1, 2, 3, 4, 5, 1, 2]
        FILLS = [("k_b", 0), ("k_b", 1), ("v_b", 0), ("k_b", 2), ("v_b", 1), ("k_b", 3), ("v_b", 2), ("v_b", 3)]
        r = Region(vtm_at)
        hT = r.take(KD, T)
        subk = r.take(2 * PH, 128)
        peer_at = r.at
        r = Region(after_base)
        hrow = r.take(5, D)
        lng, lnb = r.take(D), r.take(D)
        peer2_at = r.at
        xrow = [r.take(D) for _ in range(2)]
        wmix = [r.take(3 * KD, 128) for _ in range(2)]
        mergedT = r.take(KD, T)
        w_out = r.take(KD, D)
        sig = [r.take(T) for _ in range(2)]
        r = Region(xT_at)
        qpT = r.take(2 * PH, T)
        assert r.at <= vtm_at and peer_at <= after_base
        r = Region(peer_at)
        sv = r.take(2 * PH, PK)
        si_at = r.at
        si = r.take(2 * PH, PK).bitcast(U32)
        siF = r.take(2 * PH, PK)
        top, gate, ja, jb, gexp = (r.take(PH, PK) for _ in range(5))
        tj = r.take(PH, PK).bitcast(U32)
        jbits = r.take(PH, PK).bitcast(U32)
        e0, e1 = r.take(PH, PK), r.take(PH, PK)
        ids = [r.take(NE).bitcast(U32) for _ in range(2)]
        assert r.at <= after_base, r.at - after_base
        r = Region(peer2_at)
        sc = r.take(2 * PH, 128)
        cand = r.take(PH, PK * PK)
        oh = r.take(NE, PK)
        facc = r.take(D)
        pre = r.take(NE)
        gl = r.take(NE)
        coef = [r.take(NE) for _ in range(2)]
        ND = 4
        diag_p = [r.take(128) for _ in range(ND)]
        NR = 14
        rows = [r.take(D) for _ in range(NR)]
        r = Region(CAT["causal"][0])
        wq = [r.take(KD, 128) for _ in range(3)]
        assert r.at <= NCONST

        x_loaded, v_w_loaded, f_w_loaded = sem("x_loaded"), sem("v_w_loaded"), sem("f_w_loaded")
        w_loaded = sems("w_loaded", 3)
        z_ready, z_copied = sem("z_ready"), sem("z_copied")
        rot_ready, rope_done = sem("rot_ready"), sem("rope_done")
        f_ready, f_act, logf_ready = sem("f_ready"), sem("f_act"), sem("logf_ready")
        ones_set, zero_set = sem("ones_set"), sem("zero_set")
        negc_stored, bias_loaded, v_stored = sem("negc_stored"), sem("bias_loaded"), sem("v_stored")
        k_stored, logf_stored, y_stored = sem("k_stored"), sem("logf_stored"), sem("y_stored")
        dve_seq, act_seq = sem("dve_seq"), sem("act_seq")
        phase = sem("phase")
        s_ready, s_read, negmax_ready = sem("s_ready"), sem("s_read"), sem("negmax_ready")
        idx_added, mask_ready, diag_ready = sem("idx_added"), sem("mask_ready"), sem("diag_ready")
        pt_ready, pt_copied = sem("pt_ready"), sem("pt_copied")
        o_ready, o_copied = sem("o_ready"), sem("o_copied")
        ring_loaded = sems("ring_loaded", NSLOT)
        slot_read, pair_read = sem("slot_read"), sem("pair_read")
        spread_a, spread_d = sem("spread_a"), sem("spread_d")
        wrow_loaded, wd_ready = sem("wrow_loaded"), sem("wd_ready")
        lidx_ready, lp_loaded, lf_ones = sem("lidx_ready"), sem("lp_loaded"), sem("lf_ones")
        tail_new, tail_ready = sem("tail_new"), sem("tail_ready")
        ia_ready, relu_done, ib_ready, ib_copied = (sem(n) for n in ("ia_ready", "relu_done", "ib_ready", "ib_copied"))
        smask_ready, ss_ready, smax_ready = sem("smask_ready"), sem("ss_ready"), sem("smax_ready")
        sx_done, sdiag_ready, st_ready, st_copied = (sem(n) for n in ("sx_done", "sdiag_ready", "st_ready", "st_copied"))
        so_ready, so_copied, se_ready, se_done = (sem(n) for n in ("so_ready", "so_copied", "se_ready", "se_done"))
        masks_ready, rows_loaded, kidx_loaded = sem("masks_ready"), sem("rows_loaded"), sems("kidx_loaded", 4)
        kv_loaded = sems("kv_loaded", NB)
        xT_loaded = sem("xT_loaded")
        vnew_loaded = sems("vnew_loaded", 2)
        mix_loaded, wo_loaded, ln_loaded = sems("mix_loaded", 2), sem("wo_loaded"), sem("ln_loaded")
        mix_ready, sig_done, mix_done = sem("mix_ready"), sem("sig_done"), sem("mix_done")
        xr_loaded, h_ready, res_done = sems("xr_loaded", 2), sem("h_ready"), sem("res_done")
        var_ready, std_ready, ln_done = sem("var_ready"), sem("std_ready"), sem("ln_done")
        ht_ready, ht_copied = sem("ht_ready"), sem("ht_copied")
        wq_loaded, qp_ready, qp_copied = sems("wq_loaded", 3), sem("qp_ready"), sem("qp_copied")
        subk_loaded, ln2_loaded = sem("subk_loaded"), sem("ln2_loaded")
        sc_ready, sc_copied, gexp_in, gexp_out = (sem(n) for n in ("sc_ready", "sc_copied", "gexp_in", "gexp_out"))
        ids_ready, row_loaded = sem("ids_ready"), sems("row_loaded", NR)
        dve_used, pe_used = sem("dve_used"), sem("pe_used")
        gelu_done, coef_ready, dp_ready = sem("gelu_done"), sem("coef_ready"), sem("dp_ready")

        csc = nc.dram_tensor("neg_cumulative", [NH, T], F32, kind="Internal").ap()

        def col(j, w=1, p=128):
            return small[0:p, j:j + w]

        COL_TOP8, COL_NEGMAX, COL_RSUM, COL_RINV = 8, 80, 84, 88
        COL_SMAX, COL_SSUM, COL_SINV, COL_TOPS = 16, 17, 18, 24
        COL_BN, COL_MV, COL_STD, COL_RSTD = 32, 48, 50, 52
        COL_TOPP, COL_GSUM, COL_GINV = 56, 64, 72

        def blocks(seen):
            return [(k, min(128, seen - k)) for k in range(0, seen, 128)]

        units, uses = [], []
        for i in range(5):
            if i:
                uses += [("idx", i, h) for h in range(NI)]
            for kind in ("fox", "dsa"):
                for h in range(NH):
                    units.append((kind, i, h, len(uses)))
                    uses.append((kind, i, h))
        NU = len(units)
        idx_use = {(i, h): n for n, (k, i, h) in enumerate(uses) if k == "idx"}
        ROUNDS_P, ROUNDS_S = SEL_P // 8, SEL_S // 8

        gathers = [(i, v, k) for i in range(5) for v in (0, 1) for k in range(NE)]
        by_dve = [v == 0 or k % 8 in ((3, 5, 7) if i < 4 else (1, 3, 5, 7)) for i, v, k in gathers]
        read_before = []
        n_dve = n_pe = 0
        for d in by_dve:
            read_before.append(n_dve if d else n_pe)
            n_dve, n_pe = n_dve + d, n_pe + (not d)

        QSPANS, QBANKS = ((0, 128), (128, T)), (4, 6)

        def gather_no(i, v, k):
            return (2 * i + v) * NE + k

        def halves(b, rows_=128):
            return ps[0:rows_, b * 512:(b + 2) * 512].rearrange("p (a c) -> p a c", a=2)[:, :, 0:HT]

        def split(v):
            return v.rearrange("p (a c) -> p a c", a=2)

        def end_phase(eng, n):
            eng.drain().then_inc(phase, 1)
            eng.wait_ge(phase, 5 * n)

        block = ctx.enter_context(nc.Block())

        @block.sync
        def _(sp):
            def project():
                sp.dma_start(xT[:], io["xT"]).then_inc(x_loaded, 16)
                for m in range(NPROJ):
                    if m >= 3:
                        sp.wait_ge(z_ready, m - 2)
                    sp.dma_start(wring[m % 3], io["w_proj"][m]).then_inc(w_loaded[m % 3], 16)
                    if m == 2:
                        sp.dma_start(consts[:], io["cst"]).then_inc(x_loaded, 16)
                        sp.dma_start(pages[:], io["pages"]).then_inc(x_loaded, 16)
                        sp.dma_start(page_rows[:], io["page_rows"]).then_inc(x_loaded, 16)
                sp.wait_ge(logf_ready, 1)
                sp.dma_start(io["logf_out"], f_log).then_inc(logf_stored, 16)
                sp.dma_start(csc, f_z).then_inc(negc_stored, 16)
                sp.wait_ge(negc_stored, 16)
                sp.dma_start(heads[64:65, KB:KB + NH, :],
                             csc.rearrange("(o h) t -> o h t", o=1)).then_inc(bias_loaded, 16)
                sp.wait_ge(z_copied, NPROJ + 5)
                for i, (t0, nt) in enumerate(TILES):
                    sp.dma_start(io["v_out"][t0:t0 + nt, :], vtm[0:nt, i, :]).then_inc(v_stored, 16)
                sp.wait_ge(rope_done, len(ROPES))
                sp.dma_start(io["k_out"][:, 0:2, :], heads[0:64, KA:KA + 2, :]).then_inc(k_stored, 16)
                sp.dma_start(io["k_out"][:, 2:3, :], heads[0:64, KI:KI + 1, :]).then_inc(k_stored, 16)
                sp.dma_start(io["k_out"][:, 3:11, :], heads[0:64, KB:KB + NH, :]).then_inc(k_stored, 16)
                sp.wait_ge(v_stored, 16 * 5)
                for g in range(2):
                    src = io["v_out"][LP + 32 * g:LP + 32 * g + 32, NH * HD + NKV * HD:VW]
                    for b in range(4):
                        for h in range(NI):
                            sp.dma_start(wrow[b * 32 + h * 8:b * 32 + h * 8 + 8, g:g + 1],
                                         src[b * 8:b * 8 + 8, h:h + 1],
                                         allow_slow_non_contiguous=True).then_inc(wrow_loaded, 16)
                sp.wait_ge(bias_loaded, 16)

            def prompt():
                sp.dma_start(key_pages, io["key_rows"]).then_inc(rows_loaded, 16)
                sp.dma_start(kv_pages, io["kv_rows"]).then_inc(rows_loaded, 16)

            def sample():
                for b in range(NB):
                    sp.dma_start(tail[b * 8:b * 8 + 8, PAST:KEYS],
                                 csc[:, LP + b * SN:LP + (b + 1) * SN]).then_inc(tail_new, 16)

                def page_numbers(at):
                    return nc.values_load_multi_w_load_instructions(
                        pages[0:1, at:at + 16], engines=(mybir.EngineType.SP,), min_val=0, max_val=NPOOL - 1)[1]

                for f, (src, pr) in enumerate(FILLS):
                    for half in range(2):
                        nos = page_numbers(NB * NPG + 32 * pr + 16 * half)
                        for v in range(4):
                            s = 4 * half + v
                            if f:
                                sp.wait_ge(slot_read, NSLOT * (f - 1) + s + 1)
                            for j in range(4):
                                sp.dma_start(ring[s][:, j * 512:(j + 1) * 512],
                                             io[src][bass.ds(nos[4 * v + j], 1)].rearrange("o p n -> (o p) n")
                                             ).then_inc(ring_loaded[s], 16)
                for b in range(2, NB, 2):
                    if b < 6:
                        sp.wait_ge(slot_read, NSLOT * 7 + 2 * (KV_SLOT[b] - 2) + 2)
                    else:
                        sp.wait_ge(pair_read, 1)
                    s = KV_SLOT[b]
                    for j, no in enumerate(page_numbers(b * NPG)):
                        sp.dma_start(kv_pair[s][:, j, :], io["kv_a"][bass.ds(no, 1)].rearrange("o p n -> (o p) n")
                                     ).then_inc(kv_loaded[b], 16)
                sp.dma_start(xT[:], io["xT"]).then_inc(xT_loaded, 16)

            def merge():
                for m in range(KD):
                    if m >= 2:
                        sp.wait_ge(mix_ready, 4 * (m - 1))
                    sp.dma_start(wmix[m % 2], io["w_mix"][m]).then_inc(mix_loaded[m % 2], 16)
                    if m == 1:
                        sp.dma_start(w_out[:], io["w_out"]).then_inc(wo_loaded, 16)
                        sp.dma_start(lng, io["ln"][0:1, :].partition_broadcast(128)).then_inc(ln_loaded, 16)
                        sp.dma_start(lnb, io["ln"][1:2, :].partition_broadcast(128)).then_inc(ln_loaded, 16)
                for i, (t0, nt) in enumerate(TILES):
                    if i >= 2:
                        sp.wait_ge(res_done, i - 1)
                    sp.dma_start(xrow[i % 2][0:nt, :], io["x"][t0:t0 + nt, :]).then_inc(xr_loaded[i % 2], 16)
                sp.wait_ge(mix_done, KD)
                sp.dma_start(subk[:], io["subk"]).then_inc(subk_loaded, 16)

            def peer():
                sp.dma_start(lng, io["ln"][2:3, :].partition_broadcast(128)).then_inc(ln2_loaded, 16)
                sp.dma_start(lnb, io["ln"][3:4, :].partition_broadcast(128)).then_inc(ln2_loaded, 16)
                for n in range(4 * PH):
                    if n >= 3:
                        sp.wait_ge(qp_ready, n - 2)
                    sp.dma_start(wq[n % 3], io["w_q"][n % (2 * PH)]).then_inc(wq_loaded[n % 3], 16)
                for i, (t0, nt) in enumerate(TILES):
                    sp.wait_ge(ln_done, 5 + i + 1)
                    sp.dma_start(io["y_out"][t0:t0 + nt, :], facc[0:nt, :]).then_inc(y_stored, 16)
                sp.wait_ge(y_stored, 16 * 5)

            project()
            end_phase(sp, 1)
            prompt()
            sp.wait_ge(k_stored, 16 * 3)
            sp.wait_ge(logf_stored, 16)
            sp.wait_ge(wrow_loaded, 16 * 32)
            end_phase(sp, 2)
            sample()
            end_phase(sp, 3)
            merge()
            end_phase(sp, 4)
            peer()

        @block.gpsimd
        def _(pool):
            pool.memset(zeroed, 0.0).then_inc(zero_set, 1)
            pool.wait_ge(zero_set, 1)
            pool.memset(heads[64:65, QB:QB + NH, :], 1.0).then_inc(ones_set, 1)
            end_phase(pool, 1)
            pool.wait_ge(lidx_ready, 1)
            for j in range(NPG):
                pool.indirect_dma_start(out=lp[:, j * 128:(j + 1) * 128], out_offset=None, in_=io["logf_b"],
                                        in_offset=bass.IndirectOffsetOnAxis(ap=lidx[:, j:j + 1], axis=0)
                                        ).then_inc(lp_loaded, 16)
            for c in range(4):
                for p in range(4):
                    for j in range(4):
                        at = p * NPG + 4 * c + j
                        pool.indirect_dma_start(out=kidx[c][:, p * 512 + j * 128:p * 512 + (j + 1) * 128],
                                                out_offset=None, in_=io["kidx"],
                                                in_offset=bass.IndirectOffsetOnAxis(ap=key_rows[:, at:at + 1], axis=0)
                                                ).then_inc(kidx_loaded[c], 16)
            end_phase(pool, 2)
            pool.memset(lf_one, 1.0).then_inc(lf_ones, 1)

            def new_values(q):
                if q >= 2:
                    pool.wait_ge(so_ready, q - 1)
                for e in range(2):
                    t0 = LP + (2 * (q % 4) + e) * SN
                    pool.dma_start(vnew[q % 2][:, e, :], io["v_out"][t0:t0 + SN, :]).then_inc(vnew_loaded[q % 2], 16)

            def batch_pages(b):
                s = KV_SLOT[b]
                for j in range(NPG):
                    at = b * NPG + j
                    pool.indirect_dma_start(out=kv_pair[s][:, j, :], out_offset=None, in_=io["kv_a"].rearrange("o p n -> (o p) n"),
                                            in_offset=bass.IndirectOffsetOnAxis(ap=kv_rows[:, at:at + 1], axis=0)
                                            ).then_inc(kv_loaded[b], 16)

            new_values(0)
            new_values(1)
            pool.wait_ge(ia_ready, 8)
            batch_pages(0)
            batch_pages(1)
            new_values(2)
            new_values(3)
            new_values(4)
            pool.wait_ge(slot_read, NSLOT * 7 + 4)
            batch_pages(3)
            pool.wait_ge(slot_read, NSLOT * 8)
            batch_pages(5)
            new_values(5)
            pool.wait_ge(pair_read, 2)
            batch_pages(7)
            new_values(6)
            new_values(7)
            end_phase(pool, 3)
            end_phase(pool, 4)
            for n, (i, v, k) in enumerate(gathers):
                nt = TILES[i][1]
                if v == 0 and k == 0:
                    pool.wait_ge(ids_ready, i + 1)
                if n >= NR:
                    pool.wait_ge(dve_used if by_dve[n - NR] else pe_used, read_before[n - NR] + 1)
                pool.indirect_dma_start(out=rows[n % NR][0:nt, :], out_offset=None,
                                        in_=io["peer_v"] if v else io["peer_u"],
                                        in_offset=bass.IndirectOffsetOnAxis(ap=ids[i % 2][0:nt, k:k + 1], axis=0)
                                        ).then_inc(row_loaded[n % NR], 16)

        @block.tensor
        def _(pe):
            def project():
                pe.wait_ge(x_loaded, 64)

                def rotate(m):
                    n = 64 * PROJ[m][1]
                    pe.wait_ge(z_copied, m + 1)
                    if m:
                        pe.wait_ge(rope_done, m)
                    for a in range(2):
                        last = pe.matmul(bank(4 + a, HT, 0, n), const("rot")[0:n, 0:n],
                                         zsb[m % 2][0:n, a * HT:(a + 1) * HT], start=True, stop=True)
                    last.then_inc(rot_ready, 1)

                for m in range(NPROJ):
                    n = 64 * PROJ[m][1]
                    pe.wait_ge(w_loaded[m % 3], 16 * (m // 3 + 1))
                    if m >= 2:
                        pe.wait_ge(z_copied, m - 1)
                    for a in range(2):
                        for k in range(KD):
                            last = pe.matmul(bank(2 * (m % 2) + a, HT, 0, n), wring[m % 3][:, k, 0:n],
                                             xT[:, k, a * HT:(a + 1) * HT], start=(k == 0), stop=(k == KD - 1))
                    last.then_inc(z_ready, 1)
                    if m and PROJ[m - 1][2]:
                        rotate(m - 1)
                pe.wait_ge(f_w_loaded, 32)
                for a in range(2):
                    for k in range(KD):
                        last = pe.matmul(bank(6 + a, HT, 0, NH), w_f[:, k, :], xT[:, k, a * HT:(a + 1) * HT],
                                         start=(k == 0), stop=(k == KD - 1))
                last.then_inc(f_ready, 1)
                pe.wait_ge(v_w_loaded, 16)
                for i, (t0, nt) in enumerate(TILES):
                    n = NPROJ + i
                    pe.wait_ge(z_copied, n - 1)
                    for a, (c0, c1) in enumerate(((0, 512), (512, VW))):
                        for k in range(KD):
                            last = pe.matmul(bank(2 * (n % 2) + a, c1 - c0, 0, nt), xT[:, k, t0:t0 + nt],
                                             w_v[:, k, c0:c1], start=(k == 0), stop=(k == KD - 1))
                    last.then_inc(z_ready, 1)

            def prompt():
                def scores(n, q, kt, q0, nq, seen, rows_, bias=None, b0=0):
                    if n >= 2:
                        pe.wait_ge(s_read, n - 1)
                    for c0 in range(0, seen, 512):
                        c1 = min(c0 + 512, seen)
                        out = bank(2 * (n % 2) + c0 // 512, c1 - c0, 0, nq)
                        biased = bias is not None and c1 > b0
                        last = pe.matmul(out, heads[0:rows_, q, q0:q0 + nq], heads[0:rows_, kt, c0:c1],
                                         start=True, stop=not biased)
                        if biased:
                            at = max(b0, c0)
                            last = pe.matmul(out[:, at - c0:], ident_b[0:nq, 0:nq], bias[0:nq, at - b0:c1 - b0],
                                             start=False, stop=True)
                    last.then_inc(s_ready, 1)

                def transpose(u):
                    _, i, h, n = units[u]
                    q0, nq, seen = QTILES[i]
                    pe.wait_ge(diag_ready, u + 1)
                    if u >= 2:
                        pe.wait_ge(pt_copied, u - 1)
                    for j, (k0, nk) in enumerate(blocks(seen)):
                        last = pe.matmul(ps[0:nk, (4 + u % 2) * 512 + j * nq:(4 + u % 2) * 512 + (j + 1) * nq],
                                         prob[u % 3][0:nq, k0:k0 + nk], diag[u % 3][0:nq, 0:nq],
                                         start=True, stop=True)
                    last.then_inc(pt_ready, 1)

                def weigh(u):
                    kind, i, h, n = units[u]
                    q0, nq, seen = QTILES[i]
                    v0 = h * HD if kind == "fox" else NH * HD + (h // 4) * HD
                    pe.wait_ge(pt_copied, u + 1)
                    if u >= 2:
                        pe.wait_ge(o_copied, u - 1)
                    p0, c0 = 64 * (h % 2), 6 * 512 + 128 * (u % 2)
                    bl = blocks(seen)
                    for j, (k0, nk) in enumerate(bl):
                        last = pe.matmul(ps[p0:p0 + 64, c0:c0 + nq], vtm[0:nk, j, v0:v0 + HD],
                                         probT[u % 2][0:nk, j * nq:(j + 1) * nq],
                                         start=(j == 0), stop=(j == len(bl) - 1))
                    last.then_inc(o_ready, 1)

                pe.wait_ge(masks_ready, 1)
                for u in range(NU + 3):
                    if u < NU:
                        kind, i, h, n = units[u]
                        q0, nq, seen = QTILES[i]
                        if kind == "fox":
                            if h == 0 and i:
                                for hi in range(NI):
                                    scores(idx_use[i, hi], QI + hi, KI, q0, nq, seen, 64)
                            scores(n, QB + h, KB + h, q0, nq, seen, 65, causal_b, seen - nq)
                        else:
                            if h == 0 and i:
                                pe.wait_ge(mask_ready, i)
                            scores(n, QA + h, KA + h // 4, q0, nq, seen, 64, maskb if i else causal_b)
                    if 2 <= u < NU + 2:
                        transpose(u - 2)
                    if u >= 3:
                        weigh(u - 3)

            def sample():
                pe.wait_ge(wd_ready, 1)
                for c in range(5):
                    w = 512 if c < 4 else SN
                    if c < 4:
                        pe.wait_ge(kidx_loaded[c], 16 * 16)
                    for g in range(2):
                        n = 2 * c + g
                        if c:
                            pe.wait_ge(relu_done, n - 1)
                        for p in (2 * g, 2 * g + 1):
                            rhs = kidx[c][:, p * 512:(p + 1) * 512] if c < 4 else kin[:, p, :]
                            last = pe.matmul(bank(g, w), qis[:, p, :], rhs, start=(p % 2 == 0), stop=(p % 2 == 1))
                        last.then_inc(ia_ready, 1)
                    pe.wait_ge(relu_done, 2 * c + 2)
                    if c >= 2:
                        pe.wait_ge(ib_copied, c - 1)
                    for g in range(2):
                        last = pe.matmul(bank(2 + c % 2, w, 0, 64), wd[:, g, :], relu_s[g][:, 0:w],
                                         start=(g == 0), stop=(g == 1))
                    last.then_inc(ib_ready, 1)
                pe.wait_ge(ib_copied, 5)

                def unit(src, pr, c, e):
                    u = NSLOT * FILLS.index((src, pr)) + 2 * c + e
                    pe.wait_ge(ring_loaded[u % NSLOT], 16 * 4 * (u // NSLOT + 1))
                    return ring[u % NSLOT]

                def scores(q):
                    fox, pr = q < 4, q % 4
                    if q:
                        pe.wait_ge(sx_done, q)
                    if q == 4:
                        pe.wait_ge(smask_ready, 1)
                    pick, bias = (head_of, tail) if fox else (row_of_b, smask)
                    for c in range(4):
                        out = bank(c)
                        for e in range(2):
                            b = 2 * pr + e
                            if fox:
                                kk = unit("k_b", pr, c, e).rearrange("p (j h n) -> p j h n", j=4, h=4)
                                for hp in range(4):
                                    last = pe.matmul(out, qs[:, b, hp, :], kk[:, :, hp, :],
                                                     start=(e == 0 and hp == 0), stop=False)
                                last.then_inc(slot_read, 1)
                            else:
                                if c == 0:
                                    pe.wait_ge(kv_loaded[b], 16 * NPG)
                                kv = kv_pair[KV_SLOT[b]]
                                pe.matmul(out, qas[:, b, :], kv[:, 4 * c:4 * c + 4, 0:128], start=(e == 0), stop=False)
                        if q == c == 0:
                            pe.wait_ge(tail_ready, 1)
                        pe.matmul(out, pick[:, pr, :], bias[:, c * 512:(c + 1) * 512], start=False, stop=True)
                    out = bank(4, SN)
                    for e in range(2):
                        b = 2 * pr + e
                        if fox:
                            for hp in range(4):
                                pe.matmul(out, qs[:, b, hp, :], kbn[:, hp, b * SN:(b + 1) * SN],
                                          start=(e == 0 and hp == 0), stop=False)
                        else:
                            pe.matmul(out, qas[:, b, :], kan[:, b * SN:(b + 1) * SN], start=(e == 0), stop=False)
                    if fox:
                        pe.matmul(out, ident_b, newc_b, start=False, stop=False)
                    pe.matmul(out, pick[:, pr, :], bias[:, PAST:KEYS], start=False, stop=True).then_inc(ss_ready, 1)

                def transpose(q):
                    pe.wait_ge(sdiag_ready, q + 1)
                    for c in range(5):
                        n = 5 * q + c
                        if n >= 2:
                            pe.wait_ge(st_copied, n - 1)
                        if c < 4:
                            for j in range(4):
                                k0 = c * 512 + j * 128
                                last = pe.matmul(ps[:, (5 + n % 2) * 512 + j * 128:(5 + n % 2) * 512 + (j + 1) * 128],
                                                 prob_s[:, k0:k0 + 128], diag_s, start=True, stop=True)
                        else:
                            last = pe.matmul(bank(5 + n % 2, 128, 0, SN), prob_s[:, PAST:KEYS], diag_s,
                                             start=True, stop=True)
                        last.then_inc(st_ready, 1)

                def weigh(q):
                    fox, pr = q < 4, q % 4
                    for c in range(5):
                        pe.wait_ge(st_copied, 5 * q + c + 1)
                        if c == 0 and q:
                            pe.wait_ge(se_done, q)
                        if c == 4:
                            pe.wait_ge(vnew_loaded[q % 2], 32 * (q // 2 + 1))
                        for e in range(2):
                            b = 2 * pr + e
                            out = bank(7, 512 if fox else 128, 64 * e, 64 * e + 64)
                            if c == 4:
                                last = pe.matmul(out, probTn[0:SN, 64 * e:64 * e + 64],
                                                 vnew[q % 2][:, e, 0:512] if fox else vnew[q % 2][:, e, 512:640],
                                                 start=False, stop=True)
                                continue
                            if fox:
                                vv = unit("v_b", pr, c, e)
                            for j in range(4):
                                rhs = vv[:, j * 512:(j + 1) * 512] if fox else kv_pair[KV_SLOT[b]][:, 4 * c + j, 128:256]
                                last = pe.matmul(out, probT_s[:, c, j * 128 + 64 * e:j * 128 + 64 * e + 64], rhs,
                                                 start=(c == 0 and j == 0), stop=False)
                            if fox:
                                last.then_inc(slot_read, 1)
                            elif c == 3 and e == 1:
                                last.then_inc(pair_read, 1)
                    last.then_inc(so_ready, 1)

                def turn_back(q):
                    pe.wait_ge(so_copied, q + 1)
                    for hp in range(4 if q < 4 else 1):
                        last = pe.transpose(ps[:, 7 * 512 + hp * 128:7 * 512 + (hp + 1) * 128],
                                            osb[:, hp * 128:(hp + 1) * 128], ident)
                    last.then_inc(se_ready, 1)

                scores(0)
                transpose(0)
                for q in range(8):
                    if q < 7:
                        scores(q + 1)
                    weigh(q)
                    if q < 7:
                        transpose(q + 1)
                    turn_back(q)

            def merge():
                pe.wait_ge(xT_loaded, 16)
                for m in range(KD):
                    pe.wait_ge(mix_loaded[m % 2], 16 * (m // 2 + 1))
                    for j, (src, nk, k0) in enumerate(((xT, 8, 0), (xT, 8, 8), (yaT, 4, 16), (ybT, 4, 20))):
                        if m:
                            if j < 2:
                                pe.wait_ge(sig_done, 2 * (m - 1) + j + 1)
                            else:
                                pe.wait_ge(mix_done, m)
                        for a in range(2):
                            for k in range(nk):
                                last = pe.matmul(bank(2 * j + a, HT), wmix[m % 2][:, k0 + k, :],
                                                 src[:, k, a * HT:(a + 1) * HT], start=(k == 0), stop=(k == nk - 1))
                        last.then_inc(mix_ready, 1)
                pe.wait_ge(mix_done, KD)
                pe.wait_ge(wo_loaded, 16)

                def turn(i):
                    t0, nt = TILES[i]
                    pe.wait_ge(ln_done, i + 1)
                    if i:
                        pe.wait_ge(ht_copied, i)
                    for k in range(KD):
                        last = pe.transpose(ps[:, 4 * 512 + k * 128:4 * 512 + k * 128 + nt],
                                            hrow[0:nt, i, k * 128:(k + 1) * 128], ident[0:nt, 0:nt])
                    last.then_inc(ht_ready, 1)

                for i, (t0, nt) in enumerate(TILES):
                    if i >= 2:
                        pe.wait_ge(res_done, i - 1)
                    for a in range(2):
                        for m in range(KD):
                            last = pe.matmul(bank(2 * (i % 2) + a, 512, 0, nt), mergedT[:, m, t0:t0 + nt],
                                             w_out[:, m, a * 512:(a + 1) * 512], start=(m == 0), stop=(m == KD - 1))
                    last.then_inc(h_ready, 1)
                    if i:
                        turn(i - 1)
                turn(4)

            def peer():
                def queries(n):
                    m, t0, t1 = n % (2 * PH), *QSPANS[n // (2 * PH)]
                    w = (t1 - t0) // 2
                    pe.wait_ge(wq_loaded[n % 3], 16 * (n // 3 + 1))
                    if n >= 2:
                        pe.wait_ge(qp_copied, n - 1)
                    for a in range(2):
                        for k in range(KD):
                            last = pe.matmul(bank(QBANKS[n % 2] + a, w), wq[n % 3][:, k, :],
                                             hT[:, k, t0 + a * w:t0 + (a + 1) * w], start=(k == 0), stop=(k == KD - 1))
                    last.then_inc(qp_ready, 1)

                for m in range(2 * PH):
                    queries(m)
                pe.wait_ge(qp_copied, 2 * PH)
                pe.wait_ge(subk_loaded, 16)

                def key_scores(i):
                    t0, nt = TILES[i]
                    if i:
                        pe.wait_ge(sc_copied, i)
                    for m in range(2 * PH):
                        last = pe.matmul(ps[0:nt, m * 128:(m + 1) * 128], qpT[:, m, t0:t0 + nt], subk[:, m, :],
                                         start=True, stop=True)
                    last.then_inc(sc_ready, 1)

                key_scores(0)
                for m in range(2 * PH, 4 * PH):
                    queries(m)
                pe.wait_ge(qp_copied, 4 * PH)
                for i, (t0, nt) in enumerate(TILES):
                    if i < 4:
                        key_scores(i + 1)
                    if i:
                        pe.wait_ge(ln_done, 5 + i)
                    for k in range(NE):
                        n = gather_no(i, 1, k)
                        if by_dve[n]:
                            continue
                        pe.wait_ge(row_loaded[n % NR], 16 * (n // NR + 1))
                        pe.wait_ge(dp_ready, read_before[n] + 1)
                        for a in range(2):
                            last = pe.matmul(bank(4 + a, 512, 0, nt), diag_p[read_before[n] % ND][0:nt, 0:nt],
                                             rows[n % NR][0:nt, a * 512:(a + 1) * 512],
                                             start=(k == 0), stop=(k == NE - 2))
                        last.then_inc(pe_used, 1)

            project()
            end_phase(pe, 1)
            prompt()
            end_phase(pe, 2)
            sample()
            end_phase(pe, 3)
            merge()
            end_phase(pe, 4)
            peer()

        @block.scalar
        def _(act):
            done = [0]

            def step(ins):
                done[0] += 1
                ins.then_inc(act_seq, 1)
                act.wait_ge(act_seq, done[0])

            def project():
                act.dma_start(w_f[:], io["w_f"]).then_inc(f_w_loaded, 16)
                act.dma_start(bf[0:NH, :], io["b_forget"]).then_inc(f_w_loaded, 16)
                act.dma_start(w_v[:], io["w_v"]).then_inc(v_w_loaded, 16)
                for m, (h0, nh, rope, scale) in enumerate(PROJ):
                    n = 64 * nh
                    act.wait_ge(z_ready, m + 1)
                    if rope:
                        if m >= 2:
                            act.wait_ge(rope_done, m - 1)
                        act.activation(split(zsb[m % 2])[0:n], halves(2 * (m % 2), n), ACT.Copy,
                                       scale=scale).then_inc(z_copied, 1)
                    else:
                        z = halves(2 * (m % 2))
                        act.activation(split(heads[0:64, h0, :]), z[0:64], ACT.Copy, scale=scale)
                        act.activation(split(heads[0:64, h0 + 1, :]), z[64:128], ACT.Copy,
                                       scale=scale).then_inc(z_copied, 1)
                act.wait_ge(f_ready, 1)
                act.wait_ge(f_w_loaded, 32)
                step(act.activation(split(f_z), halves(6, NH), ACT.Identity, bias=bf[0:NH, :]))
                step(act.activation(f_tmp, f_z, ACT.Abs))
                step(act.activation(f_tmp, f_tmp, ACT.Exp, scale=-1.0))
                act.activation(f_tmp, f_tmp, ACT.Ln, bias=1.0).then_inc(f_act, 1)
                for i, (t0, nt) in enumerate(TILES):
                    n = NPROJ + i
                    act.wait_ge(z_ready, n + 1)
                    b = 2 * (n % 2)
                    act.activation(vtm[0:nt, i, :], ps[0:nt, b * 512:b * 512 + VW], ACT.Copy).then_inc(z_copied, 1)
                act.wait_ge(zero_set, 1)
                act.wait_ge(z_copied, NPROJ + 5)
                for h in range(NH):
                    for e in range(2):
                        half = h % 2
                        dst = qs.rearrange("p (b e) h c -> p b e h c", e=2)[
                            64 * half:64 * half + 64, :, e, h // 2, e * 64 + h * 8:e * 64 + h * 8 + 8]
                        src = heads[0:64, QB + h, LP:T].rearrange("p (b e t) -> p b e t", e=2, t=SN)[:, :, e, :]
                        last = act.activation(dst, src, ACT.Copy)
                    last = act.activation(kbn[64 * half:64 * half + 64, h // 2, :], heads[0:64, KB + h, LP:T], ACT.Copy)
                last.then_inc(spread_a, 1)

            def prompt():
                def move(u):
                    _, i, h, n = units[u]
                    q0, nq, seen = QTILES[i]
                    act.wait_ge(pt_ready, u + 1)
                    if u >= 2:
                        act.wait_ge(o_ready, u - 1)
                    full, rest = seen // 128, seen % 128
                    c0 = (4 + u % 2) * 512
                    last = act.activation(probT[u % 2][:, 0:full * nq], ps[:, c0:c0 + full * nq], ACT.Copy)
                    if rest:
                        last = act.activation(probT[u % 2][0:rest, full * nq:(full + 1) * nq],
                                              ps[0:rest, c0 + full * nq:c0 + (full + 1) * nq], ACT.Copy)
                    last.then_inc(pt_copied, 1)

                for u in range(NU + 2):
                    if u < NU:
                        kind, i, h, n = units[u]
                        q0, nq, seen = QTILES[i]
                        if kind == "fox" and h == 0 and i:
                            for hi in range(NI):
                                ni, a = idx_use[i, hi], NI * (i - 1) + hi
                                act.wait_ge(s_ready, ni + 1)
                                if a >= 2:
                                    act.wait_ge(idx_added, a - 1)
                                act.activation(relu[a % 2][0:nq, 0:seen],
                                               ps[0:nq, (ni % 2) * 1024:(ni % 2) * 1024 + seen], ACT.Relu
                                               ).then_inc(s_read, 1)
                        act.wait_ge(negmax_ready, u + 1)
                        if u >= 3:
                            act.wait_ge(pt_ready, u - 2)
                        act.activation(prob[u % 3][0:nq, 0:seen], ps[0:nq, (n % 2) * 1024:(n % 2) * 1024 + seen],
                                       ACT.Exp, bias=col(COL_NEGMAX + u % 3, p=nq),
                                       accum_out=col(COL_RSUM + u % 3, p=nq)).then_inc(s_read, 1)
                    if u >= 2:
                        move(u - 2)

            def sample():
                for c in range(5):
                    w = 512 if c < 4 else SN
                    for g in range(2):
                        act.wait_ge(ia_ready, 2 * c + g + 1)
                        if c:
                            act.wait_ge(ib_ready, c)
                        act.activation(relu_s[g][:, 0:w], bank(g, w), ACT.Relu).then_inc(relu_done, 1)

                def exponentials(q):
                    act.wait_ge(smax_ready, q + 1)
                    if q:
                        act.wait_ge(st_ready, 5 * q)
                    act.activation(prob_s, ps[:, 0:KEYS], ACT.Exp, bias=col(COL_SMAX),
                                   accum_out=col(COL_SSUM)).then_inc(sx_done, 1)

                def transposed(q):
                    if q:
                        act.wait_ge(so_ready, q)
                    for c in range(5):
                        n = 5 * q + c
                        act.wait_ge(st_ready, n + 1)
                        dst, src = ((probT_s[:, c, :], bank(5 + n % 2)) if c < 4
                                    else (probTn, bank(5 + n % 2, 128, 0, SN)))
                        act.activation(dst, src, ACT.Copy).then_inc(st_copied, 1)

                act.wait_ge(tail_ready, 1)
                exponentials(0)
                transposed(0)
                for q in range(8):
                    fox, pr = q < 4, q % 4
                    if q < 7:
                        exponentials(q + 1)
                    act.wait_ge(so_ready, q + 1)
                    if q:
                        act.wait_ge(se_ready, q)
                    w = 512 if fox else 128
                    act.activation(osb[:, 0:w], bank(7, w), ACT.Copy).then_inc(so_copied, 1)
                    if q < 7:
                        transposed(q + 1)
                    act.wait_ge(se_ready, q + 1)
                    for h in range(NH):
                        f0 = 64 * (h % 2 if fox else h // 4)
                        c0 = 7 * 512 + (h // 2 * 128 if fox else 0)
                        src = ps[f0:f0 + 64, c0:c0 + 128].rearrange("p (e h t) -> p e h t", e=2, h=NH)[:, :, h, :]
                        dst = (ybT if fox else yaT)[64 * (h % 2):64 * (h % 2) + 64, h // 2,
                                                    LP + pr * 16:LP + pr * 16 + 16]
                        last = act.activation(dst.rearrange("p (e t) -> p e t", e=2), src, ACT.Copy)
                    last.then_inc(se_done, 1)

            def merge():
                for m in range(KD):
                    for j in range(2):
                        act.wait_ge(mix_ready, 4 * m + j + 1)
                        if m:
                            act.wait_ge(mix_done, m)
                        act.activation(split(sig[j]), halves(2 * j), ACT.Sigmoid).then_inc(sig_done, 1)

                def turned(i):
                    t0, nt = TILES[i]
                    act.wait_ge(ht_ready, i + 1)
                    act.activation(hT[:, :, t0:t0 + nt],
                                   ps[:, 4 * 512:6 * 512].rearrange("p (k c) -> p k c", k=KD)[:, :, 0:nt],
                                   ACT.Copy).then_inc(ht_copied, 1)

                for i, (t0, nt) in enumerate(TILES):
                    root(i, nt)
                    if i:
                        turned(i - 1)
                turned(4)

            def root(n, nt):
                act.wait_ge(var_ready, n + 1)
                act.activation(col(COL_STD, p=nt), col(COL_MV + 1, p=nt), ACT.Sqrt,
                               bias=const("eps", nt)).then_inc(std_ready, 1)

            def peer():
                def queries(n):
                    t0, t1 = QSPANS[n // (2 * PH)]
                    w = (t1 - t0) // 2
                    b = QBANKS[n % 2]
                    act.wait_ge(qp_ready, n + 1)
                    act.activation(split(qpT[:, n % (2 * PH), t0:t1]),
                                   ps[:, b * 512:(b + 2) * 512].rearrange("p (a c) -> p a c", a=2)[:, :, 0:w],
                                   ACT.Copy).then_inc(qp_copied, 1)

                for m in range(2 * PH):
                    queries(m)

                def key_scores(i):
                    nt = TILES[i][1]
                    act.wait_ge(sc_ready, i + 1)
                    if i:
                        act.wait_ge(ids_ready, i)
                    act.activation(sc[0:nt].rearrange("p a b -> p (a b)"), ps[0:nt, 0:2048], ACT.Copy
                                   ).then_inc(sc_copied, 1)

                def gate_exp(i):
                    nt = TILES[i][1]
                    act.wait_ge(gexp_in, i + 1)
                    act.activation(gexp[0:nt], gate[0:nt], ACT.Exp).then_inc(gexp_out, 1)

                key_scores(0)
                gate_exp(0)
                for i, (t0, nt) in enumerate(TILES):
                    for g in range(4):
                        for m in range(4 * g, 4 * g + 4) if i == 0 else ():
                            queries(2 * PH + m)
                        act.wait_ge(dve_used, read_before[gather_no(i, 0, 32 * g + 31)] + 1)
                        if i or g:
                            act.wait_ge(coef_ready, 4 * i + g)
                        act.activation(gl[0:nt, 32 * g:32 * g + 32], pre[0:nt, 32 * g:32 * g + 32], ACT.Gelu
                                       ).then_inc(gelu_done, 1)
                    if i < 4:
                        key_scores(i + 1)
                    for k in range(NE):
                        n = gather_no(i, 1, k)
                        if by_dve[n]:
                            continue
                        r_ = read_before[n]
                        act.wait_ge(coef_ready, 4 * i + k // 32 + 1)
                        if r_ >= ND:
                            act.wait_ge(pe_used, r_ - ND + 1)
                        act.activation(diag_p[r_ % ND][0:nt, 0:nt], ident[0:nt, 0:nt], ACT.Copy,
                                       scale=coef[i % 2][0:nt, k:k + 1]).then_inc(dp_ready, 1)
                        if i < 4 and k == GATE_AT:
                            gate_exp(i + 1)
                    root(5 + i, nt)

            project()
            end_phase(act, 1)
            prompt()
            end_phase(act, 2)
            sample()
            end_phase(act, 3)
            merge()
            end_phase(act, 4)
            peer()

        @block.vector
        def _(dve):
            done = [0]

            def step(ins):
                done[0] += 1
                ins.then_inc(dve_seq, 1)
                dve.wait_ge(dve_seq, done[0])

            def project():
                dve.wait_ge(x_loaded, 64)
                for m in ROPES:
                    h0, nh, _, _ = PROJ[m]
                    n = 64 * nh
                    dve.wait_ge(rot_ready, m + 1)
                    step(dve.tensor_tensor(split(rot_s)[0:n], halves(4, n), split(const("sin", n)), ALU.mult))
                    step(dve.tensor_tensor(zsb[m % 2][0:n], zsb[m % 2][0:n], const("cos", n), ALU.mult))
                    for j in range(nh):
                        p0 = 64 * j
                        last = dve.tensor_tensor(heads[0:64, h0 + j, :], zsb[m % 2][p0:p0 + 64], rot_s[p0:p0 + 64],
                                                 ALU.add)
                    last.then_inc(rope_done, 1)
                    dve.wait_ge(rope_done, m + 1)
                dve.wait_ge(f_act, 1)
                step(dve.scalar_tensor_tensor(f_log, f_z, 0.0, f_tmp, ALU.min, ALU.subtract))
                step(dve.tensor_tensor_scan(f_sum, const("restart", NH), f_log, 0.0, ALU.mult, ALU.add))
                dve.tensor_scalar(f_z, f_sum, -1.0, None, ALU.mult).then_inc(logf_ready, 1)
                dve.wait_ge(zero_set, 1)
                for h in range(NH):
                    for e in range(2):
                        g = h // 4
                        dst = qas.rearrange("p (b e) c -> p b e c", e=2)[
                            64 * g:64 * g + 64, :, e, e * 64 + h * 8:e * 64 + h * 8 + 8]
                        src = heads[0:64, QA + h, LP:T].rearrange("p (b e t) -> p b e t", e=2, t=SN)[:, :, e, :]
                        dve.tensor_copy(dst, src)
                for h in range(NI):
                    for e in range(2):
                        for pp in range(2):
                            c0 = (2 * pp + e) * 32 + h * 8
                            dst = qis.rearrange("p (a b) c -> p a b c", b=2)[64 * e:64 * e + 64, :, pp, c0:c0 + 8]
                            src = heads[0:64, QI + h, LP:T].rearrange(
                                "p (a b e t) -> p a b e t", b=2, e=2, t=SN)[:, :, pp, e, :]
                            dve.tensor_copy(dst, src)
                for g in range(NKV):
                    dve.tensor_copy(kan[64 * g:64 * g + 64, :], heads[0:64, KA + g, LP:T])
                for e in range(2):
                    last = dve.tensor_copy(
                        kin[64 * e:64 * e + 64, :, :],
                        heads[0:64, KI, LP:T].rearrange("p (a e t) -> p a e t", e=2, t=SN)[:, :, e, :])
                last.then_inc(spread_d, 1)

            def take8(v, top8):
                step(dve.max(top8, v))
                step(dve.match_replace(v, top8, v, TAKEN))

            def prompt():
                dve.tensor_copy(ident_b, ident)
                dve.tensor_copy(newc_b, const("new_causal"))
                dve.tensor_copy(row_of_b, row_of)
                dve.tensor_copy(causal_b, causal).then_inc(masks_ready, 1)
                dve.tensor_scalar(lidx, page_rows, 8.0, const("head_no", 64), ALU.mult, ALU.add)
                dve.wait_ge(rows_loaded, 32)
                dve.tensor_scalar(key_rows, key_pages, 64.0, const("key_row"), ALU.mult, ALU.add)
                dve.tensor_scalar(kv_rows, kv_pages, 128.0, const("part"), ALU.mult, ALU.add
                                  ).then_inc(lidx_ready, 1)
                for i in range(1, 5):
                    nt = QTILES[i][1]
                    step(dve.tensor_scalar(vtm[0:nt, i, 640:VW], vtm[0:nt, i, 640:VW], IDX_SCALE, None, ALU.mult))

                def weights(u):
                    _, i, h, n = units[u]
                    q0, nq, seen = QTILES[i]
                    dve.wait_ge(s_read, n + 1)
                    step(dve.reciprocal(col(COL_RINV + u % 3, p=nq), col(COL_RSUM + u % 3, p=nq)))
                    if u >= 3:
                        dve.wait_ge(pt_ready, u - 2)
                    dve.tensor_scalar(diag[u % 3][0:nq, 0:nq], ident[0:nq, 0:nq], col(COL_RINV + u % 3, p=nq),
                                      None, ALU.mult).then_inc(diag_ready, 1)

                def result(u):
                    kind, i, h, n = units[u]
                    q0, nq, seen = QTILES[i]
                    dve.wait_ge(o_ready, u + 1)
                    p0, c0 = 64 * (h % 2), 6 * 512 + 128 * (u % 2)
                    y = ybT if kind == "fox" else yaT
                    dve.tensor_copy(y[p0:p0 + 64, h // 2, q0:q0 + nq], ps[p0:p0 + 64, c0:c0 + nq]
                                    ).then_inc(o_copied, 1)

                for u in range(NU + 4):
                    if u < NU:
                        kind, i, h, n = units[u]
                        q0, nq, seen = QTILES[i]
                        v = isc[0:nq, 0:seen]
                        if kind == "fox" and h == 0 and i:
                            for hi in range(NI):
                                a = NI * (i - 1) + hi
                                w = vtm[0:nq, i, 640 + hi:641 + hi]
                                dve.wait_ge(s_read, idx_use[i, hi] + 1)
                                rl = relu[a % 2][0:nq, 0:seen]
                                if hi == 0:
                                    dve.tensor_scalar(v, rl, w, None, ALU.mult).then_inc(idx_added, 1)
                                else:
                                    dve.scalar_tensor_tensor(v, rl, w, v, ALU.mult, ALU.add).then_inc(idx_added, 1)
                                dve.wait_ge(idx_added, a + 1)
                            own = isc[0:nq, seen - nq:seen]
                            step(dve.tensor_tensor(own, own, causal[0:nq, 0:nq], ALU.add))
                        dve.wait_ge(s_ready, n + 1)
                        if u >= 3:
                            dve.wait_ge(s_read, units[u - 3][3] + 1)
                        dve.tensor_reduce(col(COL_NEGMAX + u % 3, p=nq),
                                          ps[0:nq, (n % 2) * 1024:(n % 2) * 1024 + seen], AX_X, ALU.max,
                                          negate=True).then_inc(negmax_ready, 1)
                    if 1 <= u <= NU:
                        weights(u - 1)
                    if u >= 4:
                        result(u - 4)
                    if u < NU and kind == "fox" and i:
                        for _r in range(ROUNDS_P // NH):
                            take8(v, col(COL_TOP8, 8, nq))
                        if h == NH - 1:
                            if i > 1:
                                dve.wait_ge(s_ready, units[u - NH][3] + 1)
                            dve.tensor_scalar(maskb[0:nq, 0:seen], v, TAKEN, NEG, ALU.not_equal, ALU.mult
                                              ).then_inc(mask_ready, 1)

            def sample():
                dve.wait_ge(wrow_loaded, 16 * 32)
                step(dve.tensor_scalar(wd[:, 0, :], w_place[:, 0, :], wrow[:, 0:1], IDX_SCALE, ALU.mult, ALU.mult))
                dve.tensor_scalar(wd[:, 1, :], w_place[:, 1, :], wrow[:, 1:2], IDX_SCALE, ALU.mult, ALU.mult
                                  ).then_inc(wd_ready, 1)
                step(dve.memset(tail[:, 0:1], 0.0))
                dve.wait_ge(lp_loaded, 16 * NPG)
                dve.wait_ge(lf_ones, 1)
                dve.wait_ge(tail_new, 16 * NB)
                dve.tensor_tensor_scan(tail[:, 1:PAST], lf_one[:, 1:PAST], lp[:, 0:PAST - 1], 0.0,
                                       ALU.mult, ALU.add).then_inc(tail_ready, 1)
                for c in range(5):
                    w = 512 if c < 4 else SN
                    dve.wait_ge(ib_ready, c + 1)
                    dve.tensor_copy(isamp[:, c * 512:c * 512 + w], bank(2 + c % 2, w, 0, 64)).then_inc(ib_copied, 1)
                dve.wait_ge(ib_copied, 5)
                step(dve.tensor_tensor(isamp[:, PAST:KEYS], isamp[:, PAST:KEYS], const("idx_causal", 64), ALU.add))
                left = ROUNDS_S
                for q in range(8):
                    dve.wait_ge(ss_ready, q + 1)
                    if q:
                        dve.wait_ge(sx_done, q)
                    dve.tensor_reduce(col(COL_SMAX), ps[:, 0:KEYS], AX_X, ALU.max, negate=True
                                      ).then_inc(smax_ready, 1)
                    dve.wait_ge(sx_done, q + 1)
                    step(dve.reciprocal(col(COL_SINV), col(COL_SSUM)))
                    if q:
                        dve.wait_ge(st_ready, 5 * q)
                    dve.tensor_scalar(diag_s, ident, col(COL_SINV), None, ALU.mult).then_inc(sdiag_ready, 1)
                    now = min(left, -(-ROUNDS_S // 3))
                    for _r in range(now):
                        take8(isamp, col(COL_TOPS, 8, 64))
                    left -= now
                    if now and left == 0:
                        dve.tensor_scalar(smask, isamp, TAKEN, NEG, ALU.not_equal, ALU.mult
                                          ).then_inc(smask_ready, 1)

            def normalise(n, v, y, nt):
                for a in range(2):
                    step(dve.bn_stats(col(COL_BN + 6 * a, 6, nt), v[:, a * 512:(a + 1) * 512]))
                dve.bn_aggr(col(COL_MV, 2, nt), col(COL_BN, 12, nt)).then_inc(var_ready, 1)
                dve.wait_ge(std_ready, n + 1)
                step(dve.reciprocal(col(COL_RSTD, p=nt), col(COL_STD, p=nt)))
                step(dve.tensor_scalar(v, v, col(COL_MV, p=nt), col(COL_RSTD, p=nt), ALU.subtract, ALU.mult))
                step(dve.tensor_tensor(v, v, lng[0:nt], ALU.mult))
                dve.tensor_tensor(y, v, lnb[0:nt], ALU.add).then_inc(ln_done, 1)

            def merge():
                for m in range(KD):
                    for j in range(2):
                        dve.wait_ge(sig_done, 2 * m + j + 1)
                        dve.wait_ge(mix_ready, 4 * m + 2 + j + 1)
                        step(dve.tensor_tensor(split(sig[j]), split(sig[j]), halves(4 + 2 * j), ALU.mult))
                    dve.tensor_tensor(mergedT[:, m, :], sig[0], sig[1], ALU.add).then_inc(mix_done, 1)
                for i, (t0, nt) in enumerate(TILES):
                    v = hrow[0:nt, i, :]
                    dve.wait_ge(h_ready, i + 1)
                    dve.wait_ge(xr_loaded[i % 2], 16 * (i // 2 + 1))
                    b = 2 * (i % 2)
                    dve.scalar_tensor_tensor(v, xrow[i % 2][0:nt], ALPHA, ps[0:nt, b * 512:b * 512 + D],
                                             ALU.mult, ALU.add).then_inc(res_done, 1)
                    dve.wait_ge(res_done, i + 1)
                    if i == 0:
                        dve.wait_ge(ln_loaded, 32)
                    normalise(i, v, v, nt)

            def top16(v, vals, places):
                step(dve.max(vals[:, 0:8], v))
                step(dve.max_index(places[:, 0:8], vals[:, 0:8], v))
                step(dve.match_replace(v, vals[:, 0:8], v, TAKEN))
                step(dve.max(vals[:, 8:16], v))
                step(dve.max_index(places[:, 8:16], vals[:, 8:16], v))

            def route(i, s):
                nt = TILES[i][1]
                if s == 0:
                    dve.wait_ge(sc_copied, i + 1)
                if s < 16:
                    top16(sc[0:nt, s, :], sv[0:nt, s, :], si[0:nt, s, :])
                    return
                h = s - 16
                sv4 = sv.rearrange("p (h c) a -> p h c a", c=2)
                siF4 = siF.rearrange("p (h c) a -> p h c a", c=2)
                if h < PH:
                    cd = cand[0:nt, h, :]
                    step(dve.tensor_tensor(cd.rearrange("p (a b) -> p a b", a=PK),
                                           sv4[0:nt, h, 0, :, None].to_broadcast([nt, PK, PK]),
                                           sv4[0:nt, h, 1, None, :].to_broadcast([nt, PK, PK]), ALU.add))
                    top16(cd, top[0:nt, h, :], tj[0:nt, h, :])
                elif s == 24:
                    dve.tensor_tensor(gate[0:nt], top[0:nt], top[0:nt, :, 0:1].to_broadcast([nt, PH, PK]),
                                      ALU.subtract).then_inc(gexp_in, 1)
                    step(dve.tensor_copy(siF[0:nt], si[0:nt]))
                    step(dve.tensor_scalar(jbits[0:nt], tj[0:nt], 4, None, ALU.logical_shift_right))
                    step(dve.tensor_copy(ja[0:nt], jbits[0:nt]))
                elif s == 25:
                    step(dve.tensor_scalar(jbits[0:nt], tj[0:nt], 15, None, ALU.bitwise_and))
                    step(dve.tensor_copy(jb[0:nt], jbits[0:nt]))
                elif s in (26, 27, 28, 29):
                    c, first = divmod(s - 26, 2)
                    jx, ex = ((ja, e0), (jb, e1))[c]
                    o4 = oh[0:nt].rearrange("p (h k) a -> p h k a", h=PH)
                    if first == 0:
                        step(dve.tensor_tensor(
                            oh[0:nt], jx[0:nt].rearrange("p h k -> p (h k)")[:, :, None].to_broadcast([nt, NE, PK]),
                            const("iota16", nt)[:, None, :].to_broadcast([nt, NE, PK]), ALU.is_equal))
                    else:
                        step(dve.tensor_tensor(o4, o4, siF4[0:nt, :, c, None, :].to_broadcast([nt, PH, PK, PK]),
                                               ALU.mult))
                        step(dve.tensor_reduce(ex[0:nt].rearrange("p h k -> p (h k)"), oh[0:nt], AX_X, ALU.add))
                elif s == 30:
                    dve.scalar_tensor_tensor(ids[i % 2][0:nt], e0[0:nt].rearrange("p h k -> p (h k)"), 128.0,
                                             e1[0:nt].rearrange("p h k -> p (h k)"), ALU.mult, ALU.add
                                             ).then_inc(ids_ready, 1)
                elif s == 31:
                    dve.wait_ge(gexp_out, i + 1)
                    step(dve.tensor_reduce(col(COL_GSUM, PH, nt), gexp[0:nt], AX_X, ALU.add))
                    step(dve.reciprocal(col(COL_GINV, PH, nt), col(COL_GSUM, PH, nt)))
                    step(dve.tensor_tensor(gate[0:nt], gexp[0:nt],
                                           col(COL_GINV, PH, nt)[:, :, None].to_broadcast([nt, PH, PK]), ALU.mult))

            def peer():
                for s in range(32):
                    route(0, s)
                for i, (t0, nt) in enumerate(TILES):
                    h = hrow[0:nt, i, :]

                    def coefs(g):
                        dve.wait_ge(gelu_done, 4 * i + g + 1)
                        gf = gate[0:nt].rearrange("p h k -> p (h k)")
                        dve.tensor_tensor(coef[i % 2][0:nt, 32 * g:32 * g + 32], gf[:, 32 * g:32 * g + 32],
                                          gl[0:nt, 32 * g:32 * g + 32], ALU.mult).then_inc(coef_ready, 1)

                    for k in range(NE):
                        n = gather_no(i, 0, k)
                        dve.wait_ge(row_loaded[n % NR], 16 * (n // NR + 1))
                        dve.tensor_tensor_reduce(out=rows[n % NR][0:nt], in0=rows[n % NR][0:nt], in1=h, scale=1.0,
                                                 scalar=0.0, op0=ALU.mult, op1=ALU.add,
                                                 accum_out=pre[0:nt, k:k + 1]).then_inc(dve_used, 1)
                        if k >= 32 and k % 32 == 4:
                            coefs(k // 32 - 1)
                    coefs(3)
                    dve.wait_ge(coef_ready, 4 * i + 4)
                    if i:
                        dve.wait_ge(y_stored, 16 * i)
                    mine = [k for k in range(NE) if by_dve[gather_no(i, 1, k)]]
                    for j, k in enumerate(mine):
                        n = gather_no(i, 1, k)
                        dve.wait_ge(row_loaded[n % NR], 16 * (n // NR + 1))
                        c = coef[i % 2][0:nt, k:k + 1]
                        if j == 0:
                            ins = dve.tensor_scalar(facc[0:nt], rows[n % NR][0:nt], c, None, ALU.mult)
                        else:
                            ins = dve.scalar_tensor_tensor(facc[0:nt], rows[n % NR][0:nt], c, facc[0:nt],
                                                           ALU.mult, ALU.add)
                        ins.then_inc(dve_used, 1)
                        dve.wait_ge(dve_used, read_before[n] + 1)
                        if i < 4 and j < 32:
                            route(i + 1, j)
                    dve.wait_ge(pe_used, read_before[gather_no(i, 1, NE - 2)] + 1)
                    step(dve.tensor_tensor(facc[0:nt], facc[0:nt], ps[0:nt, 4 * 512:4 * 512 + D], ALU.add))
                    step(dve.scalar_tensor_tensor(facc[0:nt], h, ALPHA, facc[0:nt], ALU.mult, ALU.add))
                    if i == 0:
                        dve.wait_ge(ln2_loaded, 32)
                    normalise(5 + i, facc[0:nt], facc[0:nt], nt)

            project()
            end_phase(dve, 1)
            prompt()
            end_phase(dve, 2)
            sample()
            end_phase(dve, 3)
            merge()
            end_phase(dve, 4)
            peer()


_OUTS = {"y_out": (T, D), "k_out": (HD, 11, T), "v_out": (T, VW), "logf_out": (NH, T)}


def lay_out(i):
    c = np.ascontiguousarray
    x = np.concatenate([i["meta_tokens"], i["x_prompt"][0], i["x_sample"].reshape(NS, D)], axis=0)
    w = i["w_in"][0]
    cuts = np.cumsum([0, 512, 128, 128, 256, 64, 4, 512, 512, 512, 8, D, D])
    wqa, wka, wva, wqi, wki, wwi, wqb, wkb, wvb, wf, wga, wgb = (w[:, a:b] for a, b in zip(cuts[:-1], cuts[1:]))

    def chunks(a):
        return a.reshape(-1, 128, a.shape[1]).transpose(1, 0, 2)

    def column_tiles(a):
        return chunks(a).reshape(128, a.shape[0] // 128, -1, 128).transpose(2, 0, 1, 3)

    pad = np.zeros((D, 64), np.float32)
    mix = np.concatenate([column_tiles(a) for a in (wga, wgb, i["w_branch_a"][0], i["w_branch_b"][0])], axis=2)
    table = i["page_table"]
    back = table[:, ::-1]
    kb = i["cache_k_b"][0, :, ::-1].transpose(0, 2, 3, 1)
    ka = i["cache_k_a"][0].transpose(0, 2, 3, 1).reshape(NPOOL, 128, PAGE)
    out = {
        "cst": tables(),
        "xT": chunks(x.T),
        "x": x,
        "w_proj": column_tiles(np.concatenate([wqa, wka, wqi, wki, pad, wqb, wkb], axis=1)),
        "w_v": chunks(np.concatenate([wvb, wva, wwi], axis=1)),
        "w_f": chunks(wf),
        "b_forget": i["b_forget"].reshape(NH, 1),
        "pages": np.concatenate([table.reshape(1, -1),
                                 back.reshape(4, 2, 4, 4).transpose(0, 2, 1, 3).reshape(1, -1)], axis=1),
        "key_rows": np.repeat(table.reshape(4, 2, NPG).transpose(1, 0, 2).reshape(2, -1), 64, axis=0),
        "kv_rows": np.repeat(table.reshape(1, -1), 128, axis=0),
        "page_rows": np.repeat(back, NH, axis=0),
        "kidx": i["cache_k_idx"][0].transpose(0, 2, 1).reshape(NPOOL * 64, PAGE),
        "k_b": kb.reshape(NPOOL, 4, 128, PAGE).transpose(0, 2, 1, 3).reshape(NPOOL, 128, 512),
        "v_b": i["cache_v_b"][0, :, ::-1].reshape(NPOOL, PAGE, 512),
        "kv_a": np.concatenate([ka, i["cache_v_a"][0].reshape(NPOOL, PAGE, 128)], axis=2),
        "logf_b": i["cache_logf_b"][0, :, ::-1].transpose(0, 2, 1).reshape(NPOOL * NH, PAGE),
        "w_mix": mix,
        "w_out": chunks(i["w_out"][0]),
        "ln": np.concatenate([i["ln1_g"], i["ln1_b"], i["ln2_g"], i["ln2_b"]], axis=0),
        "w_q": column_tiles(i["peer_w_q"][0]),
        "subk": i["peer_sub_keys"][0].transpose(3, 1, 0, 2).reshape(128, 2 * PH, 128),
        "peer_u": i["peer_u"][0],
        "peer_v": i["peer_v"][0],
    }
    return {k: c(v) for k, v in out.items()}


def give_back(r):
    y, k, v, f = r["y_out"], r["k_out"].transpose(2, 1, 0), r["v_out"], r["logf_out"].T
    rows_ = {"k_a": k[:, 0:2], "v_a": v[:, 512:640].reshape(T, NKV, HD), "k_i": k[:, 2], "k_b": k[:, 3:11],
             "v_b": v[:, 0:512].reshape(T, NH, HD), "f": f}
    prompt = [a[None, None, 0:LP] for a in rows_.values()]
    sample = [a[LP:T].reshape((1, NB, SN) + a.shape[1:]) for a in rows_.values()]
    return (y[None, N_META:LP], y[LP:T].reshape(NB, SN, D), *prompt, *sample)


def kernel(**inputs):
    import concourse.bacc as _bacc
    from concourse.bass_utils import run_bass_kernel_spmd as _run

    arrays = lay_out({k: np.asarray(v) for k, v in inputs.items()})
    nc = _bacc.Bacc("TRN2", target_bir_lowering=False, num_devices=1)
    io = {n: nc.dram_tensor(n, a.shape, mybir.dt.from_np(a.dtype), kind="ExternalInput").ap()
          for n, a in arrays.items()}
    for n, shape in _OUTS.items():
        io[n] = nc.dram_tensor(n, shape, F32, kind="ExternalOutput").ap()
    program(nc, io)
    got = _run(nc, [arrays], core_ids=[0]).results[0]
    return tuple(np.ascontiguousarray(a) for a in give_back(got))
```

```python
from contextlib import ExitStack

import numpy as np

import concourse.bass as bass
from concourse import mybir

ALU = mybir.AluOpType
ACT = mybir.ActivationFunctionType
F32 = mybir.dt.float32
U32 = mybir.dt.uint32
I32 = mybir.dt.int32
BF16 = mybir.dt.bfloat16
AX_X = mybir.AxisListType.X

D = 1024
KD = D // 128
N_META, SEQ = 16, 512
LP = N_META + SEQ
NB, SN = 8, 8
NS = NB * SN
T = LP + NS
HT = T // 2
HD = 64
NH = 8
NKV = 2
NI = 4
PAGE, NPG = 128, 16
PAST = PAGE * NPG
NPOOL = NB * NPG * 5 // 4
KEYS = PAST + SN
ATTN_SCALE = HD ** -0.5
IDX_SCALE = (64 * NI) ** -0.5
SEL_P = 128
SEL_S = 256
NEG = -1e30
TAKEN = -3e38
ALPHA = 2.0 ** 0.25
EPS = 1e-5
VW = NH * HD + NKV * HD + NI
PH, PK = 8, 16
NE = PH * PK
TILES = [(128 * i, min(128, T - 128 * i)) for i in range(5)]
QTILES = [(128 * i, min(128, LP - 128 * i), min(128 * (i + 1), LP)) for i in range(5)]

QB, KB, QA, KA, QI, KI = 0, 8, 16, 24, 26, 30
NHEADS = 31
PROJ = ([(QA + 2 * j, 2, True, ATTN_SCALE) for j in range(4)] + [(KA, 2, True, 1.0)]
        + [(QI + 2 * j, 2, True, 1.0) for j in range(2)] + [(KI, 1, True, 1.0)]
        + [(QB + 2 * j, 2, False, ATTN_SCALE) for j in range(4)]
        + [(KB + 2 * j, 2, False, 1.0) for j in range(4)])
NPROJ = len(PROJ)
ROPES = [m for m, p in enumerate(PROJ) if p[2]]

CONSTS = [("ident", 128), ("iota16", 16), ("eps", 1), ("causal", 128), ("rot", 128), ("row_of", 512),
          ("head_of", 512), ("new_causal", 8), ("idx_causal", 8), ("w_place", 128), ("head_no", 1),
          ("key_row", 1), ("part", 1), ("cos", T), ("sin", T), ("restart", T)]
CAT, _o = {}, 0
for _n, _w in CONSTS:
    CAT[_n] = (_o, _w)
    _o += _w
NCONST = _o
GATE_AT = 70


ROUTE_MIX = (18, 29)
DOT_MIX = (9, 22, 35, 48, 61, 74)
DOT_NORM = (88, 98, 108, 118)
V0_DVE = 72
ROUTE_1 = [20 + 4 * s for s in range(12)] + [66 + 5 * s // 3 for s in range(20)]
GATE_0, GATE_3 = 102, 8
V3_ALONE = 24
GELU_AT = 2


def tables():
    c = np.zeros((128, NCONST), np.float32)

    def put(name, a):
        o, w = CAT[name]
        c[:a.shape[0], o:o + w] = a.reshape(a.shape[0], w)

    p = np.arange(128)
    put("ident", np.eye(128, dtype=np.float32))
    put("causal", np.where(p[None, :] > p[:, None], np.float32(NEG), np.float32(0)))
    rot = np.zeros((128, 128), np.float32)
    for base in (0, 64):
        for j in range(8):
            rot[base + j + 8, base + j] = -1.0
            rot[base + j, base + j + 8] = 1.0
    put("rot", rot)
    row_of = np.zeros((64, 4, 128), np.float32)
    head_of = np.zeros((64, 4, 128), np.float32)
    for pr in range(4):
        for e in range(2):
            for h in range(NH):
                for t in range(SN):
                    col = e * 64 + h * 8 + t
                    row_of[(2 * pr + e) * 8 + t, pr, col] = 1.0
                    head_of[(2 * pr + e) * 8 + h, pr, col] = 1.0
    put("row_of", row_of)
    put("head_of", head_of)
    t = p % 8
    s = np.arange(8)
    put("new_causal", np.where(s[None, :] > t[:, None], np.float32(NEG), np.float32(0)))
    put("idx_causal", np.where(s[None, :] > t[:64, None], np.float32(NEG), np.float32(0)))
    wp = np.zeros((128, 2, 64), np.float32)
    for g in range(2):
        for b in range(4):
            for h in range(NI):
                for tt in range(SN):
                    wp[b * 32 + h * 8 + tt, g, (g * 4 + b) * 8 + tt] = 1.0
    put("w_place", wp)
    put("iota16", np.tile(np.arange(16, dtype=np.float32), (128, 1)))
    put("head_no", (p % 8).astype(np.float32)[:, None])
    put("key_row", (p % 64).astype(np.float32)[:, None])
    put("part", p.astype(np.float32)[:, None])
    put("eps", np.full((128, 1), EPS, np.float32))
    pos = np.concatenate([np.arange(LP), np.tile(PAST + np.arange(SN), NB)]).astype(np.float32)
    inv = np.power(np.float32(500000.0), -np.arange(8, dtype=np.float32) / np.float32(8))
    ang = (pos[None, :] * inv[:, None]).astype(np.float32).astype(np.float64)
    cos, sin = np.ones((128, T), np.float32), np.zeros((128, T), np.float32)
    for base in (0, 64):
        for half in (0, 8):
            cos[base + half:base + half + 8] = np.cos(ang)
            sin[base + half:base + half + 8] = np.sin(ang)
    put("cos", cos)
    put("sin", sin)
    restart = np.ones((8, T), np.float32)
    restart[:, 0] = 0.0
    restart[:, LP::SN] = 0.0
    put("restart", restart)
    return c


def program(nc, io):
    ctx = ExitStack()
    with ctx:
        arena = ctx.enter_context(nc.sbuf_tensor("arena", [128, 53100], F32))
        ps = ctx.enter_context(nc.psum_tensor("ps", [128, 8 * 512], F32))

        def sem(name):
            return ctx.enter_context(nc.semaphore(name))

        def sems(name, n):
            return [sem(f"{name}{i}") for i in range(n)]

        class Region:

            def __init__(self, at):
                self.at = at

            def take(self, *shape, p=128):
                n = int(np.prod(shape))
                v = arena[0:p, self.at:self.at + n]
                self.at += n
                assert self.at <= 53100, self.at
                if len(shape) == 2:
                    v = v.rearrange("p (a b) -> p a b", a=shape[0])
                elif len(shape) == 3:
                    v = v.rearrange("p (a b c) -> p a b c", a=shape[0], b=shape[1])
                return v

        def bank(b, w=512, p0=0, p1=128):
            return ps[p0:p1, b * 512:b * 512 + w]

        base = Region(0)
        consts = base.take(NCONST)

        def const(name, p=128):
            o, w = CAT[name]
            return consts[0:p, o:o + w]

        ident, causal = const("ident"), const("causal")
        row_of = const("row_of", 64).rearrange("p (a b) -> p a b", a=4)
        head_of = const("head_of", 64).rearrange("p (a b) -> p a b", a=4)
        w_place = const("w_place").rearrange("p (a b) -> p a b", a=2)
        small = base.take(128)
        ident_b, causal_b = base.take(64).bitcast(BF16), base.take(64).bitcast(BF16)
        newc_b = base.take(4).bitcast(BF16)
        row_of_b = base.take(256, p=64).bitcast(BF16).rearrange("p (a b) -> p a b", a=4)
        xT_at = base.at
        xT = base.take(KD, T)
        yaT, ybT = base.take(4, T), base.take(4, T)
        vtm_at = base.at
        vtm = base.take(5, VW)
        qs_at = base.at
        qs = base.take(NB, 4, 128)
        qas = base.take(NB, 128)
        qis = base.take(4, 128)
        zeroed = arena[:, qs_at:base.at]
        kbn, kan, kin = base.take(4, NS), base.take(NS), base.take(4, SN)
        wd = base.take(2, 64)
        wrow = base.take(2)
        pages = base.take(2 * NB * NPG, p=1).bitcast(I32)
        page_rows = base.take(NPG, p=64).bitcast(I32)
        lidx = base.take(NPG, p=64).bitcast(U32)
        after_base = base.at

        r = Region(after_base)
        heads = r.take(NHEADS, T)
        work_at = r.at
        wring = [r.take(KD, 128) for _ in range(3)]
        w_v = r.take(KD, VW)
        zsb = [r.take(T) for _ in range(2)]
        rot_s = r.take(T)
        w_f = r.take(KD, NH)
        bf = r.take(1)
        f_z, f_tmp, f_log, f_sum = (yaT[0:NH, j, :] for j in range(4))
        r = Region(work_at)
        prob = [r.take(640) for _ in range(3)]
        probT = [r.take(512) for _ in range(2)]
        diag = [r.take(128) for _ in range(3)]
        isc = r.take(640)
        relu = [r.take(640) for _ in range(2)]
        maskb = r.take(320).bitcast(BF16)
        log_at = r.at
        lp = Region(log_at).take(PAST, p=64)
        kidx_at = [xT_at, xT_at + 2048, log_at + PAST, log_at + PAST + 2048]
        kidx = [Region(a).take(2048) for a in kidx_at]
        r = Region(CAT["cos"][0])
        key_pages, kv_pages = r.take(4 * NPG).bitcast(I32), r.take(NB * NPG).bitcast(I32)
        key_rows, kv_rows = key_pages.bitcast(U32), kv_pages.bitcast(U32)
        smask = r.take(KEYS // 2, p=64).bitcast(BF16)
        relu_s = [r.take(512), Region(xT_at + 4096).take(512)]
        assert r.at <= NCONST
        r = Region(vtm_at)
        vnew = [r.take(2, VW, p=8) for _ in range(2)]
        diag_s, probTn = r.take(128), r.take(128, p=8)
        assert r.at <= qs_at
        NSLOT = 8
        r = Region(after_base)
        ring = [r.take(2048) for _ in range(NSLOT)]
        probT_s = r.take(4, 512)
        tail, isamp = r.take(KEYS, p=64), r.take(KEYS, p=64)
        prob_s = r.take(KEYS)
        osb = r.take(512)
        lf_one = probT_s[0:64].rearrange("p a b -> p (a b)")
        assert r.at <= kidx_at[2]
        KV_AT = [xT_at, kidx_at[2]] + [after_base + 4096 * j for j in range(4)]
        kv_pair = [Region(a).take(NPG, 256) for a in KV_AT]
        KV_SLOT = [0, 1, 2, 3, 4, 5, 1, 2]
        FILLS = [("k_b", 0), ("k_b", 1), ("v_b", 0), ("k_b", 2), ("v_b", 1), ("k_b", 3), ("v_b", 2), ("v_b", 3)]
        r = Region(vtm_at)
        hT = r.take(KD, T)
        subk = r.take(2 * PH, 128)
        sv = r.take(2 * PH, PK)
        si = r.take(2 * PH, PK).bitcast(U32)
        siF = r.take(2 * PH, PK)
        top, gate, ja, jb, gexp = (r.take(PH, PK) for _ in range(5))
        tj = r.take(PH, PK).bitcast(U32)
        jbits = r.take(PH, PK).bitcast(U32)
        e0, e1 = r.take(PH, PK), r.take(PH, PK)
        ids = [r.take(NE).bitcast(U32) for _ in range(2)]
        assert r.at <= after_base, r.at - after_base
        r = Region(after_base)
        hrow = r.take(5, D)
        wmix = [Region(after_base + (1 + j) * D).take(KD, 128) for j in range(4)]
        lng, lnb = r.take(D), r.take(D)
        sc = r.take(2 * PH, 128)
        cand_at = r.at
        cand = r.take(PH, PK * PK)
        oh = r.take(NE, PK)
        facc = r.take(D)
        pre = r.take(NE)
        gl = r.take(NE)
        coef = [r.take(NE) for _ in range(2)]
        ND = 4
        diag_p = [r.take(128) for _ in range(ND)]
        NR, NR0 = 14, 6
        rows_at = r.at
        rows = [r.take(D) for _ in range(NR)]
        w_out = Region(rows_at + NR0 * D).take(KD, D)
        qpT0 = Region(rows_at).take(2 * PH, 128)
        r = Region(xT_at)
        qpT = r.take(2 * PH, T - 128)
        assert r.at <= vtm_at
        r = Region(CAT["causal"][0])
        wq_at = r.at
        wq = [r.take(KD, 128) for _ in range(3)]
        sig = [[Region(cand_at + j * 128).take(128) for j in range(2)],
               [Region(wq_at + D + j * 512).take(T - 128) for j in range(2)]]
        assert r.at <= NCONST
        xrow = [facc, Region(wq_at).take(D)]

        x_loaded, v_w_loaded, f_w_loaded = sem("x_loaded"), sem("v_w_loaded"), sem("f_w_loaded")
        w_loaded = sems("w_loaded", 3)
        z_ready, z_copied = sem("z_ready"), sem("z_copied")
        rot_ready, rope_done = sem("rot_ready"), sem("rope_done")
        f_ready, f_act, logf_ready = sem("f_ready"), sem("f_act"), sem("logf_ready")
        ones_set, zero_set = sem("ones_set"), sem("zero_set")
        negc_stored, bias_loaded, v_stored = sem("negc_stored"), sem("bias_loaded"), sem("v_stored")
        k_stored, logf_stored, y_stored = sem("k_stored"), sem("logf_stored"), sem("y_stored")
        dve_seq, act_seq = sem("dve_seq"), sem("act_seq")
        phase = sem("phase")
        s_ready, s_read, negmax_ready = sem("s_ready"), sem("s_read"), sem("negmax_ready")
        idx_added, mask_ready, diag_ready = sem("idx_added"), sem("mask_ready"), sem("diag_ready")
        pt_ready, pt_copied = sem("pt_ready"), sem("pt_copied")
        o_ready, o_copied = sem("o_ready"), sem("o_copied")
        ring_loaded = sems("ring_loaded", NSLOT)
        slot_read, pair_read = sem("slot_read"), sem("pair_read")
        spread_a, spread_d = sem("spread_a"), sem("spread_d")
        wrow_loaded, wd_ready = sem("wrow_loaded"), sem("wd_ready")
        lidx_ready, lp_loaded, lf_ones = sem("lidx_ready"), sem("lp_loaded"), sem("lf_ones")
        tail_new, tail_ready = sem("tail_new"), sem("tail_ready")
        ia_ready, relu_done, ib_ready, ib_copied = (sem(n) for n in ("ia_ready", "relu_done", "ib_ready", "ib_copied"))
        smask_ready, ss_ready, smax_ready = sem("smask_ready"), sem("ss_ready"), sem("smax_ready")
        sx_done, sdiag_ready, st_ready, st_copied = (sem(n) for n in ("sx_done", "sdiag_ready", "st_ready", "st_copied"))
        so_ready, so_copied, se_ready, se_done = (sem(n) for n in ("so_ready", "so_copied", "se_ready", "se_done"))
        masks_ready, rows_loaded, kidx_loaded = sem("masks_ready"), sem("rows_loaded"), sems("kidx_loaded", 4)
        kv_loaded = sems("kv_loaded", NB)
        xT_loaded, rows_cleared = sem("xT_loaded"), sem("rows_cleared")
        vnew_loaded = sems("vnew_loaded", 2)
        mix_loaded, wo_loaded, ln_loaded = sems("mix_loaded", 4), sem("wo_loaded"), sem("ln_loaded")
        mix_ready, sig_done, mix_done = sem("mix_ready"), sem("sig_done"), sem("mix_done")
        xr_loaded, h_ready, res_done = sems("xr_loaded", 2), sem("h_ready"), sem("res_done")
        var_ready, std_ready, ln_done = sem("var_ready"), sem("std_ready"), sem("ln_done")
        ht_ready, ht_copied = sem("ht_ready"), sem("ht_copied")
        wq_loaded, qp_ready, qp_copied = sems("wq_loaded", 3), sem("qp_ready"), sem("qp_copied")
        subk_loaded, ln2_loaded = sem("subk_loaded"), sem("ln2_loaded")
        sc_ready, sc_copied, gexp_in, gexp_out = (sem(n) for n in ("sc_ready", "sc_copied", "gexp_in", "gexp_out"))
        ids_ready, row_loaded = sem("ids_ready"), sems("row_loaded", NR)
        dve_used, pe_used = sem("dve_used"), sem("pe_used")
        gelu_done, coef_ready, dp_ready = sem("gelu_done"), sem("coef_ready"), sem("dp_ready")

        csc = nc.dram_tensor("neg_cumulative", [NH, T], F32, kind="Internal").ap()

        def col(j, w=1, p=128):
            return small[0:p, j:j + w]

        COL_TOP8, COL_NEGMAX, COL_RSUM, COL_RINV = 8, 80, 84, 88
        COL_SMAX, COL_SSUM, COL_SINV, COL_TOPS = 16, 17, 18, 24
        COL_BN, COL_MV, COL_STD, COL_RSTD = 32, 48, 50, 52
        COL_TOPP, COL_GSUM, COL_GINV = 56, 64, 72

        def blocks(seen):
            return [(k, min(128, seen - k)) for k in range(0, seen, 128)]

        units, uses = [], []
        for i in range(5):
            if i:
                uses += [("idx", i, h) for h in range(NI)]
            for kind in ("fox", "dsa"):
                for h in range(NH):
                    units.append((kind, i, h, len(uses)))
                    uses.append((kind, i, h))
        NU = len(units)
        idx_use = {(i, h): n for n, (k, i, h) in enumerate(uses) if k == "idx"}
        ROUNDS_P, ROUNDS_S = SEL_P // 8, SEL_S // 8

        gathers = [(i, v, k) for i in range(4) for v in (0, 1) for k in range(NE)][:-(NE - V3_ALONE)]
        for k in range(NE):
            gathers += [(3, 1, V3_ALONE + k)] * (k < NE - V3_ALONE) + [(4, 0, k)]
        gathers += [(4, 1, k) for k in range(NE)]
        gather_at = {g: n for n, g in enumerate(gathers)}

        def read_by_dve(i, v, k):
            if v == 0:
                return True
            return (k < V0_DVE or k % 2 == 1) if i == 0 else k % 8 in ((3, 5, 7) if i < 4 else (1, 3, 5, 7))

        by_dve = [read_by_dve(*g) for g in gathers]
        pe_first = [min(k for k in range(NE) if not read_by_dve(i, 1, k)) for i in range(5)]
        pe_last = [max(k for k in range(NE) if not read_by_dve(i, 1, k)) for i in range(5)]
        read_before, slot_of, fill_of, last_in = [], [], [], []
        n_dve = n_pe = 0
        newest, fills = {}, {}
        for n, d in enumerate(by_dve):
            read_before.append(n_dve if d else n_pe)
            n_dve, n_pe = n_dve + d, n_pe + (not d)
            s_ = n % NR0 if n < NE else (n - NE) % NR
            last_in.append(newest.get(s_))
            fills[s_] = fills.get(s_, 0) + 1
            newest[s_] = n
            slot_of.append(s_)
            fill_of.append(fills[s_])

        SPANS = ((0, 128), (128, T))

        def part_done(p):
            return 4 * (p // 3) + (1, 2, 4)[p % 3]

        def gather_no(i, v, k):
            return gather_at[i, v, k]

        def halves(b, rows_=128):
            return ps[0:rows_, b * 512:(b + 2) * 512].rearrange("p (a c) -> p a c", a=2)[:, :, 0:HT]

        def split(v):
            return v.rearrange("p (a c) -> p a c", a=2)

        def end_phase(eng, n):
            eng.drain().then_inc(phase, 1)
            eng.wait_ge(phase, 5 * n)

        block = ctx.enter_context(nc.Block())

        @block.sync
        def _(sp):
            def project():
                sp.dma_start(xT[:], io["xT"]).then_inc(x_loaded, 16)
                for m in range(NPROJ):
                    if m >= 3:
                        sp.wait_ge(z_ready, m - 2)
                    sp.dma_start(wring[m % 3], io["w_proj"][m]).then_inc(w_loaded[m % 3], 16)
                    if m == 2:
                        sp.dma_start(consts[:], io["cst"]).then_inc(x_loaded, 16)
                        sp.dma_start(pages[:], io["pages"]).then_inc(x_loaded, 16)
                        sp.dma_start(page_rows[:], io["page_rows"]).then_inc(x_loaded, 16)
                sp.wait_ge(logf_ready, 1)
                sp.dma_start(io["logf_out"], f_log).then_inc(logf_stored, 16)
                sp.dma_start(csc, f_z).then_inc(negc_stored, 16)
                sp.wait_ge(negc_stored, 16)
                sp.dma_start(heads[64:65, KB:KB + NH, :],
                             csc.rearrange("(o h) t -> o h t", o=1)).then_inc(bias_loaded, 16)
                sp.wait_ge(z_copied, NPROJ + 5)
                for i, (t0, nt) in enumerate(TILES):
                    sp.dma_start(io["v_out"][t0:t0 + nt, :], vtm[0:nt, i, :]).then_inc(v_stored, 16)
                sp.wait_ge(rope_done, len(ROPES))
                sp.dma_start(io["k_out"][:, 0:2, :], heads[0:64, KA:KA + 2, :]).then_inc(k_stored, 16)
                sp.dma_start(io["k_out"][:, 2:3, :], heads[0:64, KI:KI + 1, :]).then_inc(k_stored, 16)
                sp.dma_start(io["k_out"][:, 3:11, :], heads[0:64, KB:KB + NH, :]).then_inc(k_stored, 16)
                sp.wait_ge(v_stored, 16 * 5)
                for g in range(2):
                    src = io["v_out"][LP + 32 * g:LP + 32 * g + 32, NH * HD + NKV * HD:VW]
                    for b in range(4):
                        for h in range(NI):
                            sp.dma_start(wrow[b * 32 + h * 8:b * 32 + h * 8 + 8, g:g + 1],
                                         src[b * 8:b * 8 + 8, h:h + 1],
                                         allow_slow_non_contiguous=True).then_inc(wrow_loaded, 16)
                sp.wait_ge(bias_loaded, 16)

            def prompt():
                sp.dma_start(key_pages, io["key_rows"]).then_inc(rows_loaded, 16)
                sp.dma_start(kv_pages, io["kv_rows"]).then_inc(rows_loaded, 16)

            def sample():
                for b in range(NB):
                    sp.dma_start(tail[b * 8:b * 8 + 8, PAST:KEYS],
                                 csc[:, LP + b * SN:LP + (b + 1) * SN]).then_inc(tail_new, 16)

                def page_numbers(at):
                    return nc.values_load_multi_w_load_instructions(
                        pages[0:1, at:at + 16], engines=(mybir.EngineType.SP,), min_val=0, max_val=NPOOL - 1)[1]

                for f, (src, pr) in enumerate(FILLS):
                    for half in range(2):
                        nos = page_numbers(NB * NPG + 32 * pr + 16 * half)
                        for v in range(4):
                            s = 4 * half + v
                            if f:
                                sp.wait_ge(slot_read, NSLOT * (f - 1) + s + 1)
                            for j in range(4):
                                sp.dma_start(ring[s][:, j * 512:(j + 1) * 512],
                                             io[src][bass.ds(nos[4 * v + j], 1)].rearrange("o p n -> (o p) n")
                                             ).then_inc(ring_loaded[s], 16)
                for b in range(2, NB, 2):
                    if b < 6:
                        sp.wait_ge(slot_read, NSLOT * 7 + 2 * (KV_SLOT[b] - 2) + 2)
                    else:
                        sp.wait_ge(pair_read, 1)
                    s = KV_SLOT[b]
                    for j, no in enumerate(page_numbers(b * NPG)):
                        sp.dma_start(kv_pair[s][:, j, :], io["kv_a"][bass.ds(no, 1)].rearrange("o p n -> (o p) n")
                                     ).then_inc(kv_loaded[b], 16)
                sp.dma_start(xT[:], io["xT"]).then_inc(xT_loaded, 16)

            def merge():
                def mix_part(p):
                    m, j = p // 3 % KD, p % 3
                    if p >= 4:
                        sp.wait_ge(mix_ready, part_done(p - 4))
                    sp.dma_start(wmix[p % 4], io["w_mix"][m][:, KD * j:KD * (j + 1), :]).then_inc(mix_loaded[p % 4], 16)

                def x_rows(i):
                    t0, nt = TILES[i]
                    if i >= 2:
                        sp.wait_ge(res_done, i - 1)
                    sp.dma_start(xrow[i % 2][0:nt, :], io["x"][t0:t0 + nt, :]).then_inc(xr_loaded[i % 2], 16)

                def w_queries(n):
                    if n >= 3:
                        sp.wait_ge(qp_ready, n - 2)
                    if n == 2 * PH:
                        sp.wait_ge(mix_done, 2 * KD)
                    if n == 2 * PH + 2:
                        sp.wait_ge(res_done, 5)
                    sp.dma_start(wq[n % 3], io["w_q"][n % (2 * PH)]).then_inc(wq_loaded[n % 3], 16)

                for p in range(3 * KD):
                    mix_part(p)
                    if p == 9:
                        sp.dma_start(w_out[:], io["w_out"]).then_inc(wo_loaded, 16)
                        x_rows(0)
                        sp.dma_start(lng, io["ln"][0:1, :].partition_broadcast(128)).then_inc(ln_loaded, 16)
                        sp.dma_start(lnb, io["ln"][1:2, :].partition_broadcast(128)).then_inc(ln_loaded, 16)
                for n in range(3):
                    w_queries(n)
                sp.dma_start(subk[:], io["subk"]).then_inc(subk_loaded, 16)
                for p in range(3 * KD, 3 * KD + 4):
                    mix_part(p)
                for n in range(3, 2 * PH):
                    w_queries(n)
                sp.wait_ge(qp_ready, 2 * PH)
                x_rows(1)
                for p in range(3 * KD + 4, 6 * KD):
                    mix_part(p)
                x_rows(2)
                w_queries(2 * PH)
                w_queries(2 * PH + 1)
                x_rows(3)
                x_rows(4)
                for n in range(2 * PH + 2, 4 * PH):
                    w_queries(n)
                sp.wait_ge(ln_done, 5)
                sp.dma_start(lng, io["ln"][2:3, :].partition_broadcast(128)).then_inc(ln2_loaded, 16)
                sp.dma_start(lnb, io["ln"][3:4, :].partition_broadcast(128)).then_inc(ln2_loaded, 16)

            def peer():
                for i, (t0, nt) in enumerate(TILES):
                    sp.wait_ge(ln_done, 5 + i + 1)
                    sp.dma_start(io["y_out"][t0:t0 + nt, :], facc[0:nt, :]).then_inc(y_stored, 16)
                sp.wait_ge(y_stored, 16 * 5)

            project()
            end_phase(sp, 1)
            prompt()
            sp.wait_ge(k_stored, 16 * 3)
            sp.wait_ge(logf_stored, 16)
            sp.wait_ge(wrow_loaded, 16 * 32)
            end_phase(sp, 2)
            sample()
            end_phase(sp, 3)
            merge()
            peer()

        @block.gpsimd
        def _(pool):
            pool.memset(zeroed, 0.0).then_inc(zero_set, 1)
            pool.wait_ge(zero_set, 1)
            pool.memset(heads[64:65, QB:QB + NH, :], 1.0).then_inc(ones_set, 1)
            end_phase(pool, 1)
            pool.wait_ge(lidx_ready, 1)
            for j in range(NPG):
                pool.indirect_dma_start(out=lp[:, j * 128:(j + 1) * 128], out_offset=None, in_=io["logf_b"],
                                        in_offset=bass.IndirectOffsetOnAxis(ap=lidx[:, j:j + 1], axis=0)
                                        ).then_inc(lp_loaded, 16)
            for c in range(4):
                for p in range(4):
                    for j in range(4):
                        at = p * NPG + 4 * c + j
                        pool.indirect_dma_start(out=kidx[c][:, p * 512 + j * 128:p * 512 + (j + 1) * 128],
                                                out_offset=None, in_=io["kidx"],
                                                in_offset=bass.IndirectOffsetOnAxis(ap=key_rows[:, at:at + 1], axis=0)
                                                ).then_inc(kidx_loaded[c], 16)
            end_phase(pool, 2)
            pool.memset(lf_one, 1.0).then_inc(lf_ones, 1)

            def new_values(q):
                if q >= 2:
                    pool.wait_ge(so_ready, q - 1)
                for e in range(2):
                    t0 = LP + (2 * (q % 4) + e) * SN
                    pool.dma_start(vnew[q % 2][:, e, :], io["v_out"][t0:t0 + SN, :]).then_inc(vnew_loaded[q % 2], 16)

            def batch_pages(b):
                s = KV_SLOT[b]
                for j in range(NPG):
                    at = b * NPG + j
                    pool.indirect_dma_start(out=kv_pair[s][:, j, :], out_offset=None, in_=io["kv_a"].rearrange("o p n -> (o p) n"),
                                            in_offset=bass.IndirectOffsetOnAxis(ap=kv_rows[:, at:at + 1], axis=0)
                                            ).then_inc(kv_loaded[b], 16)

            new_values(0)
            new_values(1)
            pool.wait_ge(ia_ready, 8)
            batch_pages(0)
            batch_pages(1)
            new_values(2)
            new_values(3)
            new_values(4)
            pool.wait_ge(slot_read, NSLOT * 7 + 4)
            batch_pages(3)
            pool.wait_ge(slot_read, NSLOT * 8)
            batch_pages(5)
            new_values(5)
            pool.wait_ge(pair_read, 2)
            batch_pages(7)
            new_values(6)
            new_values(7)
            end_phase(pool, 3)
            for n, (i, v, k) in enumerate(gathers):
                nt = TILES[i][1]
                if v == 0 and k == 0:
                    pool.wait_ge(ids_ready, i + 1)
                before = last_in[n]
                if before is not None:
                    pool.wait_ge(dve_used if by_dve[before] else pe_used, read_before[before] + 1)
                elif slot_of[n] == NR0:
                    pool.wait_ge(h_ready, 5)
                if i == 4 and v and k < NR:
                    pool.memset(rows[slot_of[n]][64:128, :], 0.0).then_inc(rows_cleared, 1)
                    pool.wait_ge(rows_cleared, k + 1)
                pool.indirect_dma_start(out=rows[slot_of[n]][0:nt, :], out_offset=None,
                                        in_=io["peer_v"] if v else io["peer_u"],
                                        in_offset=bass.IndirectOffsetOnAxis(ap=ids[i % 2][0:nt, k:k + 1], axis=0)
                                        ).then_inc(row_loaded[slot_of[n]], 16)

        @block.tensor
        def _(pe):
            def project():
                pe.wait_ge(x_loaded, 64)

                def rotate(m):
                    n = 64 * PROJ[m][1]
                    pe.wait_ge(z_copied, m + 1)
                    if m:
                        pe.wait_ge(rope_done, m)
                    for a in range(2):
                        last = pe.matmul(bank(4 + a, HT, 0, n), const("rot")[0:n, 0:n],
                                         zsb[m % 2][0:n, a * HT:(a + 1) * HT], start=True, stop=True)
                    last.then_inc(rot_ready, 1)

                for m in range(NPROJ):
                    n = 64 * PROJ[m][1]
                    pe.wait_ge(w_loaded[m % 3], 16 * (m // 3 + 1))
                    if m >= 2:
                        pe.wait_ge(z_copied, m - 1)
                    for a in range(2):
                        for k in range(KD):
                            last = pe.matmul(bank(2 * (m % 2) + a, HT, 0, n), wring[m % 3][:, k, 0:n],
                                             xT[:, k, a * HT:(a + 1) * HT], start=(k == 0), stop=(k == KD - 1))
                    last.then_inc(z_ready, 1)
                    if m and PROJ[m - 1][2]:
                        rotate(m - 1)
                pe.wait_ge(f_w_loaded, 32)
                for a in range(2):
                    for k in range(KD):
                        last = pe.matmul(bank(6 + a, HT, 0, NH), w_f[:, k, :], xT[:, k, a * HT:(a + 1) * HT],
                                         start=(k == 0), stop=(k == KD - 1))
                last.then_inc(f_ready, 1)
                pe.wait_ge(v_w_loaded, 16)
                for i, (t0, nt) in enumerate(TILES):
                    n = NPROJ + i
                    pe.wait_ge(z_copied, n - 1)
                    for a, (c0, c1) in enumerate(((0, 512), (512, VW))):
                        for k in range(KD):
                            last = pe.matmul(bank(2 * (n % 2) + a, c1 - c0, 0, nt), xT[:, k, t0:t0 + nt],
                                             w_v[:, k, c0:c1], start=(k == 0), stop=(k == KD - 1))
                    last.then_inc(z_ready, 1)

            def prompt():
                def scores(n, q, kt, q0, nq, seen, rows_, bias=None, b0=0):
                    if n >= 2:
                        pe.wait_ge(s_read, n - 1)
                    for c0 in range(0, seen, 512):
                        c1 = min(c0 + 512, seen)
                        out = bank(2 * (n % 2) + c0 // 512, c1 - c0, 0, nq)
                        biased = bias is not None and c1 > b0
                        last = pe.matmul(out, heads[0:rows_, q, q0:q0 + nq], heads[0:rows_, kt, c0:c1],
                                         start=True, stop=not biased)
                        if biased:
                            at = max(b0, c0)
                            last = pe.matmul(out[:, at - c0:], ident_b[0:nq, 0:nq], bias[0:nq, at - b0:c1 - b0],
                                             start=False, stop=True)
                    last.then_inc(s_ready, 1)

                def transpose(u):
                    _, i, h, n = units[u]
                    q0, nq, seen = QTILES[i]
                    pe.wait_ge(diag_ready, u + 1)
                    if u >= 2:
                        pe.wait_ge(pt_copied, u - 1)
                    for j, (k0, nk) in enumerate(blocks(seen)):
                        last = pe.matmul(ps[0:nk, (4 + u % 2) * 512 + j * nq:(4 + u % 2) * 512 + (j + 1) * nq],
                                         prob[u % 3][0:nq, k0:k0 + nk], diag[u % 3][0:nq, 0:nq],
                                         start=True, stop=True)
                    last.then_inc(pt_ready, 1)

                def weigh(u):
                    kind, i, h, n = units[u]
                    q0, nq, seen = QTILES[i]
                    v0 = h * HD if kind == "fox" else NH * HD + (h // 4) * HD
                    pe.wait_ge(pt_copied, u + 1)
                    if u >= 2:
                        pe.wait_ge(o_copied, u - 1)
                    p0, c0 = 64 * (h % 2), 6 * 512 + 128 * (u % 2)
                    bl = blocks(seen)
                    for j, (k0, nk) in enumerate(bl):
                        last = pe.matmul(ps[p0:p0 + 64, c0:c0 + nq], vtm[0:nk, j, v0:v0 + HD],
                                         probT[u % 2][0:nk, j * nq:(j + 1) * nq],
                                         start=(j == 0), stop=(j == len(bl) - 1))
                    last.then_inc(o_ready, 1)

                pe.wait_ge(masks_ready, 1)
                for u in range(NU + 3):
                    if u < NU:
                        kind, i, h, n = units[u]
                        q0, nq, seen = QTILES[i]
                        if kind == "fox":
                            if h == 0 and i:
                                for hi in range(NI):
                                    scores(idx_use[i, hi], QI + hi, KI, q0, nq, seen, 64)
                            scores(n, QB + h, KB + h, q0, nq, seen, 65, causal_b, seen - nq)
                        else:
                            if h == 0 and i:
                                pe.wait_ge(mask_ready, i)
                            scores(n, QA + h, KA + h // 4, q0, nq, seen, 64, maskb if i else causal_b)
                    if 2 <= u < NU + 2:
                        transpose(u - 2)
                    if u >= 3:
                        weigh(u - 3)

            def sample():
                pe.wait_ge(wd_ready, 1)
                for c in range(5):
                    w = 512 if c < 4 else SN
                    if c < 4:
                        pe.wait_ge(kidx_loaded[c], 16 * 16)
                    for g in range(2):
                        n = 2 * c + g
                        if c:
                            pe.wait_ge(relu_done, n - 1)
                        for p in (2 * g, 2 * g + 1):
                            rhs = kidx[c][:, p * 512:(p + 1) * 512] if c < 4 else kin[:, p, :]
                            last = pe.matmul(bank(g, w), qis[:, p, :], rhs, start=(p % 2 == 0), stop=(p % 2 == 1))
                        last.then_inc(ia_ready, 1)
                    pe.wait_ge(relu_done, 2 * c + 2)
                    if c >= 2:
                        pe.wait_ge(ib_copied, c - 1)
                    for g in range(2):
                        last = pe.matmul(bank(2 + c % 2, w, 0, 64), wd[:, g, :], relu_s[g][:, 0:w],
                                         start=(g == 0), stop=(g == 1))
                    last.then_inc(ib_ready, 1)
                pe.wait_ge(ib_copied, 5)

                def unit(src, pr, c, e):
                    u = NSLOT * FILLS.index((src, pr)) + 2 * c + e
                    pe.wait_ge(ring_loaded[u % NSLOT], 16 * 4 * (u // NSLOT + 1))
                    return ring[u % NSLOT]

                def scores(q):
                    fox, pr = q < 4, q % 4
                    if q:
                        pe.wait_ge(sx_done, q)
                    if q == 4:
                        pe.wait_ge(smask_ready, 1)
                    pick, bias = (head_of, tail) if fox else (row_of_b, smask)
                    for c in range(4):
                        out = bank(c)
                        for e in range(2):
                            b = 2 * pr + e
                            if fox:
                                kk = unit("k_b", pr, c, e).rearrange("p (j h n) -> p j h n", j=4, h=4)
                                for hp in range(4):
                                    last = pe.matmul(out, qs[:, b, hp, :], kk[:, :, hp, :],
                                                     start=(e == 0 and hp == 0), stop=False)
                                last.then_inc(slot_read, 1)
                            else:
                                if c == 0:
                                    pe.wait_ge(kv_loaded[b], 16 * NPG)
                                kv = kv_pair[KV_SLOT[b]]
                                pe.matmul(out, qas[:, b, :], kv[:, 4 * c:4 * c + 4, 0:128], start=(e == 0), stop=False)
                        if q == c == 0:
                            pe.wait_ge(tail_ready, 1)
                        pe.matmul(out, pick[:, pr, :], bias[:, c * 512:(c + 1) * 512], start=False, stop=True)
                    out = bank(4, SN)
                    for e in range(2):
                        b = 2 * pr + e
                        if fox:
                            for hp in range(4):
                                pe.matmul(out, qs[:, b, hp, :], kbn[:, hp, b * SN:(b + 1) * SN],
                                          start=(e == 0 and hp == 0), stop=False)
                        else:
                            pe.matmul(out, qas[:, b, :], kan[:, b * SN:(b + 1) * SN], start=(e == 0), stop=False)
                    if fox:
                        pe.matmul(out, ident_b, newc_b, start=False, stop=False)
                    pe.matmul(out, pick[:, pr, :], bias[:, PAST:KEYS], start=False, stop=True).then_inc(ss_ready, 1)

                def transpose(q):
                    pe.wait_ge(sdiag_ready, q + 1)
                    for c in range(5):
                        n = 5 * q + c
                        if n >= 2:
                            pe.wait_ge(st_copied, n - 1)
                        if c < 4:
                            for j in range(4):
                                k0 = c * 512 + j * 128
                                last = pe.matmul(ps[:, (5 + n % 2) * 512 + j * 128:(5 + n % 2) * 512 + (j + 1) * 128],
                                                 prob_s[:, k0:k0 + 128], diag_s, start=True, stop=True)
                        else:
                            last = pe.matmul(bank(5 + n % 2, 128, 0, SN), prob_s[:, PAST:KEYS], diag_s,
                                             start=True, stop=True)
                        last.then_inc(st_ready, 1)

                def weigh(q):
                    fox, pr = q < 4, q % 4
                    for c in range(5):
                        pe.wait_ge(st_copied, 5 * q + c + 1)
                        if c == 0 and q:
                            pe.wait_ge(se_done, q)
                        if c == 4:
                            pe.wait_ge(vnew_loaded[q % 2], 32 * (q // 2 + 1))
                        for e in range(2):
                            b = 2 * pr + e
                            out = bank(7, 512 if fox else 128, 64 * e, 64 * e + 64)
                            if c == 4:
                                last = pe.matmul(out, probTn[0:SN, 64 * e:64 * e + 64],
                                                 vnew[q % 2][:, e, 0:512] if fox else vnew[q % 2][:, e, 512:640],
                                                 start=False, stop=True)
                                continue
                            if fox:
                                vv = unit("v_b", pr, c, e)
                            for j in range(4):
                                rhs = vv[:, j * 512:(j + 1) * 512] if fox else kv_pair[KV_SLOT[b]][:, 4 * c + j, 128:256]
                                last = pe.matmul(out, probT_s[:, c, j * 128 + 64 * e:j * 128 + 64 * e + 64], rhs,
                                                 start=(c == 0 and j == 0), stop=False)
                            if fox:
                                last.then_inc(slot_read, 1)
                            elif c == 3 and e == 1:
                                last.then_inc(pair_read, 1)
                    last.then_inc(so_ready, 1)

                def turn_back(q):
                    pe.wait_ge(so_copied, q + 1)
                    for hp in range(4 if q < 4 else 1):
                        last = pe.transpose(ps[:, 7 * 512 + hp * 128:7 * 512 + (hp + 1) * 128],
                                            osb[:, hp * 128:(hp + 1) * 128], ident)
                    last.then_inc(se_ready, 1)

                scores(0)
                transpose(0)
                for q in range(8):
                    if q < 7:
                        scores(q + 1)
                    weigh(q)
                    if q < 7:
                        transpose(q + 1)
                    turn_back(q)

            def mix(n):
                t0, t1 = SPANS[n // KD]
                b = 4 * (n % 2)
                for j, (src, nk, part, k0) in enumerate(((xT, 8, 0, 0), (xT, 8, 1, 0), (yaT, 4, 2, 0), (ybT, 4, 2, 4))):
                    p = 3 * n + part
                    pe.wait_ge(mix_loaded[p % 4], 16 * (p // 4 + 1))
                    if n >= 2:
                        if j < 2:
                            pe.wait_ge(sig_done, 2 * (n - 2) + j + 1)
                        else:
                            pe.wait_ge(mix_done, n - 1)
                    for k in range(nk):
                        last = pe.matmul(bank(b + j, t1 - t0), wmix[p % 4][:, k0 + k, :], src[:, k, t0:t1],
                                         start=(k == 0), stop=(k == nk - 1))
                    last.then_inc(mix_ready, 1)

            def out_product(i):
                t0, nt = TILES[i]
                if i >= 2:
                    pe.wait_ge(res_done, i - 1)
                for a in range(2):
                    for m in range(KD):
                        last = pe.matmul(bank(2 * (i % 2) + a, 512, 0, nt), hT[:, m, t0:t0 + nt],
                                         w_out[:, m, a * 512:(a + 1) * 512], start=(m == 0), stop=(m == KD - 1))
                last.then_inc(h_ready, 1)

            def turn(i):
                t0, nt = TILES[i]
                pe.wait_ge(ln_done, i + 1)
                if i:
                    pe.wait_ge(ht_copied, i)
                for k in range(KD):
                    last = pe.transpose(ps[:, 4 * 512 + k * 128:4 * 512 + k * 128 + nt],
                                        hrow[0:nt, i, k * 128:(k + 1) * 128], ident[0:nt, 0:nt])
                last.then_inc(ht_ready, 1)

            def queries(n):
                t0, t1 = SPANS[n // (2 * PH)]
                pe.wait_ge(wq_loaded[n % 3], 16 * (n // 3 + 1))
                if n >= 2:
                    pe.wait_ge(qp_copied, n - 1)
                for k in range(KD):
                    last = pe.matmul(bank(6 + n % 2, t1 - t0), wq[n % 3][:, k, :], hT[:, k, t0:t1],
                                     start=(k == 0), stop=(k == KD - 1))
                last.then_inc(qp_ready, 1)

            def key_scores(i, g):
                t0, nt = TILES[i]
                if i < 2:
                    pe.wait_ge(qp_copied, 2 * PH * i + 4 * g + 4)
                if i:
                    pe.wait_ge(sc_copied, 4 * (i - 1) + g + 1)
                q = qpT0 if i == 0 else qpT[:, :, t0 - 128:t0 - 128 + nt]
                for m in range(4 * g, 4 * g + 4):
                    last = pe.matmul(ps[0:nt, m * 128:(m + 1) * 128], q[:, m, :], subk[:, m, :], start=True, stop=True)
                last.then_inc(sc_ready, 1)

            def queries_and_scores(i):
                for m in range(2 * PH):
                    queries(2 * PH * i + m)
                    if m % 4 == 1 and m > 4:
                        key_scores(i, m // 4 - 1)
                key_scores(i, 3)

            def merge():
                pe.wait_ge(xT_loaded, 16)
                for n in range(KD):
                    mix(n)
                pe.wait_ge(mix_done, KD)
                pe.wait_ge(wo_loaded, 16)
                out_product(0)
                turn(0)
                pe.wait_ge(ht_copied, 1)
                pe.wait_ge(subk_loaded, 16)
                queries_and_scores(0)
                pe.wait_ge(sc_copied, 4)
                pe.wait_ge(qp_copied, 2 * PH)
                for n in range(KD, 2 * KD):
                    mix(n)
                pe.wait_ge(mix_done, 2 * KD)
                for i in range(1, 5):
                    out_product(i)
                    if i > 1:
                        turn(i - 1)
                turn(4)
                pe.wait_ge(res_done, 5)
                pe.wait_ge(ht_copied, 5)
                queries_and_scores(1)

            def peer():
                for n, (i, v, k) in enumerate(gathers):
                    nt = TILES[i][1]
                    if v == k == 0 and 0 < i < 4:
                        for g in range(4):
                            key_scores(i + 1, g)
                    if by_dve[n]:
                        continue
                    if k == pe_first[i] and i:
                        pe.wait_ge(ln_done, 5 + i)
                    pe.wait_ge(row_loaded[slot_of[n]], 16 * fill_of[n])
                    pe.wait_ge(dp_ready, read_before[n] + 1)
                    for a in range(2):
                        last = pe.matmul(bank(4 + a, 512, 0, nt), diag_p[read_before[n] % ND][:, 0:nt],
                                         rows[slot_of[n]][:, a * 512:(a + 1) * 512],
                                         start=(k == pe_first[i]), stop=(k == pe_last[i]))
                    last.then_inc(pe_used, 1)

            project()
            end_phase(pe, 1)
            prompt()
            end_phase(pe, 2)
            sample()
            end_phase(pe, 3)
            merge()
            peer()

        @block.scalar
        def _(act):
            done = [0]

            def step(ins):
                done[0] += 1
                ins.then_inc(act_seq, 1)
                act.wait_ge(act_seq, done[0])

            def project():
                act.dma_start(w_f[:], io["w_f"]).then_inc(f_w_loaded, 16)
                act.dma_start(bf[0:NH, :], io["b_forget"]).then_inc(f_w_loaded, 16)
                act.dma_start(w_v[:], io["w_v"]).then_inc(v_w_loaded, 16)
                for m, (h0, nh, rope, scale) in enumerate(PROJ):
                    n = 64 * nh
                    act.wait_ge(z_ready, m + 1)
                    if rope:
                        if m >= 2:
                            act.wait_ge(rope_done, m - 1)
                        act.activation(split(zsb[m % 2])[0:n], halves(2 * (m % 2), n), ACT.Copy,
                                       scale=scale).then_inc(z_copied, 1)
                    else:
                        z = halves(2 * (m % 2))
                        act.activation(split(heads[0:64, h0, :]), z[0:64], ACT.Copy, scale=scale)
                        act.activation(split(heads[0:64, h0 + 1, :]), z[64:128], ACT.Copy,
                                       scale=scale).then_inc(z_copied, 1)
                act.wait_ge(f_ready, 1)
                act.wait_ge(f_w_loaded, 32)
                step(act.activation(split(f_z), halves(6, NH), ACT.Identity, bias=bf[0:NH, :]))
                step(act.activation(f_tmp, f_z, ACT.Abs))
                step(act.activation(f_tmp, f_tmp, ACT.Exp, scale=-1.0))
                act.activation(f_tmp, f_tmp, ACT.Ln, bias=1.0).then_inc(f_act, 1)
                for i, (t0, nt) in enumerate(TILES):
                    n = NPROJ + i
                    act.wait_ge(z_ready, n + 1)
                    b = 2 * (n % 2)
                    act.activation(vtm[0:nt, i, :], ps[0:nt, b * 512:b * 512 + VW], ACT.Copy).then_inc(z_copied, 1)
                act.wait_ge(zero_set, 1)
                act.wait_ge(z_copied, NPROJ + 5)
                for h in range(NH):
                    for e in range(2):
                        half = h % 2
                        dst = qs.rearrange("p (b e) h c -> p b e h c", e=2)[
                            64 * half:64 * half + 64, :, e, h // 2, e * 64 + h * 8:e * 64 + h * 8 + 8]
                        src = heads[0:64, QB + h, LP:T].rearrange("p (b e t) -> p b e t", e=2, t=SN)[:, :, e, :]
                        last = act.activation(dst, src, ACT.Copy)
                    last = act.activation(kbn[64 * half:64 * half + 64, h // 2, :], heads[0:64, KB + h, LP:T], ACT.Copy)
                last.then_inc(spread_a, 1)

            def prompt():
                def move(u):
                    _, i, h, n = units[u]
                    q0, nq, seen = QTILES[i]
                    act.wait_ge(pt_ready, u + 1)
                    if u >= 2:
                        act.wait_ge(o_ready, u - 1)
                    full, rest = seen // 128, seen % 128
                    c0 = (4 + u % 2) * 512
                    last = act.activation(probT[u % 2][:, 0:full * nq], ps[:, c0:c0 + full * nq], ACT.Copy)
                    if rest:
                        last = act.activation(probT[u % 2][0:rest, full * nq:(full + 1) * nq],
                                              ps[0:rest, c0 + full * nq:c0 + (full + 1) * nq], ACT.Copy)
                    last.then_inc(pt_copied, 1)

                for u in range(NU + 2):
                    if u < NU:
                        kind, i, h, n = units[u]
                        q0, nq, seen = QTILES[i]
                        if kind == "fox" and h == 0 and i:
                            for hi in range(NI):
                                ni, a = idx_use[i, hi], NI * (i - 1) + hi
                                act.wait_ge(s_ready, ni + 1)
                                if a >= 2:
                                    act.wait_ge(idx_added, a - 1)
                                act.activation(relu[a % 2][0:nq, 0:seen],
                                               ps[0:nq, (ni % 2) * 1024:(ni % 2) * 1024 + seen], ACT.Relu
                                               ).then_inc(s_read, 1)
                        act.wait_ge(negmax_ready, u + 1)
                        if u >= 3:
                            act.wait_ge(pt_ready, u - 2)
                        act.activation(prob[u % 3][0:nq, 0:seen], ps[0:nq, (n % 2) * 1024:(n % 2) * 1024 + seen],
                                       ACT.Exp, bias=col(COL_NEGMAX + u % 3, p=nq),
                                       accum_out=col(COL_RSUM + u % 3, p=nq)).then_inc(s_read, 1)
                    if u >= 2:
                        move(u - 2)

            def sample():
                for c in range(5):
                    w = 512 if c < 4 else SN
                    for g in range(2):
                        act.wait_ge(ia_ready, 2 * c + g + 1)
                        if c:
                            act.wait_ge(ib_ready, c)
                        act.activation(relu_s[g][:, 0:w], bank(g, w), ACT.Relu).then_inc(relu_done, 1)

                def exponentials(q):
                    act.wait_ge(smax_ready, q + 1)
                    if q:
                        act.wait_ge(st_ready, 5 * q)
                    act.activation(prob_s, ps[:, 0:KEYS], ACT.Exp, bias=col(COL_SMAX),
                                   accum_out=col(COL_SSUM)).then_inc(sx_done, 1)

                def transposed(q):
                    if q:
                        act.wait_ge(so_ready, q)
                    for c in range(5):
                        n = 5 * q + c
                        act.wait_ge(st_ready, n + 1)
                        dst, src = ((probT_s[:, c, :], bank(5 + n % 2)) if c < 4
                                    else (probTn, bank(5 + n % 2, 128, 0, SN)))
                        act.activation(dst, src, ACT.Copy).then_inc(st_copied, 1)

                act.wait_ge(tail_ready, 1)
                exponentials(0)
                transposed(0)
                for q in range(8):
                    fox, pr = q < 4, q % 4
                    if q < 7:
                        exponentials(q + 1)
                    act.wait_ge(so_ready, q + 1)
                    if q:
                        act.wait_ge(se_ready, q)
                    w = 512 if fox else 128
                    act.activation(osb[:, 0:w], bank(7, w), ACT.Copy).then_inc(so_copied, 1)
                    if q < 7:
                        transposed(q + 1)
                    act.wait_ge(se_ready, q + 1)
                    for h in range(NH):
                        f0 = 64 * (h % 2 if fox else h // 4)
                        c0 = 7 * 512 + (h // 2 * 128 if fox else 0)
                        src = ps[f0:f0 + 64, c0:c0 + 128].rearrange("p (e h t) -> p e h t", e=2, h=NH)[:, :, h, :]
                        dst = (ybT if fox else yaT)[64 * (h % 2):64 * (h % 2) + 64, h // 2,
                                                    LP + pr * 16:LP + pr * 16 + 16]
                        last = act.activation(dst.rearrange("p (e t) -> p e t", e=2), src, ACT.Copy)
                    last.then_inc(se_done, 1)

            def sigmoids(n):
                t0, t1 = SPANS[n // KD]
                for j in range(2):
                    act.wait_ge(mix_ready, 4 * n + j + 1)
                    if n:
                        act.wait_ge(mix_done, n)
                    act.activation(sig[n // KD][j], bank(4 * (n % 2) + j, t1 - t0), ACT.Sigmoid).then_inc(sig_done, 1)

            def turned(i):
                t0, nt = TILES[i]
                act.wait_ge(ht_ready, i + 1)
                act.activation(hT[:, :, t0:t0 + nt],
                               ps[:, 4 * 512:6 * 512].rearrange("p (k c) -> p k c", k=KD)[:, :, 0:nt],
                               ACT.Copy).then_inc(ht_copied, 1)

            def root(n, nt):
                act.wait_ge(var_ready, n + 1)
                act.activation(col(COL_STD, p=nt), col(COL_MV + 1, p=nt), ACT.Sqrt,
                               bias=const("eps", nt)).then_inc(std_ready, 1)

            def queries(n):
                t0, t1 = SPANS[n // (2 * PH)]
                act.wait_ge(qp_ready, n + 1)
                dst = (qpT if n // (2 * PH) else qpT0)[:, n % (2 * PH), :]
                act.activation(dst, bank(6 + n % 2, t1 - t0), ACT.Copy).then_inc(qp_copied, 1)

            def key_scores(i, g):
                nt = TILES[i][1]
                act.wait_ge(sc_ready, 4 * i + g + 1)
                if i:
                    act.wait_ge(ids_ready, i)
                act.activation(sc[0:nt, 4 * g:4 * g + 4, :].rearrange("p a b -> p (a b)"), bank(g, 512, 0, nt), ACT.Copy
                               ).then_inc(sc_copied, 1)

            def gate_exp(i):
                nt = TILES[i][1]
                act.wait_ge(gexp_in, i + 1)
                act.activation(gexp[0:nt], gate[0:nt], ACT.Exp).then_inc(gexp_out, 1)

            def gelu(i, g):
                nt = TILES[i][1]
                act.wait_ge(dve_used, read_before[gather_no(i, 0, 32 * g + 31)] + 1)
                if i:
                    act.wait_ge(coef_ready, 4 * i + g)
                act.activation(gl[0:nt, 32 * g:32 * g + 32], pre[0:nt, 32 * g:32 * g + 32], ACT.Gelu
                               ).then_inc(gelu_done, 1)

            def queries_and_scores(i):
                for m in range(2 * PH):
                    queries(2 * PH * i + m)
                    if m % 4 == 1 and m > 4:
                        key_scores(i, m // 4 - 1)
                    if i == 1 and m == GELU_AT:
                        for g in range(4):
                            gelu(0, g)
                key_scores(i, 3)

            def merge():
                for n in range(KD):
                    sigmoids(n)
                root(0, TILES[0][1])
                turned(0)
                queries_and_scores(0)
                sigmoids(KD)
                sigmoids(KD + 1)
                gate_exp(0)
                for n in range(KD + 2, 2 * KD):
                    sigmoids(n)
                for i in range(1, 5):
                    root(i, TILES[i][1])
                    if i > 1:
                        turned(i - 1)
                turned(4)
                queries_and_scores(1)

            def peer():
                for n, (i, v, k) in enumerate(gathers):
                    nt = TILES[i][1]
                    if v == k == 0 and i == 3:
                        for g in range(4):
                            key_scores(4, g)
                    if v == 0 and i and k % 32 == 31:
                        gelu(i, k // 32)
                        for g in range(4 if i < 3 and k == NE - 1 else 0):
                            key_scores(i + 1, g)
                    if not by_dve[n]:
                        r_ = read_before[n]
                        act.wait_ge(coef_ready, 4 * i + k // 32 + 1)
                        if k == pe_first[4] and i == 4:
                            act.wait_ge(pe_used, r_)
                            for d in diag_p:
                                step(act.activation(d, ident, ACT.Copy, scale=0.0))
                        if r_ >= ND:
                            act.wait_ge(pe_used, r_ - ND + 1)
                        act.activation(diag_p[r_ % ND][0:nt, 0:nt], ident[0:nt, 0:nt], ACT.Copy,
                                       scale=coef[i % 2][0:nt, k:k + 1]).then_inc(dp_ready, 1)
                        if i < 4 and k == (GATE_0, GATE_AT, GATE_AT, GATE_3)[i]:
                            gate_exp(i + 1)
                    if v and k == NE - 1:
                        root(5 + i, nt)

            project()
            end_phase(act, 1)
            prompt()
            end_phase(act, 2)
            sample()
            end_phase(act, 3)
            merge()
            peer()

        @block.vector
        def _(dve):
            done = [0]

            def step(ins):
                done[0] += 1
                ins.then_inc(dve_seq, 1)
                dve.wait_ge(dve_seq, done[0])

            def project():
                dve.wait_ge(x_loaded, 64)
                for m in ROPES:
                    h0, nh, _, _ = PROJ[m]
                    n = 64 * nh
                    dve.wait_ge(rot_ready, m + 1)
                    step(dve.tensor_tensor(split(rot_s)[0:n], halves(4, n), split(const("sin", n)), ALU.mult))
                    step(dve.tensor_tensor(zsb[m % 2][0:n], zsb[m % 2][0:n], const("cos", n), ALU.mult))
                    for j in range(nh):
                        p0 = 64 * j
                        last = dve.tensor_tensor(heads[0:64, h0 + j, :], zsb[m % 2][p0:p0 + 64], rot_s[p0:p0 + 64],
                                                 ALU.add)
                    last.then_inc(rope_done, 1)
                    dve.wait_ge(rope_done, m + 1)
                dve.wait_ge(f_act, 1)
                step(dve.scalar_tensor_tensor(f_log, f_z, 0.0, f_tmp, ALU.min, ALU.subtract))
                step(dve.tensor_tensor_scan(f_sum, const("restart", NH), f_log, 0.0, ALU.mult, ALU.add))
                dve.tensor_scalar(f_z, f_sum, -1.0, None, ALU.mult).then_inc(logf_ready, 1)
                dve.wait_ge(zero_set, 1)
                for h in range(NH):
                    for e in range(2):
                        g = h // 4
                        dst = qas.rearrange("p (b e) c -> p b e c", e=2)[
                            64 * g:64 * g + 64, :, e, e * 64 + h * 8:e * 64 + h * 8 + 8]
                        src = heads[0:64, QA + h, LP:T].rearrange("p (b e t) -> p b e t", e=2, t=SN)[:, :, e, :]
                        dve.tensor_copy(dst, src)
                for h in range(NI):
                    for e in range(2):
                        for pp in range(2):
                            c0 = (2 * pp + e) * 32 + h * 8
                            dst = qis.rearrange("p (a b) c -> p a b c", b=2)[64 * e:64 * e + 64, :, pp, c0:c0 + 8]
                            src = heads[0:64, QI + h, LP:T].rearrange(
                                "p (a b e t) -> p a b e t", b=2, e=2, t=SN)[:, :, pp, e, :]
                            dve.tensor_copy(dst, src)
                for g in range(NKV):
                    dve.tensor_copy(kan[64 * g:64 * g + 64, :], heads[0:64, KA + g, LP:T])
                for e in range(2):
                    last = dve.tensor_copy(
                        kin[64 * e:64 * e + 64, :, :],
                        heads[0:64, KI, LP:T].rearrange("p (a e t) -> p a e t", e=2, t=SN)[:, :, e, :])
                last.then_inc(spread_d, 1)

            def take8(v, top8):
                step(dve.max(top8, v))
                step(dve.match_replace(v, top8, v, TAKEN))

            def prompt():
                dve.tensor_copy(ident_b, ident)
                dve.tensor_copy(newc_b, const("new_causal"))
                dve.tensor_copy(row_of_b, row_of)
                dve.tensor_copy(causal_b, causal).then_inc(masks_ready, 1)
                dve.tensor_scalar(lidx, page_rows, 8.0, const("head_no", 64), ALU.mult, ALU.add)
                dve.wait_ge(rows_loaded, 32)
                dve.tensor_scalar(key_rows, key_pages, 64.0, const("key_row"), ALU.mult, ALU.add)
                dve.tensor_scalar(kv_rows, kv_pages, 128.0, const("part"), ALU.mult, ALU.add
                                  ).then_inc(lidx_ready, 1)
                for i in range(1, 5):
                    nt = QTILES[i][1]
                    step(dve.tensor_scalar(vtm[0:nt, i, 640:VW], vtm[0:nt, i, 640:VW], IDX_SCALE, None, ALU.mult))

                def weights(u):
                    _, i, h, n = units[u]
                    q0, nq, seen = QTILES[i]
                    dve.wait_ge(s_read, n + 1)
                    step(dve.reciprocal(col(COL_RINV + u % 3, p=nq), col(COL_RSUM + u % 3, p=nq)))
                    if u >= 3:
                        dve.wait_ge(pt_ready, u - 2)
                    dve.tensor_scalar(diag[u % 3][0:nq, 0:nq], ident[0:nq, 0:nq], col(COL_RINV + u % 3, p=nq),
                                      None, ALU.mult).then_inc(diag_ready, 1)

                def result(u):
                    kind, i, h, n = units[u]
                    q0, nq, seen = QTILES[i]
                    dve.wait_ge(o_ready, u + 1)
                    p0, c0 = 64 * (h % 2), 6 * 512 + 128 * (u % 2)
                    y = ybT if kind == "fox" else yaT
                    dve.tensor_copy(y[p0:p0 + 64, h // 2, q0:q0 + nq], ps[p0:p0 + 64, c0:c0 + nq]
                                    ).then_inc(o_copied, 1)

                for u in range(NU + 4):
                    if u < NU:
                        kind, i, h, n = units[u]
                        q0, nq, seen = QTILES[i]
                        v = isc[0:nq, 0:seen]
                        if kind == "fox" and h == 0 and i:
                            for hi in range(NI):
                                a = NI * (i - 1) + hi
                                w = vtm[0:nq, i, 640 + hi:641 + hi]
                                dve.wait_ge(s_read, idx_use[i, hi] + 1)
                                rl = relu[a % 2][0:nq, 0:seen]
                                if hi == 0:
                                    dve.tensor_scalar(v, rl, w, None, ALU.mult).then_inc(idx_added, 1)
                                else:
                                    dve.scalar_tensor_tensor(v, rl, w, v, ALU.mult, ALU.add).then_inc(idx_added, 1)
                                dve.wait_ge(idx_added, a + 1)
                            own = isc[0:nq, seen - nq:seen]
                            step(dve.tensor_tensor(own, own, causal[0:nq, 0:nq], ALU.add))
                        dve.wait_ge(s_ready, n + 1)
                        if u >= 3:
                            dve.wait_ge(s_read, units[u - 3][3] + 1)
                        dve.tensor_reduce(col(COL_NEGMAX + u % 3, p=nq),
                                          ps[0:nq, (n % 2) * 1024:(n % 2) * 1024 + seen], AX_X, ALU.max,
                                          negate=True).then_inc(negmax_ready, 1)
                    if 1 <= u <= NU:
                        weights(u - 1)
                    if u >= 4:
                        result(u - 4)
                    if u < NU and kind == "fox" and i:
                        for _r in range(ROUNDS_P // NH):
                            take8(v, col(COL_TOP8, 8, nq))
                        if h == NH - 1:
                            if i > 1:
                                dve.wait_ge(s_ready, units[u - NH][3] + 1)
                            dve.tensor_scalar(maskb[0:nq, 0:seen], v, TAKEN, NEG, ALU.not_equal, ALU.mult
                                              ).then_inc(mask_ready, 1)

            def sample():
                dve.wait_ge(wrow_loaded, 16 * 32)
                step(dve.tensor_scalar(wd[:, 0, :], w_place[:, 0, :], wrow[:, 0:1], IDX_SCALE, ALU.mult, ALU.mult))
                dve.tensor_scalar(wd[:, 1, :], w_place[:, 1, :], wrow[:, 1:2], IDX_SCALE, ALU.mult, ALU.mult
                                  ).then_inc(wd_ready, 1)
                step(dve.memset(tail[:, 0:1], 0.0))
                dve.wait_ge(lp_loaded, 16 * NPG)
                dve.wait_ge(lf_ones, 1)
                dve.wait_ge(tail_new, 16 * NB)
                dve.tensor_tensor_scan(tail[:, 1:PAST], lf_one[:, 1:PAST], lp[:, 0:PAST - 1], 0.0,
                                       ALU.mult, ALU.add).then_inc(tail_ready, 1)
                for c in range(5):
                    w = 512 if c < 4 else SN
                    dve.wait_ge(ib_ready, c + 1)
                    dve.tensor_copy(isamp[:, c * 512:c * 512 + w], bank(2 + c % 2, w, 0, 64)).then_inc(ib_copied, 1)
                dve.wait_ge(ib_copied, 5)
                step(dve.tensor_tensor(isamp[:, PAST:KEYS], isamp[:, PAST:KEYS], const("idx_causal", 64), ALU.add))
                left = ROUNDS_S
                for q in range(8):
                    dve.wait_ge(ss_ready, q + 1)
                    if q:
                        dve.wait_ge(sx_done, q)
                    dve.tensor_reduce(col(COL_SMAX), ps[:, 0:KEYS], AX_X, ALU.max, negate=True
                                      ).then_inc(smax_ready, 1)
                    dve.wait_ge(sx_done, q + 1)
                    step(dve.reciprocal(col(COL_SINV), col(COL_SSUM)))
                    if q:
                        dve.wait_ge(st_ready, 5 * q)
                    dve.tensor_scalar(diag_s, ident, col(COL_SINV), None, ALU.mult).then_inc(sdiag_ready, 1)
                    now = min(left, -(-ROUNDS_S // 3))
                    for _r in range(now):
                        take8(isamp, col(COL_TOPS, 8, 64))
                    left -= now
                    if now and left == 0:
                        dve.tensor_scalar(smask, isamp, TAKEN, NEG, ALU.not_equal, ALU.mult
                                          ).then_inc(smask_ready, 1)

            def normalise(n, v, y, nt):
                for a in range(2):
                    step(dve.bn_stats(col(COL_BN + 6 * a, 6, nt), v[:, a * 512:(a + 1) * 512]))
                dve.bn_aggr(col(COL_MV, 2, nt), col(COL_BN, 12, nt)).then_inc(var_ready, 1)
                dve.wait_ge(std_ready, n + 1)
                step(dve.reciprocal(col(COL_RSTD, p=nt), col(COL_STD, p=nt)))
                step(dve.tensor_scalar(v, v, col(COL_MV, p=nt), col(COL_RSTD, p=nt), ALU.subtract, ALU.mult))
                step(dve.tensor_tensor(v, v, lng[0:nt], ALU.mult))
                dve.tensor_tensor(y, v, lnb[0:nt], ALU.add).then_inc(ln_done, 1)

            def mixed(n):
                t0, t1 = SPANS[n // KD]
                s0, s1 = sig[n // KD]
                for j, s_ in enumerate((s0, s1)):
                    dve.wait_ge(sig_done, 2 * n + j + 1)
                    dve.wait_ge(mix_ready, 4 * n + 2 + j + 1)
                    step(dve.tensor_tensor(s_, s_, bank(4 * (n % 2) + 2 + j, t1 - t0), ALU.mult))
                dve.tensor_tensor(hT[:, n % KD, t0:t1], s0, s1, ALU.add).then_inc(mix_done, 1)

            def first_norm(i):
                nt = TILES[i][1]
                v = hrow[0:nt, i, :]
                dve.wait_ge(h_ready, i + 1)
                dve.wait_ge(xr_loaded[i % 2], 16 * (i // 2 + 1))
                b = 2 * (i % 2)
                dve.scalar_tensor_tensor(v, xrow[i % 2][0:nt], ALPHA, ps[0:nt, b * 512:b * 512 + D],
                                         ALU.mult, ALU.add).then_inc(res_done, 1)
                dve.wait_ge(res_done, i + 1)
                normalise(i, v, v, nt)

            def merge():
                for n in range(KD):
                    mixed(n)
                dve.wait_ge(ln_loaded, 32)
                first_norm(0)
                for s in range(32):
                    route(0, s)
                    if s in ROUTE_MIX:
                        mixed(KD + ROUTE_MIX.index(s))

            def top16(v, vals, places):
                step(dve.max(vals[:, 0:8], v))
                step(dve.max_index(places[:, 0:8], vals[:, 0:8], v))
                step(dve.match_replace(v, vals[:, 0:8], v, TAKEN))
                step(dve.max(vals[:, 8:16], v))
                step(dve.max_index(places[:, 8:16], vals[:, 8:16], v))

            def route(i, s):
                nt = TILES[i][1]
                if s < 16 and s % 4 == 0:
                    dve.wait_ge(sc_copied, 4 * i + s // 4 + 1)
                if s < 16:
                    top16(sc[0:nt, s, :], sv[0:nt, s, :], si[0:nt, s, :])
                    return
                h = s - 16
                sv4 = sv.rearrange("p (h c) a -> p h c a", c=2)
                siF4 = siF.rearrange("p (h c) a -> p h c a", c=2)
                if h < PH:
                    cd = cand[0:nt, h, :]
                    step(dve.tensor_tensor(cd.rearrange("p (a b) -> p a b", a=PK),
                                           sv4[0:nt, h, 0, :, None].to_broadcast([nt, PK, PK]),
                                           sv4[0:nt, h, 1, None, :].to_broadcast([nt, PK, PK]), ALU.add))
                    top16(cd, top[0:nt, h, :], tj[0:nt, h, :])
                elif s == 24:
                    dve.tensor_tensor(gate[0:nt], top[0:nt], top[0:nt, :, 0:1].to_broadcast([nt, PH, PK]),
                                      ALU.subtract).then_inc(gexp_in, 1)
                    step(dve.tensor_copy(siF[0:nt], si[0:nt]))
                    step(dve.tensor_scalar(jbits[0:nt], tj[0:nt], 4, None, ALU.logical_shift_right))
                    step(dve.tensor_copy(ja[0:nt], jbits[0:nt]))
                elif s == 25:
                    step(dve.tensor_scalar(jbits[0:nt], tj[0:nt], 15, None, ALU.bitwise_and))
                    step(dve.tensor_copy(jb[0:nt], jbits[0:nt]))
                elif s in (26, 27, 28, 29):
                    c, first = divmod(s - 26, 2)
                    jx, ex = ((ja, e0), (jb, e1))[c]
                    o4 = oh[0:nt].rearrange("p (h k) a -> p h k a", h=PH)
                    if first == 0:
                        step(dve.tensor_tensor(
                            oh[0:nt], jx[0:nt].rearrange("p h k -> p (h k)")[:, :, None].to_broadcast([nt, NE, PK]),
                            const("iota16", nt)[:, None, :].to_broadcast([nt, NE, PK]), ALU.is_equal))
                    else:
                        step(dve.tensor_tensor(o4, o4, siF4[0:nt, :, c, None, :].to_broadcast([nt, PH, PK, PK]),
                                               ALU.mult))
                        step(dve.tensor_reduce(ex[0:nt].rearrange("p h k -> p (h k)"), oh[0:nt], AX_X, ALU.add))
                elif s == 30:
                    dve.scalar_tensor_tensor(ids[i % 2][0:nt], e0[0:nt].rearrange("p h k -> p (h k)"), 128.0,
                                             e1[0:nt].rearrange("p h k -> p (h k)"), ALU.mult, ALU.add
                                             ).then_inc(ids_ready, 1)
                elif s == 31:
                    dve.wait_ge(gexp_out, i + 1)
                    step(dve.tensor_reduce(col(COL_GSUM, PH, nt), gexp[0:nt], AX_X, ALU.add))
                    step(dve.reciprocal(col(COL_GINV, PH, nt), col(COL_GSUM, PH, nt)))
                    step(dve.tensor_tensor(gate[0:nt], gexp[0:nt],
                                           col(COL_GINV, PH, nt)[:, :, None].to_broadcast([nt, PH, PK]), ALU.mult))

            def coefs(i, g):
                nt = TILES[i][1]
                dve.wait_ge(gelu_done, 4 * i + g + 1)
                gf = gate[0:nt].rearrange("p h k -> p (h k)")
                dve.tensor_tensor(coef[i % 2][0:nt, 32 * g:32 * g + 32], gf[:, 32 * g:32 * g + 32],
                                  gl[0:nt, 32 * g:32 * g + 32], ALU.mult).then_inc(coef_ready, 1)

            def finish(i):
                nt = TILES[i][1]
                dve.wait_ge(pe_used, read_before[gather_no(i, 1, pe_last[i])] + 1)
                step(dve.tensor_tensor(facc[0:nt], facc[0:nt], ps[0:nt, 4 * 512:4 * 512 + D], ALU.add))
                step(dve.scalar_tensor_tensor(facc[0:nt], hrow[0:nt, i, :], ALPHA, facc[0:nt], ALU.mult, ALU.add))
                if i == 0:
                    dve.wait_ge(ln2_loaded, 32)
                normalise(5 + i, facc[0:nt], facc[0:nt], nt)

            def peer():
                for n, (i, v, k) in enumerate(gathers):
                    if not by_dve[n]:
                        continue
                    nt = TILES[i][1]
                    row = rows[slot_of[n]][0:nt]
                    if v == 0:
                        dve.wait_ge(row_loaded[slot_of[n]], 16 * fill_of[n])
                        dve.tensor_tensor_reduce(out=row, in0=row, in1=hrow[0:nt, i, :], scale=1.0,
                                                 scalar=0.0, op0=ALU.mult, op1=ALU.add,
                                                 accum_out=pre[0:nt, k:k + 1]).then_inc(dve_used, 1)
                        if i and k >= 32 and k % 32 == 4:
                            coefs(i, k // 32 - 1)
                        if i == 0 and k in DOT_MIX:
                            mixed(KD + len(ROUTE_MIX) + DOT_MIX.index(k))
                        if i == 0 and k in DOT_NORM:
                            first_norm(1 + DOT_NORM.index(k))
                        if i == 3 and k % 5 == 4 and k < 5 * 24:
                            route(4, k // 5)
                        if k == NE - 1:
                            for g in range(3 if i else 0, 4):
                                coefs(i, g)
                        continue
                    j = sum(read_by_dve(i, 1, k_) for k_ in range(k))
                    c = coef[i % 2][0:nt, k:k + 1]
                    if j == 0:
                        dve.wait_ge(coef_ready, 4 * i + 4)
                        if i:
                            dve.wait_ge(y_stored, 16 * i)
                    dve.wait_ge(row_loaded[slot_of[n]], 16 * fill_of[n])
                    if j == 0:
                        ins = dve.tensor_scalar(facc[0:nt], row, c, None, ALU.mult)
                    else:
                        ins = dve.scalar_tensor_tensor(facc[0:nt], row, c, facc[0:nt], ALU.mult, ALU.add)
                    ins.then_inc(dve_used, 1)
                    dve.wait_ge(dve_used, read_before[n] + 1)
                    if i == 0 and j in ROUTE_1:
                        route(1, ROUTE_1.index(j))
                    elif i in (1, 2) and j < 32:
                        route(i + 1, j)
                    elif i == 3 and j < 8:
                        route(4, 24 + j)
                    if k == NE - 1:
                        finish(i)

            project()
            end_phase(dve, 1)
            prompt()
            end_phase(dve, 2)
            sample()
            end_phase(dve, 3)
            merge()
            peer()


_OUTS = {"y_out": (T, D), "k_out": (HD, 11, T), "v_out": (T, VW), "logf_out": (NH, T)}


def lay_out(i):
    c = np.ascontiguousarray
    x = np.concatenate([i["meta_tokens"], i["x_prompt"][0], i["x_sample"].reshape(NS, D)], axis=0)
    w = i["w_in"][0]
    cuts = np.cumsum([0, 512, 128, 128, 256, 64, 4, 512, 512, 512, 8, D, D])
    wqa, wka, wva, wqi, wki, wwi, wqb, wkb, wvb, wf, wga, wgb = (w[:, a:b] for a, b in zip(cuts[:-1], cuts[1:]))

    def chunks(a):
        return a.reshape(-1, 128, a.shape[1]).transpose(1, 0, 2)

    def column_tiles(a):
        return chunks(a).reshape(128, a.shape[0] // 128, -1, 128).transpose(2, 0, 1, 3)

    pad = np.zeros((D, 64), np.float32)
    mix = np.concatenate([column_tiles(a) for a in (wga, wgb, i["w_branch_a"][0], i["w_branch_b"][0])], axis=2)
    table = i["page_table"]
    back = table[:, ::-1]
    kb = i["cache_k_b"][0, :, ::-1].transpose(0, 2, 3, 1)
    ka = i["cache_k_a"][0].transpose(0, 2, 3, 1).reshape(NPOOL, 128, PAGE)
    out = {
        "cst": tables(),
        "xT": chunks(x.T),
        "x": x,
        "w_proj": column_tiles(np.concatenate([wqa, wka, wqi, wki, pad, wqb, wkb], axis=1)),
        "w_v": chunks(np.concatenate([wvb, wva, wwi], axis=1)),
        "w_f": chunks(wf),
        "b_forget": i["b_forget"].reshape(NH, 1),
        "pages": np.concatenate([table.reshape(1, -1),
                                 back.reshape(4, 2, 4, 4).transpose(0, 2, 1, 3).reshape(1, -1)], axis=1),
        "key_rows": np.repeat(table.reshape(4, 2, NPG).transpose(1, 0, 2).reshape(2, -1), 64, axis=0),
        "kv_rows": np.repeat(table.reshape(1, -1), 128, axis=0),
        "page_rows": np.repeat(back, NH, axis=0),
        "kidx": i["cache_k_idx"][0].transpose(0, 2, 1).reshape(NPOOL * 64, PAGE),
        "k_b": kb.reshape(NPOOL, 4, 128, PAGE).transpose(0, 2, 1, 3).reshape(NPOOL, 128, 512),
        "v_b": i["cache_v_b"][0, :, ::-1].reshape(NPOOL, PAGE, 512),
        "kv_a": np.concatenate([ka, i["cache_v_a"][0].reshape(NPOOL, PAGE, 128)], axis=2),
        "logf_b": i["cache_logf_b"][0, :, ::-1].transpose(0, 2, 1).reshape(NPOOL * NH, PAGE),
        "w_mix": mix,
        "w_out": chunks(i["w_out"][0]),
        "ln": np.concatenate([i["ln1_g"], i["ln1_b"], i["ln2_g"], i["ln2_b"]], axis=0),
        "w_q": column_tiles(i["peer_w_q"][0]),
        "subk": i["peer_sub_keys"][0].transpose(3, 1, 0, 2).reshape(128, 2 * PH, 128),
        "peer_u": i["peer_u"][0],
        "peer_v": i["peer_v"][0],
    }
    return {k: c(v) for k, v in out.items()}


def give_back(r):
    y, k, v, f = r["y_out"], r["k_out"].transpose(2, 1, 0), r["v_out"], r["logf_out"].T
    rows_ = {"k_a": k[:, 0:2], "v_a": v[:, 512:640].reshape(T, NKV, HD), "k_i": k[:, 2], "k_b": k[:, 3:11],
             "v_b": v[:, 0:512].reshape(T, NH, HD), "f": f}
    prompt = [a[None, None, 0:LP] for a in rows_.values()]
    sample = [a[LP:T].reshape((1, NB, SN) + a.shape[1:]) for a in rows_.values()]
    return (y[None, N_META:LP], y[LP:T].reshape(NB, SN, D), *prompt, *sample)


def kernel(**inputs):
    import concourse.bacc as _bacc
    from concourse.bass_utils import run_bass_kernel_spmd as _run

    arrays = lay_out({k: np.asarray(v) for k, v in inputs.items()})
    nc = _bacc.Bacc("TRN2", target_bir_lowering=False, num_devices=1)
    io = {n: nc.dram_tensor(n, a.shape, mybir.dt.from_np(a.dtype), kind="ExternalInput").ap()
          for n, a in arrays.items()}
    for n, shape in _OUTS.items():
        io[n] = nc.dram_tensor(n, shape, F32, kind="ExternalOutput").ap()
    program(nc, io)
    got = _run(nc, [arrays], core_ids=[0]).results[0]
    return tuple(np.ascontiguousarray(a) for a in give_back(got))
```
